# Optimizing a Trainium2 kernel written in Bass

```python
import jax, jax.numpy as jnp
from jax import lax
import numpy as np

D_MODEL = 2048
BATCH = 1
SEQ = 256
DEPTH = 2

CHUNK = 64
N_A_LAYERS = DEPTH // 2
N_B_LAYERS = DEPTH - N_A_LAYERS
HG_KDIM = 128
HG_HEADS = D_MODEL // HG_KDIM
HG_VDIM = D_MODEL // HG_HEADS
HG_FDIM = HG_HEADS * HG_KDIM
HG_BLOCK = CHUNK // 4
FOX_HDIM = 128
FOX_HEADS = D_MODEL // FOX_HDIM
Q_BLOCK = 128
FORGET_BIAS_INIT = 2.0
EPS = 1e-6


def rmsnorm(x, w):
    xf = x.astype(jnp.float32)
    y = xf * lax.rsqrt(jnp.mean(xf * xf, axis=-1, keepdims=True) + EPS)
    return (y * w.astype(jnp.float32)).astype(x.dtype)

def head_rmsnorm(x, w):
    xf = x.astype(jnp.float32)
    return xf * lax.rsqrt(jnp.mean(xf * xf, axis=-1, keepdims=True) + EPS) * w.astype(jnp.float32)

def hgrn2_chunkwise(q, k, v, g):
    B, H, T, dk = q.shape
    dv = v.shape[-1]
    n = T // HG_BLOCK

    def to_blocks(a):
        return jnp.moveaxis(a.reshape(B, H, n, HG_BLOCK, a.shape[-1]), 2, 0)

    mask = jnp.tril(jnp.ones((HG_BLOCK, HG_BLOCK), dtype=bool))[:, :, None]

    def step(S, blk):
        qc, kc, vc, gc = blk
        b = jnp.cumsum(gc, axis=-2)
        diff = b[..., :, None, :] - b[..., None, :, :]
        decay = jnp.exp(jnp.where(mask, diff, -jnp.inf))
        A = jnp.einsum('bhtd,bhsd,bhtsd->bhts', qc, kc, decay)
        o = (jnp.einsum('bhts,bhse->bhte', A, vc)
             + jnp.einsum('bhtd,bhde->bhte', qc * jnp.exp(b), S))
        b_last = b[..., -1:, :]
        S = (jnp.exp(b_last[..., 0, :])[..., None] * S
             + jnp.einsum('bhsd,bhse->bhde', kc * jnp.exp(b_last - b), vc))
        return S, o

    S0 = jnp.zeros((B, H, dk, dv), jnp.float32)
    _, o = lax.scan(step, S0, (to_blocks(q), to_blocks(k), to_blocks(v), to_blocks(g)))
    return jnp.moveaxis(o, 0, 2).reshape(B, H, T, dv)

def hgrn2_layer(x, norm_w, w_in, lb, out_norm_w, w_out):
    B, T, _ = x.shape
    h = rmsnorm(x, norm_w)
    proj = h @ w_in
    q = proj[..., :HG_FDIM]
    fz = proj[..., HG_FDIM:2 * HG_FDIM]
    i = proj[..., 2 * HG_FDIM:2 * HG_FDIM + D_MODEL]
    gate = proj[..., 2 * HG_FDIM + D_MODEL:]
    heads_k = lambda a: a.reshape(B, T, HG_HEADS, HG_KDIM).astype(jnp.float32).transpose(0, 2, 1, 3)
    q, fz = heads_k(q), heads_k(fz)
    i = i.reshape(B, T, HG_HEADS, HG_VDIM).astype(jnp.float32).transpose(0, 2, 1, 3)
    lb = lb.reshape(HG_HEADS, 1, HG_KDIM)
    log_f = jnp.logaddexp(jnp.log(lb), jnp.log1p(-lb) + jax.nn.log_sigmoid(fz))
    k = (1.0 - lb) * jax.nn.sigmoid(-fz)
    o = hgrn2_chunkwise(q, k, i, log_f)
    o = head_rmsnorm(o.transpose(0, 2, 1, 3), out_norm_w.reshape(HG_HEADS, HG_VDIM))
    o = o.reshape(B, T, D_MODEL) * jax.nn.silu(gate.astype(jnp.float32))
    return x + (o.astype(x.dtype) @ w_out)

def shared_kv(x, norm_w, w_kvf, f_bias, k_norm_w):
    B, T, _ = x.shape
    h = rmsnorm(x, norm_w)
    kvf = h @ w_kvf
    k = kvf[..., :D_MODEL].reshape(B, T, FOX_HEADS, FOX_HDIM)
    v = kvf[..., D_MODEL:2 * D_MODEL].reshape(B, T, FOX_HEADS, FOX_HDIM)
    fz = kvf[..., 2 * D_MODEL:].astype(jnp.float32) + f_bias.astype(jnp.float32)
    k = head_rmsnorm(k, k_norm_w).transpose(0, 2, 1, 3)
    v = v.astype(jnp.float32).transpose(0, 2, 1, 3)
    F = jnp.cumsum(jax.nn.log_sigmoid(fz), axis=1).transpose(0, 2, 1)
    return k, v, F

def forgetting_attention(q, k, v, F):
    T = q.shape[2]
    scale = FOX_HDIM ** -0.5
    local = jnp.arange(Q_BLOCK)
    outs = []
    for blk in range(T // Q_BLOCK):
        q0 = blk * Q_BLOCK
        kend = q0 + Q_BLOCK
        s = (jnp.einsum('bhqd,bhkd->bhqk', q[:, :, q0:kend], k[:, :, :kend]) * scale
             + F[:, :, q0:kend, None] - F[:, :, None, :kend])
        causal = (q0 + local)[:, None] >= jnp.arange(kend)[None, :]
        p = jax.nn.softmax(jnp.where(causal, s, -jnp.inf), axis=-1)
        outs.append(jnp.einsum('bhqk,bhkd->bhqd', p, v[:, :, :kend]))
    return jnp.concatenate(outs, axis=2)

def fox_layer(x, norm_w, w_in, q_norm_w, out_norm_w, w_out, k, v, F):
    B, T, _ = x.shape
    h = rmsnorm(x, norm_w)
    proj = h @ w_in
    q = proj[..., :D_MODEL].reshape(B, T, FOX_HEADS, FOX_HDIM)
    gate = proj[..., D_MODEL:]
    q = head_rmsnorm(q, q_norm_w).transpose(0, 2, 1, 3)
    o = forgetting_attention(q, k, v, F)
    o = head_rmsnorm(o.transpose(0, 2, 1, 3), out_norm_w.reshape(FOX_HEADS, FOX_HDIM))
    o = o.reshape(B, T, D_MODEL) * jax.nn.silu(gate.astype(jnp.float32))
    return x + (o.astype(x.dtype) @ w_out)

def first_inputs(seed: int = 0) -> dict:
    key = jax.random.key(seed)
    ks = jax.random.split(key, 16)
    D = D_MODEL
    s = D ** -0.5
    nrm = jax.random.normal
    return {
        "x": nrm(ks[0], (BATCH, SEQ, D), jnp.float32),
        "a_norm_w": 1.0 + 0.02 * nrm(ks[1], (N_A_LAYERS, D), jnp.float32),
        "a_w_in": s * nrm(ks[2], (N_A_LAYERS, D, 2 * HG_FDIM + 2 * D), jnp.float32),
        "a_lb_logits": 0.1 * nrm(ks[3], (N_A_LAYERS, HG_FDIM), jnp.float32),
        "a_out_norm_w": 1.0 + 0.02 * nrm(ks[4], (N_A_LAYERS, D), jnp.float32),
        "a_w_out": s * nrm(ks[5], (N_A_LAYERS, D, D), jnp.float32),
        "kv_norm_w": 1.0 + 0.02 * nrm(ks[6], (D,), jnp.float32),
        "kv_w": s * nrm(ks[7], (D, 2 * D + FOX_HEADS), jnp.float32),
        "kv_f_bias": FORGET_BIAS_INIT + 0.1 * nrm(ks[8], (FOX_HEADS,), jnp.float32),
        "k_norm_w": 1.0 + 0.02 * nrm(ks[9], (FOX_HDIM,), jnp.float32),
        "b_norm_w": 1.0 + 0.02 * nrm(ks[10], (N_B_LAYERS, D), jnp.float32),
        "b_w_in": s * nrm(ks[11], (N_B_LAYERS, D, 2 * D), jnp.float32),
        "b_q_norm_w": 1.0 + 0.02 * nrm(ks[12], (N_B_LAYERS, FOX_HDIM), jnp.float32),
        "b_out_norm_w": 1.0 + 0.02 * nrm(ks[13], (N_B_LAYERS, D), jnp.float32),
        "b_w_out": s * nrm(ks[14], (N_B_LAYERS, D, D), jnp.float32),
    }

def first_block(x, a_norm_w, a_w_in, a_lb_logits, a_out_norm_w, a_w_out,
              kv_norm_w, kv_w, kv_f_bias, k_norm_w,
              b_norm_w, b_w_in, b_q_norm_w, b_out_norm_w, b_w_out):
    lb_all = jnp.cumsum(jax.nn.softmax(a_lb_logits.astype(jnp.float32), axis=0), axis=0)
    lb_all = lb_all - lb_all[0:1]
    k = v = F = None
    for layer in range(DEPTH):
        if layer < N_A_LAYERS:
            x = hgrn2_layer(x, a_norm_w[layer], a_w_in[layer], lb_all[layer],
                            a_out_norm_w[layer], a_w_out[layer])
        else:
            if layer == N_A_LAYERS:
                k, v, F = shared_kv(x, kv_norm_w, kv_w, kv_f_bias, k_norm_w)
            j = layer - N_A_LAYERS
            x = fox_layer(x, b_norm_w[j], b_w_in[j], b_q_norm_w[j], b_out_norm_w[j],
                          b_w_out[j], k, v, F)
    return x


DEPTH_2 = 1

RNN_WIDTH = D_MODEL
RNN_BLOCKS = 16
CONV_WIDTH = 4
RG_C = 8.0
N_HEADS = 16
HEAD_DIM = D_MODEL // N_HEADS
KV_RANK = 512
IDX_HEADS = 16
IDX_DIM = 64
TOPK_MAX = 256
PEER_HEADS = 8
PEER_KEYS = 128
PEER_EXPERTS = PEER_KEYS * PEER_KEYS
PEER_QDIM = 256
PEER_TOPK = 16
PEER_CHUNK = 128

SPLITS = (RNN_WIDTH, N_HEADS * HEAD_DIM, KV_RANK, IDX_HEADS * IDX_DIM, IDX_DIM, IDX_HEADS, D_MODEL, D_MODEL)
IN_WIDTH = sum(SPLITS)


def rmsnorm_2(x, g):
    xf = x.astype(jnp.float32)
    y = xf * lax.rsqrt(jnp.mean(xf * xf, axis=-1, keepdims=True) + EPS)
    return (y * g.astype(jnp.float32)).astype(x.dtype)

def layernorm(x, g, b):
    xf = x.astype(jnp.float32)
    mu = jnp.mean(xf, axis=-1, keepdims=True)
    var = jnp.mean(jnp.square(xf - mu), axis=-1, keepdims=True)
    y = (xf - mu) * lax.rsqrt(var + EPS)
    return (y * g.astype(jnp.float32) + b.astype(jnp.float32)).astype(x.dtype)

def causal_conv(x, w, b):
    s = x.shape[1]
    xp = jnp.pad(x, ((0, 0), (CONV_WIDTH - 1, 0), (0, 0)))
    y = b
    for i in range(CONV_WIDTH):
        y = y + xp[:, i:i + s] * w[i]
    return y

def rg_lru(x, wa, ba, wx, bx, lam):
    bsz, s, _ = x.shape
    xb = x.reshape(bsz, s, RNN_BLOCKS, -1)
    r = jax.nn.sigmoid(jnp.einsum('bsnc,ncd->bsnd', xb, wa).reshape(bsz, s, -1) + ba)
    i = jax.nn.sigmoid(jnp.einsum('bsnc,ncd->bsnd', xb, wx).reshape(bsz, s, -1) + bx)
    log_a = -RG_C * r.astype(jnp.float32) * jax.nn.softplus(-lam.astype(jnp.float32))
    a = jnp.exp(log_a)
    u = jnp.sqrt(-jnp.expm1(2.0 * log_a)) * (i * x).astype(jnp.float32)

    def combine(c1, c2):
        a1, b1 = c1
        a2, b2 = c2
        return a1 * a2, a2 * b1 + b2

    _, h = lax.associative_scan(combine, (a, u), axis=1)
    return h.astype(x.dtype)

def dsa_attention(q, c_kv, q_idx, k_idx, w_idx, w_uk, w_uv):
    bsz, s = c_kv.shape[:2]
    topk = min(TOPK_MAX, s // 4)
    key_pos = jnp.arange(s)

    def block(blk):
        t0 = blk * Q_BLOCK
        sl = lambda a: lax.dynamic_slice_in_dim(a, t0, Q_BLOCK, axis=1)
        qb, qib, wib = sl(q), sl(q_idx), sl(w_idx)
        qpos = t0 + jnp.arange(Q_BLOCK)
        rel = jax.nn.relu(jnp.einsum('bqhd,bsd->bqhs', qib, k_idx) * IDX_DIM ** -0.5)
        iscore = jnp.einsum('bqhs,bqh->bqs', rel, wib).astype(jnp.float32)
        causal = key_pos[None, :] <= qpos[:, None]
        iscore = jnp.where(causal[None], iscore, -jnp.inf)
        _, sel = lax.top_k(iscore, topk)
        valid = sel <= qpos[None, :, None]
        c_sel = jax.vmap(lambda c, ix: c[ix])(c_kv, sel)
        q_lat = jnp.einsum('bqhd,hcd->bqhc', qb, w_uk)
        logits = jnp.einsum('bqhc,bqkc->bqhk', q_lat, c_sel).astype(jnp.float32) * HEAD_DIM ** -0.5
        logits = jnp.where(valid[:, :, None, :], logits, -jnp.inf)
        p = jax.nn.softmax(logits, axis=-1).astype(c_sel.dtype)
        o_lat = jnp.einsum('bqhk,bqkc->bqhc', p, c_sel)
        o = jnp.einsum('bqhc,hcd->bqhd', o_lat, w_uv)
        return o.reshape(bsz, Q_BLOCK, -1)

    out = lax.map(block, jnp.arange(s // Q_BLOCK))
    return out.transpose(1, 0, 2, 3).reshape(bsz, s, -1)

def peer(x, wq, keys1, keys2, u, v):
    bsz, s, d = x.shape
    t = bsz * s
    xf = x.reshape(t, d)
    q = (xf @ wq).reshape(t, PEER_HEADS, PEER_QDIM)
    half = PEER_QDIM // 2
    s1 = jnp.einsum('thd,kd->thk', q[..., :half], keys1)
    s2 = jnp.einsum('thd,kd->thk', q[..., half:], keys2)
    v1, i1 = lax.top_k(s1, PEER_TOPK)
    v2, i2 = lax.top_k(s2, PEER_TOPK)
    cand_s = (v1[..., :, None] + v2[..., None, :]).reshape(t, PEER_HEADS, -1)
    cand_i = (i1[..., :, None] * PEER_KEYS + i2[..., None, :]).reshape(t, PEER_HEADS, -1)
    top_s, pos = lax.top_k(cand_s, PEER_TOPK)
    expert = jnp.take_along_axis(cand_i, pos, axis=-1).reshape(t, -1)
    gate = jax.nn.softmax(top_s.astype(jnp.float32), axis=-1).astype(x.dtype).reshape(t, -1)
    n_chunks = t // PEER_CHUNK

    def chunk(args):
        xc, ec, gc = args
        z = jnp.einsum('cd,ced->ce', xc, u[ec])
        act = jax.nn.gelu(z, approximate=False) * gc
        return jnp.einsum('ce,ced->cd', act, v[ec])

    out = lax.map(chunk, (xf.reshape(n_chunks, PEER_CHUNK, d),
                          expert.reshape(n_chunks, PEER_CHUNK, -1),
                          gate.reshape(n_chunks, PEER_CHUNK, -1)))
    return out.reshape(bsz, s, d)

def second_inputs(seed: int = 0) -> dict:
    key = jax.random.key(seed)
    ks = jax.random.split(key, 24)
    f32 = jnp.float32
    nrm = lambda k, shape, scale: jax.random.normal(k, shape, f32) * scale
    gain = lambda k, shape: 1.0 + 0.05 * jax.random.normal(k, shape, f32)
    bw = RNN_WIDTH // RNN_BLOCKS
    a_c = jax.random.uniform(ks[9], (DEPTH_2, RNN_WIDTH), f32, 0.9, 0.999)
    a = a_c ** (1.0 / RG_C)
    rg_lambda = jnp.log(a) - jnp.log1p(-a)
    return {
        "x": nrm(ks[0], (BATCH, SEQ, D_MODEL), 1.0),
        "norm_mix_g": gain(ks[1], (DEPTH_2, D_MODEL)),
        "w_in": nrm(ks[2], (DEPTH_2, D_MODEL, IN_WIDTH), D_MODEL ** -0.5),
        "conv_w": nrm(ks[3], (DEPTH_2, CONV_WIDTH, RNN_WIDTH), CONV_WIDTH ** -0.5),
        "conv_b": nrm(ks[4], (DEPTH_2, RNN_WIDTH), 0.02),
        "rg_wa": nrm(ks[5], (DEPTH_2, RNN_BLOCKS, bw, bw), bw ** -0.5),
        "rg_ba": nrm(ks[6], (DEPTH_2, RNN_WIDTH), 0.1),
        "rg_wx": nrm(ks[7], (DEPTH_2, RNN_BLOCKS, bw, bw), bw ** -0.5),
        "rg_bx": nrm(ks[8], (DEPTH_2, RNN_WIDTH), 0.1),
        "rg_lambda": rg_lambda,
        "kv_norm_g": gain(ks[10], (DEPTH_2, KV_RANK)),
        "w_uk": nrm(ks[11], (DEPTH_2, N_HEADS, KV_RANK, HEAD_DIM), KV_RANK ** -0.5),
        "w_uv": nrm(ks[12], (DEPTH_2, N_HEADS, KV_RANK, HEAD_DIM), KV_RANK ** -0.5),
        "idx_ln_g": gain(ks[13], (DEPTH_2, IDX_DIM)),
        "idx_ln_b": nrm(ks[14], (DEPTH_2, IDX_DIM), 0.02),
        "w_o": nrm(ks[15], (DEPTH_2, D_MODEL, D_MODEL), D_MODEL ** -0.5),
        "norm_ffn_g": gain(ks[16], (DEPTH_2, D_MODEL)),
        "peer_wq": nrm(ks[17], (DEPTH_2, D_MODEL, PEER_HEADS * PEER_QDIM), D_MODEL ** -0.5),
        "peer_keys1": nrm(ks[18], (DEPTH_2, PEER_KEYS, PEER_QDIM // 2), (PEER_QDIM // 2) ** -0.5),
        "peer_keys2": nrm(ks[19], (DEPTH_2, PEER_KEYS, PEER_QDIM // 2), (PEER_QDIM // 2) ** -0.5),
        "peer_u": nrm(ks[20], (DEPTH_2, PEER_EXPERTS, D_MODEL), D_MODEL ** -0.5),
        "peer_v": nrm(ks[21], (DEPTH_2, PEER_EXPERTS, D_MODEL), PEER_HEADS ** -0.5),
        "norm_final_g": gain(ks[22], (D_MODEL,)),
    }

def second_block(x, norm_mix_g, w_in, conv_w, conv_b, rg_wa, rg_ba, rg_wx, rg_bx, rg_lambda,
              kv_norm_g, w_uk, w_uv, idx_ln_g, idx_ln_b, w_o, norm_ffn_g, peer_wq,
              peer_keys1, peer_keys2, peer_u, peer_v, norm_final_g):
    bsz, s, _ = x.shape
    split_points = [int(p) for p in np.cumsum(SPLITS)[:-1]]
    for l in range(DEPTH_2):
        h = rmsnorm_2(x, norm_mix_g[l])
        proj = h @ w_in[l]
        xr, q, ckv, qi, ki, wi, gr, ga = jnp.split(proj, split_points, axis=-1)
        y_rnn = rg_lru(causal_conv(xr, conv_w[l], conv_b[l]),
                       rg_wa[l], rg_ba[l], rg_wx[l], rg_bx[l], rg_lambda[l])
        ckv = rmsnorm_2(ckv, kv_norm_g[l])
        ki = layernorm(ki, idx_ln_g[l], idx_ln_b[l])
        wi = wi * IDX_HEADS ** -0.5
        y_attn = dsa_attention(q.reshape(bsz, s, N_HEADS, HEAD_DIM), ckv,
                               qi.reshape(bsz, s, IDX_HEADS, IDX_DIM), ki, wi, w_uk[l], w_uv[l])
        mixed = jax.nn.sigmoid(gr) * y_rnn + jax.nn.sigmoid(ga) * y_attn
        x = x + mixed @ w_o[l]
        x = x + peer(rmsnorm_2(x, norm_ffn_g[l]), peer_wq[l], peer_keys1[l], peer_keys2[l],
                     peer_u[l], peer_v[l])
    return rmsnorm_2(x, norm_final_g)


def setup_inputs(seed=0):
    out = dict(first_inputs(seed))
    for name, value in second_inputs(seed + 1).items():
        if name != "x":
            out[name + "_2"] = value
    return out


def reference(
    x, a_norm_w, a_w_in, a_lb_logits, a_out_norm_w, a_w_out, kv_norm_w, kv_w, kv_f_bias,
    k_norm_w, b_norm_w, b_w_in, b_q_norm_w, b_out_norm_w, b_w_out, norm_mix_g_2, w_in_2,
    conv_w_2, conv_b_2, rg_wa_2, rg_ba_2, rg_wx_2, rg_bx_2, rg_lambda_2, kv_norm_g_2, w_uk_2,
    w_uv_2, idx_ln_g_2, idx_ln_b_2, w_o_2, norm_ffn_g_2, peer_wq_2, peer_keys1_2, peer_keys2_2,
    peer_u_2, peer_v_2, norm_final_g_2,
):
    x = first_block(
        x, a_norm_w, a_w_in, a_lb_logits, a_out_norm_w, a_w_out, kv_norm_w, kv_w, kv_f_bias,
        k_norm_w, b_norm_w, b_w_in, b_q_norm_w, b_out_norm_w, b_w_out,
    )
    return second_block(
        x, norm_mix_g_2, w_in_2, conv_w_2, conv_b_2, rg_wa_2, rg_ba_2, rg_wx_2, rg_bx_2,
        rg_lambda_2, kv_norm_g_2, w_uk_2, w_uv_2, idx_ln_g_2, idx_ln_b_2, w_o_2, norm_ffn_g_2,
        peer_wq_2, peer_keys1_2, peer_keys2_2, peer_u_2, peer_v_2, norm_final_g_2,
    )


_drawn_inputs = setup_inputs


def setup_inputs(seed=0):
    import zlib

    import numpy as np

    out = dict(_drawn_inputs(seed))
    spreads = {}
    factors = {'k_norm_w': 3.372,
     'b_q_norm_w': 3.721,
     'b_out_norm_w': 2.962,
     'rg_ba_2': 19.397,
     'rg_bx_2': 11.483,
     'kv_norm_g_2': 4.129,
     'idx_ln_g_2': 3.333,
     'idx_ln_b_2': 5.631,
     'conv_b_2': 3.027,
     'norm_ffn_g_2': 3.403}
    for name, (base, spread) in spreads.items():
        noise = np.random.default_rng([zlib.crc32(name.encode()), seed]).standard_normal(out[name].shape)
        drawn = base * np.exp(spread * noise) if base else spread * noise
        out[name] = __import__('jax').numpy.asarray(drawn.astype(out[name].dtype))
    for name, factor in factors.items():
        out[name] = (out[name] * factor).astype(out[name].dtype)
    return out
```

```python
from contextlib import ExitStack

import concourse.bass as bass
from concourse import mybir

ALU = mybir.AluOpType
ACT = mybir.ActivationFunctionType
AX = mybir.AxisListType
F32 = mybir.dt.float32
I32 = mybir.dt.int32
U32 = mybir.dt.uint32
ds = bass.ds

P = 128
D = 2048
T = 256
KC = D // P
NT = T // P
HEADS = 16
PAIRS = HEADS // 2
G = 2 * P
W2 = 2 * T
EPS = 1e-6
HD_SCALE = float(P) ** -0.5
LEVELS = 7
SC = P + T
NEG = -1e30
TAKEN = -3.3e38
KV_RANK = 512
RC = KV_RANK // P
IDX_HEADS = 16
IDX_DIM = 64
TOPK = min(256, T // 4)
RG_C = 8.0
PEER_HEADS = 8
PEER_TOPK = 16
SLOTS_PER_TOKEN = PEER_HEADS * PEER_TOPK
GB = 4

PRM = {}
for _n in ("a_norm", "a_lb", "a_onorm", "kv_norm", "b_norm", "b_onorm", "mix", "cw0", "cw1", "cw2", "cw3",
           "cb", "ba", "bx", "lam", "ffn"):
    PRM[_n] = len(PRM) * KC
PRM["k_norm"] = 16 * KC
PRM["q_norm"] = PRM["k_norm"] + 1
PRM["ckv"] = PRM["q_norm"] + 1
PRM["idx_g"] = PRM["ckv"] + RC
PRM["idx_b"] = PRM["idx_g"] + 1
NPRM = PRM["idx_b"] + 1

FILLS = {"A": (8, 8, 8, 8), "OA": (2, 2, 2, 2), "F": (8, 8, 8, 8), "OF": (2, 2, 2, 2), "X": (3, 1, 1, 2),
         "C": (8, 8, 8, 8), "OC": (2, 2, 2, 2), "Q": (2, 2, 2, 2)}
BASE = {}
_at = (0, 0, 0, 0)
for _n, _f in FILLS.items():
    BASE[_n] = _at
    _at = tuple(a + b for a, b in zip(_at, _f))
FILLED = _at


def past_zero(value):
    return not isinstance(value, int) or value > 0


def program(nc, x_fm, prm_h, f_bias_h, w_in_a, w_out_a, w_kv, w_in_b, w_out_b, w_in_c, rg_wa, rg_wx, w_uk, w_uv,
            w_out_c, w_q, keys1, keys2, peer_u, peer_v, g_ffn, g_fin, out):
    ctx = ExitStack()
    with ctx:
        def sb_in(stack, name, shape, dt=F32):
            return stack.enter_context(nc.sbuf_tensor(name, shape, dt))

        def sem(name):
            return ctx.enter_context(nc.semaphore(name))

        def sb(name, shape, dt=F32):
            return sb_in(ctx, name, shape, dt)

        xT = sb("xT", [P, KC, T])
        hT = sb("hT", [P, KC, T])
        hkvT = sb("hkvT", [P, KC, T])
        oT = sb("oT", [P, KC, T])
        Wm = sb("Wm", [P, 4, KC * G])
        prm = sb("prm", [P, NPRM])
        fbias = sb("fbias", [HEADS, 1])
        ident = sb("ident", [P, P])
        ones = sb("ones", [P, P])
        eps = sb("eps", [P, 1])
        lb = sb("lb", [P, KC])
        omlb = sb("omlb", [P, KC])
        rg_c = sb("rg_c", [P, KC])
        qw = sb("qw", [P, 1])
        sp = sb("sp", [P, 8, KC])
        tri = sb("tri", [P, SC])
        rstd = sb("rstd", [P, T])
        sq = sb("sq", [P, 4, W2])
        W = [Wm[:, s, :].rearrange("p (k n) -> p k n", k=KC) for s in range(4)]
        B = [ctx.enter_context(nc.psum_tensor(f"bank{b}", [P, 512], F32)) for b in range(8)]

        w_loaded = [sem(f"w_loaded{s}") for s in range(4)]
        proj_done = [sem(f"proj_done{s}") for s in range(4)]
        pool_passed = sem("pool_passed")
        sp_passed = sem("sp_passed")
        params_in = sem("params_in")
        bias_in = sem("bias_in")
        x_in = sem("x_in")
        consts_ready = sem("consts_ready")
        lb_e_ready = sem("lb_e_ready")
        lam_e_ready = sem("lam_e_ready")
        lam_w_ready = sem("lam_w_ready")
        lam_l_ready = sem("lam_l_ready")

        NORMS = ("A", "F", "C", "Q")
        x_ready = {n: sem(f"x_ready_{n}") for n in NORMS}
        sq_ready = {n: sem(f"sq_ready_{n}") for n in NORMS}
        ss_done = {n: sem(f"ss_done_{n}") for n in NORMS}
        rstd_ready = {n: sem(f"rstd_ready_{n}") for n in NORMS}
        h_ready = {n: sem(f"h_ready_{n}") for n in NORMS}
        mixed = {n: sem(f"mixed_{n}") for n in "AFC"}

        def per_stage(stage, names):
            return {n: sem(f"{stage}_{n}") for n in names.split()}

        sA = per_stage("A", "fz_read qz_ready v_ready sig_ready gate_read f_ready lv_done at_ready o_done o_read "
                            "osq_ready oss_done ors_ready")
        sF = per_stage("F", "wf_in fz_done z_ready l_ready ksq_ready kss_done krs_ready kn_ready "
                            "qsq_ready qss_done qrs_ready qn_ready v_ready sig_ready gate_read sel_ready s_done "
                            "nmax_ready e_done p_ready pt_done pt_ready o_done o_read osq_ready oss_done ors_ready")
        sX = per_stage("X", "ckv_read csq_ready css_done crs_ready ckv_ready kw_ready kc_ready krs_ready "
                            "kn_ready kt_done kt_ready qi_ready rel_done relu_ready relu_used")
        sC = per_stage("C", "small_in xr_read xc_ready rg_done ri_read la_ready ex_ready prod_ready root_ready q_ready "
                            "kv_done kT_ready v_ready rsig_ready asig_ready mix_ready s_done nmax_ready e_done "
                            "p_ready pt_done pt_ready o_done o_read")
        sQ = per_stage("Q", "keys_in kt_done kt_ready xtr_done xtok_ready g_in tss_ready trs_ready htok_ready "
                            "qp_ready sc_done sc_ready idx0_ready idx1_ready sub_ready gexp_ready z_ready "
                            "g_ready diag_ready idx_u_copied idx_v_copied dots_done acc_done fss_ready frs_ready fin_ready stored")
        u_loaded = [sem(f"u_loaded{b}") for b in range(GB)]
        v_loaded = [sem(f"v_loaded{b}") for b in range(GB)]

        m = ExitStack()
        f0 = sb_in(m, "f0", [P, W2])
        k0 = sb_in(m, "k0", [P, W2])
        q_a = sb_in(m, "q_a", [P, W2])
        QL = [sb_in(m, f"QL{n}", [P, W2]) for n in range(LEVELS + 1)]
        KL = [sb_in(m, f"KL{n}", [P, W2]) for n in range(LEVELS + 1)]
        TL = [sb_in(m, f"TL{n}", [P, W2 >> n]) for n in range(LEVELS)]
        lmask = sb_in(m, "lmask", [P, LEVELS, P // 2])
        AT = sb_in(m, "AT", [P, 2 * NT, P])
        AToff = sb_in(m, "AToff", [P, 2, P])
        v_a = sb_in(m, "v_a", [P, NT, G])
        osq_a = sb_in(m, "osq_a", [P, W2])
        ors_a = sb_in(m, "ors_a", [P, W2])
        on_a = sb_in(m, "on_a", [P, W2])
        sig_a = sb_in(m, "sig_a", [P, W2])
        gate_a = sb_in(m, "gate_a", [P, W2])
        m.close()
        m = ExitStack()
        wf = sb_in(m, "wf", [P, KC, HEADS])
        fcum = sb_in(m, "fcum", [P, T])
        fneg = sb_in(m, "fneg", [P, T])
        fz = sb_in(m, "fz", [HEADS, 5, T])
        selF = sb_in(m, "selF", [P, 2, T])
        selO = sb_in(m, "selO", [P, 2, T])
        ksq = sb_in(m, "ksq", [P, W2])
        krs = sb_in(m, "krs", [P, W2])
        qsq = sb_in(m, "qsq", [P, W2])
        qrs = sb_in(m, "qrs", [P, W2])
        kT_f = sb_in(m, "kT_f", [P, 2, T])
        qT_f = sb_in(m, "qT_f", [P, 2, T])
        v_f = sb_in(m, "v_f", [P, NT, G])
        osq_f = sb_in(m, "osq_f", [P, W2])
        ors_f = sb_in(m, "ors_f", [P, W2])
        on_f = sb_in(m, "on_f", [P, W2])
        sig_f = sb_in(m, "sig_f", [P, W2])
        gate_f = sb_in(m, "gate_f", [P, W2])
        prob_f = sb_in(m, "prob_f", [P, 2, SC])
        probT_f = sb_in(m, "probT_f", [P, 2, SC])
        nmax_f = sb_in(m, "nmax_f", [P, 4])
        rsum_f = sb_in(m, "rsum_f", [P, 4])
        rinv_f = sb_in(m, "rinv_f", [P, 4])
        m.close()
        m = ExitStack()
        ckvT = sb_in(m, "ckvT", [P, RC, T])
        selmask = sb_in(m, "selmask", [P, SC])
        csq = hkvT[:, 0:RC, :]
        crs = sb_in(m, "crs", [P, T])
        kw = sb_in(m, "kw", [P, NT, IDX_DIM + IDX_HEADS])
        kc = sb_in(m, "kc", [P, NT, IDX_DIM])
        kdup = sb_in(m, "kdup", [P, NT, 2, IDX_DIM])
        kst = sb_in(m, "kst", [P, 4, NT])
        kiT = sb_in(m, "kiT", [P, T])
        qi = sb_in(m, "qi", [P, 2, W2])
        relu = hkvT[:, 4:10, :].rearrange("p k t -> p (k t)").rearrange("p (n s) -> p n s", n=4)
        iscore = sb_in(m, "iscore", [P, SC])
        top8 = sb_in(m, "top8", [P, 2, 8])
        uk = sb_in(m, "uk", [P, 2, RC, P])
        uv = sb_in(m, "uv", [P, RC, 2, P])
        wa = sb_in(m, "wa", [P, 2, P])
        wx = sb_in(m, "wx", [P, 2, P])
        xc = sb_in(m, "xc", [P, 2, T])
        rg = sb_in(m, "rg", [P, 2, 2, T])
        la = sb_in(m, "la", [P, W2])
        ae = hkvT[:, 10:16, :].rearrange("p (n k) t -> p n (k t)", n=3)
        ub = sb_in(m, "ub", [P, 2, W2])
        hs = sb_in(m, "hs", [P, W2])
        rsig = sb_in(m, "rsig", [P, W2])
        asig = sb_in(m, "asig", [P, W2])
        mixr = sb_in(m, "mixr", [P, W2])
        qT_c = sb_in(m, "qT_c", [P, 2, T])
        kT_c = sb_in(m, "kT_c", [P, 2, T])
        v_c = sb_in(m, "v_c", [P, NT, G])
        on_c = sb_in(m, "on_c", [P, W2])
        prob_c = sb_in(m, "prob_c", [P, 2, SC])
        probT_c = sb_in(m, "probT_c", [P, 2, SC])
        nmax_c = sb_in(m, "nmax_c", [P, 4])
        rsum_c = sb_in(m, "rsum_c", [P, 4])
        rinv_c = sb_in(m, "rinv_c", [P, 4])
        m.close()
        m = ExitStack()
        keys = sb_in(m, "keys", [P, 2, P])
        keysT = sb_in(m, "keysT", [P, 2, P])
        gffn = sb_in(m, "gffn", [P, D])
        gfin = sb_in(m, "gfin", [P, D])
        tstat = sb_in(m, "tstat", [P, 4, NT])
        qp = sb_in(m, "qp", [P, 2, 2, T])
        S12 = sb_in(m, "S12", [P, NT, PEER_HEADS, 2 * P])
        work = [sb_in(m, f"work{n}", [P, P]) for n in range(2)]
        rest = [sb_in(m, f"rest{n}", [P, P]) for n in range(2)]
        vtop = sb_in(m, "vtop", [P, 2, PEER_TOPK])
        itop = sb_in(m, "itop", [P, 2, PEER_TOPK], U32)
        itopf = sb_in(m, "itopf", [P, 2, PEER_TOPK])
        cand = sb_in(m, "cand", [P, PEER_TOPK * PEER_TOPK])
        cand2 = sb_in(m, "cand2", [P, PEER_TOPK * PEER_TOPK])
        ctop = sb_in(m, "ctop", [P, PEER_TOPK])
        cpos = sb_in(m, "cpos", [P, PEER_TOPK], U32)
        cab = sb_in(m, "cab", [P, 2, PEER_TOPK], U32)
        cabf = sb_in(m, "cabf", [P, 2, PEER_TOPK])
        iota16 = sb_in(m, "iota16", [P, PEER_TOPK])
        onehot = sb_in(m, "onehot", [P, 2, PEER_TOPK, PEER_TOPK])
        epart = sb_in(m, "epart", [P, 2, PEER_TOPK])
        tops = sb_in(m, "tops", [P, NT, PEER_HEADS, PEER_TOPK])
        gsum = sb_in(m, "gsum", [P, 2, PEER_HEADS])
        expert = sb_in(m, "expert", [P, NT, SLOTS_PER_TOKEN], I32)
        idx_u = sb_in(m, "idx_u", [P, GB], I32)
        idx_v = sb_in(m, "idx_v", [P, GB], I32)
        z4 = sb_in(m, "z4", [P, GB])
        g4 = sb_in(m, "g4", [P, GB])
        act4 = sb_in(m, "act4", [P, GB])
        diag = sb_in(m, "diag", [P, GB, P])
        fss = sb_in(m, "fss", [P, 8])
        m.close()
        x_tok = oT[:, :, :].rearrange("p (n k) t -> p n (k t)", n=NT)
        h_tok = hkvT[:, :, :].rearrange("p (n k) t -> p n (k t)", n=NT)
        y_tok1 = hT[:, 0:8, :].rearrange("p k t -> p (k t)")
        sq_scr = xT[:, 0:8, :].rearrange("p k t -> p (k t)")
        y_tok0 = hT[:, 8:16, :].rearrange("p k t -> p (k t)")
        ubuf = [Wm[:, b // 2, (b % 2) * D:(b % 2 + 1) * D] for b in range(GB)]
        vbuf = [Wm[:, 2 + b // 2, (b % 2) * D:(b % 2 + 1) * D] for b in range(GB)]

        def col(name, j):
            return prm[:, ds(j + PRM[name], 1)] if not isinstance(j, int) else prm[:, PRM[name] + j:PRM[name] + j + 1]

        def chunk(t, j, n=1):
            return t[:, ds(j, n), :].rearrange("p k t -> p (k t)")

        def halves(t, h):
            return t.rearrange("p (b two r) -> p b two r", two=2, r=h)

        def over(t, n):
            return t.unsqueeze(2).broadcast_to([P, t.shape[1], n])

        block = ctx.enter_context(nc.Block())

        @block.sync
        def _(eng):
            def load(stage, s, n, src):
                if past_zero(n + BASE[stage][s]):
                    eng.wait_ge(proj_done[s], n + BASE[stage][s])
                    eng.sem_inc(sp_passed, 1)
                eng.dma_start(W[s][:, :, 0:src.shape[2]], src).then_inc(w_loaded[s], 16)

            def cols(w, at, n=G):
                return w.rearrange("(k p) n -> p k n", p=P)[:, :, ds(at, n)]

            def pairs(stage, sources, more=None):
                def body(i):
                    for s, (w, at) in enumerate(sources):
                        load(stage, s, i, cols(w, i * G + at))
                        if s == 0 and more is not None:
                            more(i)
                body(0)
                with eng.Fori(1, PAIRS) as i:
                    body(i)

            def eight(stage, w):
                for g in range(KC // 2):
                    load(stage, g % 4, g // 4, cols(w, g * G))

            eng.dma_start(prm[:, :], prm_h).then_inc(params_in, 16)
            for c in range(4):
                eng.dma_start(xT[:, 4 * c:4 * c + 4, :], x_fm[:, 4 * c:4 * c + 4, :]).then_inc(x_in, 16)
            eng.dma_start(fbias[:, :], f_bias_h).then_inc(bias_in, 16)
            pairs("A", [(w_in_a, D), (w_in_a, 0), (w_in_a, 2 * D), (w_in_a, 3 * D)])
            eight("OA", w_out_a)
            eng.wait_ge(mixed["A"], PAIRS)
            eng.dma_start(wf[:, :, :], cols(w_kv, 2 * D, HEADS)).then_inc(sF["wf_in"], 16)
            pairs("F", [(w_kv, 0), (w_in_b, 0), (w_kv, D), (w_in_b, D)])
            eight("OF", w_out_b)
            load("X", 0, 0, cols(w_in_c, 2 * D))
            load("X", 1, 0, cols(w_in_c, 2 * D + G))
            q0 = 2 * D + KV_RANK
            load("X", 2, 0, cols(w_in_c, q0 + IDX_HEADS * IDX_DIM, IDX_DIM + IDX_HEADS))
            for g in range(4):
                load("X", 3 if g % 2 == 0 else 0, g // 2 + g % 2, cols(w_in_c, q0 + g * G))

            g0 = q0 + IDX_HEADS * IDX_DIM + IDX_DIM + IDX_HEADS

            def small(i):
                if past_zero(i * 2):
                    eng.wait_ge(sC["kv_done"], i * 2)
                    eng.sem_inc(sp_passed, 1)
                for dst, src in ((uk, w_uk[ds(i * 2, 2)].rearrange("h (c p) d -> p h c d", p=P)),
                                 (uv, w_uv[ds(i * 2, 2)].rearrange("h (c p) d -> p c h d", p=P))):
                    for j in range(2):
                        d_, s_ = (dst[:, j], src[:, j]) if dst is uk else (dst[:, :, j], src[:, :, j])
                        eng.dma_start(d_, s_).then_inc(sC["small_in"], 16)
                for dst, src in ((wa, rg_wa), (wx, rg_wx)):
                    eng.dma_start(dst[:, :, :], src[ds(i * 2, 2)].rearrange("n c d -> c n d")).then_inc(sC["small_in"], 16)

            pairs("C", [(w_in_c, 0), (w_in_c, D), (w_in_c, g0), (w_in_c, g0 + D)], small)
            eight("OC", w_out_c)
            eng.wait_ge(mixed["C"], PAIRS)
            for n, k_ in enumerate((keys1, keys2)):
                eng.dma_start(keys[:, n, :], k_).then_inc(sQ["keys_in"], 16)
            eng.dma_start(gffn[:, :], g_ffn.broadcast_to([P, D])).then_inc(sQ["g_in"], 16)
            eng.dma_start(gfin[:, :], g_fin.broadcast_to([P, D])).then_inc(sQ["g_in"], 16)
            eight("Q", w_q)
            for tile in range(NT):
                eng.wait_ge(sQ["fin_ready"], tile + 1)
                eng.dma_start(out[tile * P:(tile + 1) * P, :], y_tok0 if tile == 0 else y_tok1).then_inc(sQ["stored"], 16)
            eng.wait_ge(sQ["stored"], 16 * NT)

        @block.gpsimd
        def _(eng):
            eng.memset(ones[:, :], 1.0)
            eng.memset(eps[:, :], EPS)
            eng.memset(ident[:, :], 0.0)
            eng.memset(tri[:, :], 0.0)
            eng.memset(lmask[:, :, :], 1.0)
            eng.drain()
            eng.affine_select(out=ident[:, :], in_=ident[:, :], pattern=[[-1, P]], compare_op=ALU.not_equal, fill=1.0,
                              base=0, channel_multiplier=1)
            for a in (0, T):
                eng.affine_select(out=tri[:, a:a + P], in_=tri[:, a:a + P], pattern=[[-1, P]], compare_op=ALU.is_ge,
                                  fill=NEG, base=0, channel_multiplier=1)
            for l in range(LEVELS):
                h, nb = 1 << l, P >> (l + 1)
                v = lmask[:, l, :].rearrange("p (b r) -> p b r", r=h)
                eng.affine_select(out=v, in_=v, pattern=[[-2 * h, nb], [0, h]], compare_op=ALU.is_ge, fill=0.0,
                                  base=0, channel_multiplier=1)
            eng.drain()
            for l in range(LEVELS):
                h, nb = 1 << l, P >> (l + 1)
                v = lmask[:, l, :].rearrange("p (b r) -> p b r", r=h)
                last = eng.affine_select(out=v, in_=v, pattern=[[2 * h, nb], [0, h]], compare_op=ALU.is_ge, fill=0.0,
                                         base=h - 1, channel_multiplier=-1)
            eng.drain().then_inc(consts_ready, 1)

            eng.wait_ge(mixed["C"], PAIRS)
            eng.iota(iota16[:, :], pattern=[[1, PEER_TOPK]], base=0, channel_multiplier=0,
                     allow_small_or_imprecise_dtypes=True).then_inc(consts_ready, 1)
            for s in range(4):
                eng.wait_ge(proj_done[s], FILLED[s])

            def gather(idx, j, tile, table, bufs, used, copied, landed):
                n = tile * (SLOTS_PER_TOKEN // GB) + j
                for b in range(GB):
                    if past_zero((n - 1) * GB + b + 1):
                        eng.wait_ge(used, (n - 1) * GB + b + 1)
                    eng.tensor_copy(idx[:, b:b + 1], expert[:, tile, ds(j * GB + b, 1)]).then_inc(copied, 1)
                    eng.wait_ge(copied, n * GB + b + 1)
                    eng.sem_inc(pool_passed, 1)
                    eng.indirect_dma_start(out=bufs[b], out_offset=None, in_=table,
                                           in_offset=bass.IndirectOffsetOnAxis(ap=idx[:, b:b + 1], axis=0)
                                           ).then_inc(landed[b], 16)

            def gather_u(tile, j):
                gather(idx_u, j, tile, peer_u, ubuf, sQ["dots_done"], sQ["idx_u_copied"], u_loaded)

            def gather_v(tile, j):
                gather(idx_v, j, tile, peer_v, vbuf, sQ["acc_done"], sQ["idx_v_copied"], v_loaded)

            turns = SLOTS_PER_TOKEN // GB
            eng.wait_ge(sQ["idx0_ready"], PEER_HEADS)
            gather_u(0, 0)
            gather_u(0, 1)
            gather_v(0, 0)
            with eng.Fori(2, turns) as j:
                gather_u(0, j)
                gather_v(0, j - 1)
            eng.wait_ge(sQ["idx1_ready"], PEER_HEADS)
            gather_u(1, 0)
            gather_v(0, turns - 1)
            with eng.Fori(1, turns) as j:
                gather_u(1, j)
                gather_v(1, j - 1)
            gather_v(1, turns - 1)

        @block.tensor
        def _(eng):
            def enter(stage, s, i):
                eng.wait_ge(w_loaded[s], (i + (BASE[stage][s] + 1)) * 16)

            def project(stage, s, i, rhs):
                enter(stage, s, i)
                for j in range(2):
                    for k in range(KC):
                        last = eng.matmul(B[s][:, j * T:(j + 1) * T], W[s][:, k, j * P:(j + 1) * P], rhs[:, k, :],
                                          start=(k == 0), stop=(k == KC - 1))
                last.then_inc(proj_done[s], 1)

            def project_tok(stage, s, i, lhs, n=G):
                enter(stage, s, i)
                for t in range(NT):
                    for k in range(KC):
                        last = eng.matmul(B[s][:, t * n:(t + 1) * n], lhs[:, k, t * P:(t + 1) * P], W[s][:, k, 0:n],
                                          start=(k == 0), stop=(k == KC - 1))
                last.then_inc(proj_done[s], 1)

            def norm_sum(name, g):
                eng.wait_ge(sq_ready[name], g + 1)
                for c in range(2):
                    last = eng.matmul(B[4][:, 0:T], ones[:, :], sq[:, g % 4, c * T:(c + 1) * T],
                                      start=(g == 0 and c == 0), stop=(g == KC // 2 - 1 and c == 1))
                last.then_inc(ss_done[name], 1)

            def out_projection(stage, mixer, name):
                eng.wait_ge(mixed[mixer], PAIRS)
                for g in range(KC // 2):
                    if g >= 4:
                        if past_zero(g - 3):
                            eng.wait_ge(x_ready[name], g - 3)
                    project(stage, g % 4, g // 4, oT)
                    if g >= 1:
                        norm_sum(name, g - 1)
                norm_sum(name, KC // 2 - 1)

            def pair_loop(body):
                body(0, True)
                with eng.Fori(1, PAIRS) as i:
                    body(i, False)

            def head_sum(bank, src, done):
                eng.matmul(B[bank][:, :], ones[:, :], src[:, :], start=True, stop=True).then_inc(done, 1)

            def transpose_probs(prob, done):
                for j in range(2):
                    for a in range(3):
                        last = eng.transpose(B[6 + j][:, a * P:(a + 1) * P], prob[:, j, a * P:(a + 1) * P], ident[:, :])
                    last.then_inc(done, 1)

            def weigh_values(bank, v, probT, done):
                for j in range(2):
                    c = slice(j * P, (j + 1) * P)
                    o = j * T
                    eng.matmul(B[bank][:, o:o + P], v[:, 0, c], probT[:, j, 0:P], start=True, stop=True)
                    eng.matmul(B[bank][:, o + P:o + T], v[:, 0, c], probT[:, j, P:2 * P], start=True, stop=False)
                    last = eng.matmul(B[bank][:, o + P:o + T], v[:, 1, c], probT[:, j, 2 * P:3 * P], start=False, stop=True)
                last.then_inc(done, 1)

            eng.wait_ge(consts_ready, 1)
            for g in range(KC // 2):
                norm_sum("A", g)

            s = sA

            def a_values(i):
                eng.wait_ge(s["at_ready"], i + 1)
                eng.wait_ge(s["v_ready"], i + 1)
                for j in range(2):
                    c = slice(j * P, (j + 1) * P)
                    eng.matmul(B[4][:, j * T:j * T + P], v_a[:, 0, c], AT[:, 2 * j, :], start=True, stop=True)
                    eng.matmul(B[4][:, j * T + P:(j + 1) * T], v_a[:, 0, c], AToff[:, j, :], start=True, stop=False)
                    last = eng.matmul(B[4][:, j * T + P:(j + 1) * T], v_a[:, 1, c], AT[:, 2 * j + 1, :], start=False, stop=True)
                last.then_inc(s["o_done"], 1)

            def a_norm(i):
                eng.wait_ge(s["osq_ready"], i + 1)
                head_sum(5, osq_a, s["oss_done"])

            def a_levels(i):
                if past_zero(i):
                    eng.wait_ge(s["o_read"], i)
                    eng.wait_ge(s["ors_ready"], i)
                eng.wait_ge(s["f_ready"], i + 1)
                for j in range(2):
                    for t in range(NT):
                        a = j * T + t * P
                        eng.matmul(B[4][:, a:a + P], KL[0][:, a:a + P], q_a[:, a:a + P], start=True, stop=True)
                for l in range(LEVELS):
                    h = 1 << l
                    bank, at = (B[5 + l // 2], (l % 2) * T) if l < 6 else (B[3], 0)
                    if l == 6:
                        eng.wait_ge(s["gate_read"], i + 1)
                    for n in range(2 * NT):
                        last = eng.matmul(bank[:, at + n * (P // 2):at + (n + 1) * (P // 2)], KL[l][:, n * P:(n + 1) * P],
                                          halves(QL[l][:, n * P:(n + 1) * P], h)[:, :, 1, :], start=True, stop=True)
                for j in range(2):
                    last = eng.matmul(B[3][:, T + j * P:T + (j + 1) * P], KL[7][:, j * T:j * T + P],
                                      QL[7][:, j * T + P:(j + 1) * T], start=True, stop=True)
                last.then_inc(s["lv_done"], 1)

            def a_body(i, first):
                if first:
                    eng.wait_ge(h_ready["A"], KC)
                if past_zero(i):
                    eng.wait_ge(s["fz_read"], i)
                project("A", 0, i, hT)
                if not first:
                    a_values(i - 1)
                if past_zero(i):
                    eng.wait_ge(s["qz_ready"], i)
                project("A", 1, i, hT)
                if not first:
                    a_norm(i - 1)
                if past_zero(i):
                    eng.wait_ge(s["v_ready"], i)
                project_tok("A", 2, i, hT)
                if past_zero(i):
                    eng.wait_ge(s["at_ready"], i)
                project("A", 3, i, hT)
                a_levels(i)

            pair_loop(a_body)
            a_values(PAIRS - 1)
            a_norm(PAIRS - 1)
            out_projection("OA", "A", "F")

            s = sF
            eng.wait_ge(s["wf_in"], 16)
            eng.wait_ge(h_ready["F"], KC)
            for k in range(KC):
                last = eng.matmul(B[5][0:HEADS, 0:T], wf[:, k, :], hkvT[:, k, :], start=(k == 0), stop=(k == KC - 1))
            last.then_inc(s["fz_done"], 1)

            def f_transpose(i):
                eng.wait_ge(s["p_ready"], i + 1)
                transpose_probs(prob_f, s["pt_done"])

            def f_values(i):
                eng.wait_ge(s["pt_ready"], i + 1)
                eng.wait_ge(s["v_ready"], i + 1)
                weigh_values(5, v_f, probT_f, s["o_done"])

            def f_norm(i):
                eng.wait_ge(s["osq_ready"], i + 1)
                head_sum(6, osq_f, s["oss_done"])

            def f_body(i, first):
                if past_zero(i):
                    eng.wait_ge(s["kn_ready"], i)
                project("F", 0, i, hkvT)
                if first:
                    eng.wait_ge(h_ready["F"], 2 * KC)
                if not first:
                    f_transpose(i - 1)
                if past_zero(i):
                    eng.wait_ge(s["qn_ready"], i)
                project("F", 1, i, hT)
                eng.wait_ge(s["ksq_ready"], i + 1)
                if past_zero(i):
                    eng.wait_ge(s["qrs_ready"], i)
                head_sum(4, ksq, s["kss_done"])
                if not first:
                    f_values(i - 1)
                if past_zero(i):
                    eng.wait_ge(s["v_ready"], i)
                project_tok("F", 2, i, hkvT)
                eng.wait_ge(s["qsq_ready"], i + 1)
                eng.wait_ge(s["krs_ready"], i + 1)
                head_sum(4, qsq, s["qss_done"])
                if not first:
                    f_norm(i - 1)
                if past_zero(i):
                    eng.wait_ge(s["gate_read"], i)
                project("F", 3, i, hT)
                eng.wait_ge(s["kn_ready"], i + 1)
                eng.wait_ge(s["qn_ready"], i + 1)
                eng.wait_ge(s["sel_ready"], i + 1)
                if past_zero(i):
                    eng.wait_ge(s["ors_ready"], i)
                for j in range(2):
                    for t in range(NT):
                        n = (t + 1) * P
                        o = B[6 + j][:, t * P:t * P + n]
                        tt = slice(t * P, (t + 1) * P)
                        eng.matmul(o, qT_f[:, j, tt], kT_f[:, j, 0:n], start=True, stop=False)
                        eng.matmul(o, ones[:, :], selF[:, j, 0:n], start=False, stop=False)
                        last = eng.matmul(o, fcum[:, tt], selO[:, j, 0:n], start=False, stop=True)
                    last.then_inc(s["s_done"], 1)

            pair_loop(f_body)
            f_transpose(PAIRS - 1)
            f_values(PAIRS - 1)
            f_norm(PAIRS - 1)
            out_projection("OF", "F", "C")

            s = sX
            eng.wait_ge(h_ready["C"], KC)
            project("X", 0, 0, hT)
            project("X", 1, 0, hT)
            project_tok("X", 2, 0, hT, IDX_DIM + IDX_HEADS)
            eng.wait_ge(s["csq_ready"], 1)
            for c in range(RC):
                last = eng.matmul(B[4][:, 0:T], ones[:, :], csq[:, c, :], start=(c == 0), stop=(c == RC - 1))
            last.then_inc(s["css_done"], 1)
            for g in range(4):
                slot = 3 if g % 2 == 0 else 0
                if g == 1:
                    eng.wait_ge(s["ckv_read"], 1)
                if past_zero(g - 1):
                    eng.wait_ge(s["qi_ready"], g - 1)
                project("X", slot, g // 2 + g % 2, hT)
                if g == 0:
                    eng.wait_ge(s["kn_ready"], 1)
                    for t in range(NT):
                        last = eng.transpose(B[5][:, t * P:(t + 1) * P], kdup[:, t].rearrange("p a d -> p (a d)"), ident[:, :])
                    last.then_inc(s["kt_done"], 1)
                    eng.wait_ge(s["kt_ready"], 1)
                eng.wait_ge(s["qi_ready"], g + 1)
                for q in range(4):
                    n = 4 * g + q
                    b = 6 + n % 2
                    if past_zero(n - 1):
                        eng.wait_ge(s["relu_ready"], n - 1)
                    pr = slice(IDX_DIM * (q % 2), IDX_DIM * (q % 2 + 1))
                    for t in range(NT):
                        a = (q // 2) * T + t * P
                        last = eng.matmul(B[b][:, t * P:t * P + (t + 1) * P], qi[pr, g % 2, a:a + P], kiT[pr, 0:(t + 1) * P],
                                          start=True, stop=True)
                    last.then_inc(s["rel_done"], 1)
            eng.wait_ge(s["relu_ready"], IDX_HEADS)

            s = sC
            eng.wait_ge(sX["ckv_ready"], 1)

            def c_transpose(i):
                eng.wait_ge(s["p_ready"], i + 1)
                transpose_probs(prob_c, s["pt_done"])

            def c_values(i):
                eng.wait_ge(s["pt_ready"], i + 1)
                eng.wait_ge(s["v_ready"], i + 1)
                weigh_values(6, v_c, probT_c, s["o_done"])

            def c_body(i, first):
                if past_zero(i):
                    eng.wait_ge(s["xr_read"], i)
                project("C", 0, i, hT)
                if not first:
                    c_transpose(i - 1)
                if past_zero(i):
                    eng.wait_ge(s["q_ready"], i)
                project("C", 1, i, hT)
                eng.wait_ge(s["small_in"], (i + 1) * 96)
                eng.wait_ge(s["xc_ready"], i + 1)
                if past_zero(i):
                    eng.wait_ge(s["kT_ready"], i)
                    eng.wait_ge(s["v_ready"], i)
                for n, w in enumerate((wa, wx)):
                    for j in range(2):
                        last = eng.matmul(B[4 + n][:, j * T:(j + 1) * T], w[:, j, :], xc[:, j, :], start=True, stop=True)
                last.then_inc(s["rg_done"], 1)
                if not first:
                    c_values(i - 1)
                if past_zero(i):
                    eng.wait_ge(s["mix_ready"], i)
                project("C", 2, i, hT)
                eng.wait_ge(s["ri_read"], i + 1)
                for j in range(2):
                    for c in range(RC):
                        last = eng.matmul(B[4][:, j * T:(j + 1) * T], uk[:, j, c, :], ckvT[:, c, :],
                                          start=(c == 0), stop=(c == RC - 1))
                last.then_inc(s["kv_done"], 1)
                for t in range(NT):
                    for c in range(RC):
                        last = eng.matmul(B[5][:, t * G:(t + 1) * G], ckvT[:, c, t * P:(t + 1) * P],
                                          uv[:, c].rearrange("p h d -> p (h d)"), start=(c == 0), stop=(c == RC - 1))
                last.then_inc(s["kv_done"], 1)
                if past_zero(i):
                    eng.wait_ge(s["asig_ready"], i)
                project("C", 3, i, hT)
                eng.wait_ge(s["kT_ready"], i + 1)
                eng.wait_ge(s["q_ready"], i + 1)
                if past_zero(i):
                    eng.wait_ge(s["o_read"], i)
                for j in range(2):
                    for t in range(NT):
                        n = (t + 1) * P
                        last = eng.matmul(B[6 + j][:, t * P:t * P + n], qT_c[:, j, t * P:(t + 1) * P], kT_c[:, j, 0:n],
                                          start=True, stop=True)
                    last.then_inc(s["s_done"], 1)

            pair_loop(c_body)
            c_transpose(PAIRS - 1)
            c_values(PAIRS - 1)
            out_projection("OC", "C", "Q")

            s = sQ
            eng.wait_ge(s["keys_in"], 32)
            for n in range(2):
                last = eng.transpose(B[5][:, n * P:(n + 1) * P], keys[:, n, :], ident[:, :])
            last.then_inc(s["kt_done"], 1)
            for n in range(2 * 4):
                t, quarter = n // 4, n % 4
                b = 6 + n % 2
                if past_zero(n - 1):
                    eng.wait_ge(s["xtok_ready"], n - 1)
                for c in range(4):
                    last = eng.transpose(B[b][:, c * P:(c + 1) * P], xT[:, 4 * quarter + c, t * P:(t + 1) * P], ident[:, :])
                last.then_inc(s["xtr_done"], 1)
            eng.wait_ge(h_ready["Q"], KC)

            def key_scores(g):
                eng.wait_ge(s["qp_ready"], g + 1)
                if g == 0:
                    eng.wait_ge(s["kt_ready"], 1)
                if past_zero(g - 1):
                    eng.wait_ge(s["sc_ready"], g - 1)
                for t in range(NT):
                    for n in range(2):
                        last = eng.matmul(B[4 + g % 2][:, (2 * t + n) * P:(2 * t + n + 1) * P],
                                          qp[:, g % 2, n, t * P:(t + 1) * P], keysT[:, n, :], start=True, stop=True)
                last.then_inc(s["sc_done"], 1)

            for g in range(PEER_HEADS):
                if past_zero(g - 3):
                    eng.wait_ge(s["qp_ready"], g - 3)
                project("Q", g % 4, g // 4, hT)
                if g >= 1:
                    key_scores(g - 1)
            key_scores(PEER_HEADS - 1)

            def accumulate(tile, j, final):
                n = tile * (SLOTS_PER_TOKEN // GB) + j
                for b in range(GB):
                    eng.wait_ge(s["diag_ready"], n * GB + b + 1)
                    eng.wait_ge(v_loaded[b], (n + 1) * 16)
                    for c in range(4):
                        last = eng.matmul(B[4 * tile + c][:, :], diag[:, b, :], vbuf[b][:, c * 512:(c + 1) * 512],
                                          start=False, stop=(final and b == GB - 1), skip_group_check=True)
                    last.then_inc(s["acc_done"], 1)

            eng.wait_ge(s["xtok_ready"], 8)
            eng.wait_ge(s["sc_ready"], PEER_HEADS)
            for tile in range(NT):
                for c in range(4):
                    eng.matmul(B[4 * tile + c][:, :], ident[:, :], x_tok[:, tile, c * 512:(c + 1) * 512],
                               start=True, stop=False, skip_group_check=True)
                with eng.Fori(0, SLOTS_PER_TOKEN // GB - 1) as j:
                    accumulate(tile, j, False)
                accumulate(tile, SLOTS_PER_TOKEN // GB - 1, True)

        @block.scalar
        def _(eng):
            def rsqrt(out, src, scale):
                eng.activation(out, src, ACT.Ln, bias=eps[0:out.shape[0], 0:1], scale=scale)
                eng.drain()
                return eng.activation(out, out, ACT.Exp, scale=-0.5)

            def square_chunks(name, g):
                eng.wait_ge(x_ready[name], g + 1)
                if past_zero(g - 3):
                    eng.wait_ge(ss_done[name], g - 3)
                eng.activation(sq[:, g % 4, :], chunk(xT, 2 * g, 2), ACT.Square).then_inc(sq_ready[name], 1)

            def stream_norm(name):
                eng.wait_ge(ss_done[name], KC // 2)
                rsqrt(rstd[:, :], B[4][:, 0:T], 1.0 / D).then_inc(rstd_ready[name], 1)

            def pair_loop(body):
                body(0, True)
                with eng.Fori(1, PAIRS) as i:
                    body(i, False)

            eng.wait_ge(consts_ready, 1)
            eng.wait_ge(x_in, 64)
            for g in range(KC // 2):
                if past_zero(g - 3):
                    eng.wait_ge(ss_done["A"], g - 3)
                eng.activation(sq[:, g % 4, :], chunk(xT, 2 * g, 2), ACT.Square).then_inc(sq_ready["A"], 1)
            stream_norm("A")
            eng.wait_ge(lb_e_ready, 1)
            eng.activation(sp[:, 1, :], sp[:, 0, :], ACT.Exp).then_inc(lb_e_ready, 1)
            eng.wait_ge(lam_e_ready, 1)
            eng.activation(sp[:, 5, :], sp[:, 4, :], ACT.Exp, scale=-1.0).then_inc(lam_e_ready, 1)
            eng.wait_ge(lam_w_ready, 1)
            eng.activation(sp[:, 7, :], sp[:, 6, :], ACT.Ln).then_inc(lam_l_ready, 1)

            s = sA

            def a_body(i, first):
                eng.wait_ge(proj_done[0], i + (BASE["A"][0] + 1))
                if past_zero(i):
                    eng.wait_ge(s["f_ready"], i)
                eng.activation(f0[:, :], B[0][:, :], ACT.Sigmoid)
                eng.activation(k0[:, :], B[0][:, :], ACT.Sigmoid, scale=-1.0).then_inc(s["fz_read"], 1)
                if not first:
                    if past_zero(i):
                        eng.wait_ge(s["o_done"], i)
                    eng.activation(osq_a[:, :], B[4][:, :], ACT.Square).then_inc(s["osq_ready"], 1)
                eng.wait_ge(proj_done[1], i + (BASE["A"][1] + 1))
                if past_zero(i):
                    eng.wait_ge(s["lv_done"], i)
                eng.activation(q_a[:, :], B[1][:, :], ACT.Copy).then_inc(s["qz_ready"], 1)
                if not first:
                    a_rstd(i - 1)
                eng.wait_ge(proj_done[2], i + (BASE["A"][2] + 1))
                if past_zero(i):
                    eng.wait_ge(s["o_done"], i)
                eng.activation(v_a[:, :, :].rearrange("p t g -> p (t g)"), B[2][:, :], ACT.Copy).then_inc(s["v_ready"], 1)
                eng.wait_ge(proj_done[3], i + (BASE["A"][3] + 1))
                if past_zero(i):
                    eng.wait_ge(s["gate_read"], i)
                eng.activation(sig_a[:, :], B[3][:, :], ACT.Sigmoid).then_inc(s["sig_ready"], 1)

            def a_rstd(i):
                eng.wait_ge(s["oss_done"], i + 1)
                if past_zero(i):
                    eng.wait_ge(s["o_read"], i)
                rsqrt(ors_a[:, :], B[5][:, :], 1.0 / P).then_inc(s["ors_ready"], 1)

            pair_loop(a_body)
            eng.wait_ge(s["o_done"], PAIRS)
            eng.activation(osq_a[:, :], B[4][:, :], ACT.Square).then_inc(s["osq_ready"], 1)
            a_rstd(PAIRS - 1)
            for g in range(KC // 2):
                square_chunks("F", g)
            stream_norm("F")

            s = sF
            eng.wait_ge(s["z_ready"], 1)
            eng.activation(fz[:, 2, :], fz[:, 1, :], ACT.Exp, scale=-1.0)
            eng.drain()
            eng.activation(fz[:, 3, :], fz[:, 2, :], ACT.Ln, bias=ones[0:HEADS, 0:1]).then_inc(s["l_ready"], 1)

            def softmax_exp(s, i, prob, nmax, rsum):
                eng.wait_ge(s["nmax_ready"], i + 1)
                for j in range(2):
                    for t in range(NT):
                        p = prob[:, j, t * P:t * P + (t + 1) * P]
                        last = eng.activation(p, p, ACT.Exp, bias=nmax[:, 2 * j + t:2 * j + t + 1],
                                              accum_out=rsum[:, 2 * j + t:2 * j + t + 1])
                last.then_inc(s["e_done"], 1)

            def copy_probs(s, i, probT):
                if past_zero(i):
                    eng.wait_ge(s["o_done"], i)
                for j in range(2):
                    eng.wait_ge(s["pt_done"], i * 2 + j + 1)
                    last = eng.activation(probT[:, j, :], B[6 + j][:, 0:SC], ACT.Copy)
                last.then_inc(s["pt_ready"], 1)

            def f_square_out(i):
                eng.wait_ge(s["o_done"], i + 1)
                eng.activation(osq_f[:, :], B[5][:, :], ACT.Square).then_inc(s["osq_ready"], 1)

            def f_rstd_out(i):
                eng.wait_ge(s["oss_done"], i + 1)
                if past_zero(i):
                    eng.wait_ge(s["o_read"], i)
                rsqrt(ors_f[:, :], B[6][:, :], 1.0 / P).then_inc(s["ors_ready"], 1)

            def f_body(i, first):
                eng.wait_ge(proj_done[0], i + (BASE["F"][0] + 1))
                eng.activation(ksq[:, :], B[0][:, :], ACT.Square).then_inc(s["ksq_ready"], 1)
                if not first:
                    copy_probs(s, i - 1, probT_f)
                eng.wait_ge(proj_done[1], i + (BASE["F"][1] + 1))
                eng.activation(qsq[:, :], B[1][:, :], ACT.Square).then_inc(s["qsq_ready"], 1)
                eng.wait_ge(s["kss_done"], i + 1)
                if past_zero(i):
                    eng.wait_ge(s["kn_ready"], i)
                rsqrt(krs[:, :], B[4][:, :], 1.0 / P).then_inc(s["krs_ready"], 1)
                if not first:
                    f_square_out(i - 1)
                eng.wait_ge(proj_done[2], i + (BASE["F"][2] + 1))
                if past_zero(i):
                    eng.wait_ge(s["o_done"], i)
                eng.activation(v_f[:, :, :].rearrange("p t g -> p (t g)"), B[2][:, :], ACT.Copy).then_inc(s["v_ready"], 1)
                eng.wait_ge(s["qss_done"], i + 1)
                if past_zero(i):
                    eng.wait_ge(s["qn_ready"], i)
                rsqrt(qrs[:, :], B[4][:, :], 1.0 / P).then_inc(s["qrs_ready"], 1)
                if not first:
                    f_rstd_out(i - 1)
                eng.wait_ge(proj_done[3], i + (BASE["F"][3] + 1))
                if past_zero(i):
                    eng.wait_ge(s["gate_read"], i)
                eng.activation(sig_f[:, :], B[3][:, :], ACT.Sigmoid).then_inc(s["sig_ready"], 1)
                softmax_exp(s, i, prob_f, nmax_f, rsum_f)

            pair_loop(f_body)
            copy_probs(s, PAIRS - 1, probT_f)
            f_square_out(PAIRS - 1)
            f_rstd_out(PAIRS - 1)
            for g in range(KC // 2):
                square_chunks("C", g)
            stream_norm("C")

            s = sX
            for n in range(2):
                eng.wait_ge(proj_done[n], BASE["X"][n] + 1)
                eng.activation(csq[:, 2 * n:2 * n + 2, :].rearrange("p c t -> p (c t)"), B[n][:, :], ACT.Square)
            eng.drain().then_inc(s["csq_ready"], 1)
            eng.wait_ge(proj_done[2], BASE["X"][2] + 1)
            eng.activation(kw[:, :, :].rearrange("p t n -> p (t n)"), B[2][:, 0:NT * (IDX_DIM + IDX_HEADS)],
                           ACT.Copy).then_inc(s["kw_ready"], 1)
            eng.wait_ge(s["css_done"], 1)
            rsqrt(crs[:, :], B[4][:, 0:T], 1.0 / KV_RANK).then_inc(s["crs_ready"], 1)
            eng.wait_ge(s["kc_ready"], 1)
            for t in range(NT):
                eng.activation(kdup[:, t, 0, :], kc[:, t, :], ACT.Square, accum_out=kst[:, 1, t:t + 1])
            eng.drain()
            rsqrt(kst[:, 2, :], kst[:, 1, :], 1.0 / IDX_DIM).then_inc(s["krs_ready"], 1)
            for g in range(4):
                slot = 3 if g % 2 == 0 else 0
                eng.wait_ge(proj_done[slot], BASE["X"][slot] + g // 2 + g % 2 + 1)
                if past_zero(4 * (g - 1)):
                    eng.wait_ge(s["rel_done"], 4 * (g - 1))
                eng.activation(qi[:, g % 2, :], B[slot][:, :], ACT.Copy, scale=float(IDX_DIM) ** -0.5).then_inc(s["qi_ready"], 1)
                for q in range(4):
                    n = 4 * g + q
                    eng.wait_ge(s["rel_done"], n + 1)
                    if past_zero(n - 3):
                        eng.wait_ge(s["relu_used"], n - 3)
                    eng.activation(relu[:, n % 4, :], B[6 + n % 2][:, 0:SC], ACT.Relu).then_inc(s["relu_ready"], 1)

            s = sC

            def c_body(i, first):
                if not first:
                    copy_probs(s, i - 1, probT_c)
                eng.wait_ge(proj_done[1], i + (BASE["C"][1] + 1))
                if past_zero(i * 2):
                    eng.wait_ge(s["s_done"], i * 2)
                eng.activation(qT_c[:, :, :].rearrange("p h t -> p (h t)"), B[1][:, :], ACT.Copy,
                               scale=HD_SCALE).then_inc(s["q_ready"], 1)
                eng.wait_ge(s["rg_done"], i + 1)
                if past_zero(i):
                    eng.wait_ge(s["mix_ready"], i)
                for n, b in enumerate(("ba", "bx")):
                    for j in range(2):
                        last = eng.activation(rg[:, n, j, :], B[4 + n][:, j * T:(j + 1) * T], ACT.Sigmoid,
                                              bias=col(b, i * 2 + j))
                last.then_inc(s["ri_read"], 1)
                eng.wait_ge(s["la_ready"], i + 1)
                eng.activation(ae[:, 0, :], la[:, :], ACT.Exp)
                eng.activation(ae[:, 1, :], la[:, :], ACT.Exp, scale=2.0)
                eng.activation(ae[:, 2, :], la[:, :], ACT.Tanh, scale=-1.0).then_inc(s["ex_ready"], 1)
                eng.wait_ge(s["prod_ready"], i + 1)
                eng.activation(ub[:, 0, :], ub[:, 0, :], ACT.Sqrt).then_inc(s["root_ready"], 1)
                eng.wait_ge(proj_done[2], i + (BASE["C"][2] + 1))
                eng.activation(rsig[:, :], B[2][:, :], ACT.Sigmoid).then_inc(s["rsig_ready"], 1)
                eng.wait_ge(s["kv_done"], i * 2 + 1)
                eng.activation(kT_c[:, :, :].rearrange("p h t -> p (h t)"), B[4][:, :], ACT.Copy).then_inc(s["kT_ready"], 1)
                eng.wait_ge(s["kv_done"], i * 2 + 2)
                if past_zero(i):
                    eng.wait_ge(s["o_done"], i)
                eng.activation(v_c[:, :, :].rearrange("p t g -> p (t g)"), B[5][:, :], ACT.Copy).then_inc(s["v_ready"], 1)
                eng.wait_ge(proj_done[3], i + (BASE["C"][3] + 1))
                if past_zero(i):
                    eng.wait_ge(s["o_read"], i)
                eng.activation(asig[:, :], B[3][:, :], ACT.Sigmoid).then_inc(s["asig_ready"], 1)
                softmax_exp(s, i, prob_c, nmax_c, rsum_c)

            pair_loop(c_body)
            copy_probs(s, PAIRS - 1, probT_c)
            for g in range(KC // 2):
                square_chunks("Q", g)
            stream_norm("Q")

            s = sQ
            eng.wait_ge(s["kt_done"], 1)
            eng.activation(keysT[:, :, :].rearrange("p n k -> p (n k)"), B[5][:, 0:2 * P], ACT.Copy).then_inc(s["kt_ready"], 1)
            for n in range(8):
                t, quarter = n // 4, n % 4
                eng.wait_ge(s["xtr_done"], n + 1)
                eng.activation(x_tok[:, t, quarter * 512:(quarter + 1) * 512], B[6 + n % 2][:, :], ACT.Copy).then_inc(s["xtok_ready"], 1)
            eng.drain()
            eng.wait_ge(h_ready["Q"], KC)

            def evacuate(g):
                eng.wait_ge(proj_done[g % 4], BASE["Q"][g % 4] + g // 4 + 1)
                if past_zero(g - 1):
                    eng.wait_ge(s["sc_done"], g - 1)
                eng.activation(qp[:, g % 2, :, :].rearrange("p n t -> p (n t)"), B[g % 4][:, :], ACT.Copy).then_inc(s["qp_ready"], 1)

            def keep_scores(g):
                eng.wait_ge(s["sc_done"], g + 1)
                eng.activation(S12[:, :, g, :], B[4 + g % 2][:, :].rearrange("p (t n) -> p t n", t=NT), ACT.Copy).then_inc(s["sc_ready"], 1)

            for g in range(PEER_HEADS):
                evacuate(g)
                if g >= 1:
                    keep_scores(g - 1)
                if g < NT:
                    eng.activation(sq_scr, x_tok[:, g, :], ACT.Square, accum_out=tstat[:, 0, g:g + 1])
                    eng.drain()
                    rsqrt(tstat[:, 1, g:g + 1], tstat[:, 0, g:g + 1], 1.0 / D).then_inc(s["trs_ready"], 1)
            keep_scores(PEER_HEADS - 1)

            def gate_exp(tile):
                eng.wait_ge(s["sub_ready"], tile + 1)
                t_ = tops[:, tile].rearrange("p h k -> p (h k)")
                eng.activation(t_, t_, ACT.Exp).then_inc(s["gexp_ready"], 1)

            def gelu(tile, j):
                n = tile * (SLOTS_PER_TOKEN // GB) + j
                eng.wait_ge(s["z_ready"], n + 1)
                eng.activation(g4[:, :], z4[:, :], ACT.Gelu).then_inc(s["g_ready"], 1)

            gate_exp(0)
            with eng.Fori(0, PEER_HEADS) as j:
                gelu(0, j)
            gate_exp(1)
            with eng.Fori(PEER_HEADS, SLOTS_PER_TOKEN // GB) as j:
                gelu(0, j)

            def final_norm(tile):
                eng.wait_ge(s["acc_done"], (tile + 1) * SLOTS_PER_TOKEN)
                for c in range(4):
                    eng.activation(x_tok[:, tile, c * 512:(c + 1) * 512], B[4 * tile + c][:, :], ACT.Square,
                                   accum_out=fss[:, 4 * tile + c:4 * tile + c + 1])
                eng.drain().then_inc(s["fss_ready"], 1)
                eng.wait_ge(s["tss_ready"], tile + 1)
                rsqrt(tstat[:, 3, tile:tile + 1], tstat[:, 2, tile:tile + 1], 1.0 / D).then_inc(s["frs_ready"], 1)

            gelu(1, 0)
            gelu(1, 1)
            final_norm(0)
            with eng.Fori(2, SLOTS_PER_TOKEN // GB) as j:
                gelu(1, j)
            final_norm(1)

        @block.vector
        def _(eng):
            def stream_norm(name, outs):
                eng.wait_ge(rstd_ready[name], 1)
                for dst, weight in outs:
                    for c in range(KC):
                        eng.scalar_tensor_tensor(out=dst[:, c, :], in0=xT[:, c, :], scalar=col(weight, c), in1=rstd[:, :],
                                                 op0=ALU.mult, op1=ALU.mult).then_inc(h_ready[name], 1)

            def add_to_stream(stage, name):
                for g in range(KC // 2):
                    eng.wait_ge(proj_done[g % 4], BASE[stage][g % 4] + g // 4 + 1)
                    eng.tensor_tensor(chunk(xT, 2 * g, 2), B[g % 4][:, :], chunk(xT, 2 * g, 2), ALU.add).then_inc(x_ready[name], 1)

            def pair_loop(body):
                body(0, True)
                with eng.Fori(1, PAIRS) as i:
                    body(i, False)

            eng.wait_ge(params_in, 16)
            lbl = prm[:, PRM["a_lb"]:PRM["a_lb"] + KC]
            eng.tensor_tensor(sp[:, 0, :], lbl, lbl, ALU.subtract).then_inc(lb_e_ready, 1)
            lam = prm[:, PRM["lam"]:PRM["lam"] + KC]
            eng.tensor_scalar(sp[:, 3, :], lam, -1.0, 0.0, ALU.mult, ALU.max)
            eng.drain()
            eng.scalar_tensor_tensor(out=sp[:, 4, :], in0=sp[:, 3, :], scalar=2.0, in1=lam, op0=ALU.mult,
                                     op1=ALU.add).then_inc(lam_e_ready, 1)
            eng.tensor_scalar(qw[:, :], prm[:, PRM["q_norm"]:PRM["q_norm"] + 1], HD_SCALE, None, ALU.mult)
            for n in range(1, LEVELS + 1):
                eng.memset(KL[n][:, :], 0.0)
            eng.wait_ge(x_in, 64)
            eng.wait_ge(lb_e_ready, 2)
            eng.reciprocal(sp[:, 2, :], sp[:, 1, :])
            eng.drain()
            eng.tensor_tensor(sp[:, 0, :], sp[:, 1, :], sp[:, 2, :], ALU.mult)
            eng.drain()
            eng.tensor_tensor(lb[:, :], sp[:, 0, :], sp[:, 0, :], ALU.subtract)
            eng.drain()
            eng.tensor_scalar(omlb[:, :], lb[:, :], -1.0, 1.0, ALU.mult, ALU.add)
            eng.wait_ge(lam_e_ready, 2)
            eng.tensor_scalar(sp[:, 6, :], sp[:, 5, :], 1.0, None, ALU.add)
            eng.drain().then_inc(lam_w_ready, 1)
            eng.tensor_scalar(sp[:, 0, :], sp[:, 6, :], 1.0, None, ALU.is_equal)
            eng.drain()
            eng.scalar_tensor_tensor(out=sp[:, 1, :], in0=sp[:, 6, :], scalar=-1.0, in1=sp[:, 0, :], op0=ALU.add, op1=ALU.add)
            eng.drain()
            eng.reciprocal(sp[:, 2, :], sp[:, 1, :])
            eng.wait_ge(lam_l_ready, 1)
            eng.drain()
            eng.tensor_tensor(sp[:, 1, :], sp[:, 7, :], sp[:, 2, :], ALU.mult)
            eng.drain()
            eng.tensor_tensor(sp[:, 1, :], sp[:, 1, :], sp[:, 0, :], ALU.add)
            eng.drain()
            eng.tensor_tensor(sp[:, 1, :], sp[:, 1, :], sp[:, 5, :], ALU.mult)
            eng.drain()
            eng.tensor_tensor(sp[:, 1, :], sp[:, 1, :], sp[:, 3, :], ALU.add)
            eng.drain()
            eng.tensor_scalar(rg_c[:, :], sp[:, 1, :], -RG_C, None, ALU.mult)
            stream_norm("A", [(hT, "a_norm")])

            s = sA
            eng.wait_ge(consts_ready, 1)

            def decays(i):
                eng.wait_ge(s["fz_read"], i + 1)
                if past_zero(i):
                    eng.wait_ge(s["lv_done"], i)
                for j in range(2):
                    a = slice(j * T, (j + 1) * T)
                    eng.tensor_scalar(TL[0][:, a], f0[:, a], omlb[:, ds(i * 2 + j, 1)], lb[:, ds(i * 2 + j, 1)], ALU.mult, ALU.add)
                    eng.tensor_scalar(KL[0][:, a], k0[:, a], omlb[:, ds(i * 2 + j, 1)], None, ALU.mult)
                eng.drain()
                eng.wait_ge(s["qz_ready"], i + 1)
                eng.tensor_tensor(QL[0][:, :], q_a[:, :], TL[0][:, :], ALU.mult)
                eng.drain()
                for l in range(LEVELS):
                    h = 1 << l
                    seg = TL[l][:, :].rearrange("p (b two) -> p b two", two=2)
                    q0, q1 = halves(QL[l][:, :], h), halves(QL[l + 1][:, :], h)
                    k0_, k1_ = halves(KL[l][:, :], h), halves(KL[l + 1][:, :], h)
                    eng.tensor_tensor(q1[:, :, 1, :], q0[:, :, 1, :], over(seg[:, :, 0], h), ALU.mult)
                    eng.tensor_tensor(k1_[:, :, 0, :], k0_[:, :, 0, :], over(seg[:, :, 1], h), ALU.mult)
                    eng.tensor_copy(q1[:, :, 0, :], q0[:, :, 0, :])
                    last = eng.tensor_copy(k1_[:, :, 1, :], k0_[:, :, 1, :])
                    if l < LEVELS - 1:
                        eng.tensor_tensor(TL[l + 1][:, :], seg[:, :, 0], seg[:, :, 1], ALU.mult)
                        eng.drain()
                    else:
                        last.then_inc(s["f_ready"], 1)

            def gated_out(s, i, bank, ors, on, gate, weight, name):
                eng.wait_ge(s["ors_ready"], i + 1)
                eng.tensor_tensor(on[:, :], B[bank][:, :], ors[:, :], ALU.mult).then_inc(s["o_read"], 1)
                eng.drain()
                for j in range(2):
                    a = slice(j * T, (j + 1) * T)
                    last = eng.scalar_tensor_tensor(out=chunk(oT, i * 2 + j), in0=on[:, a], scalar=col(weight, i * 2 + j),
                                                    in1=gate[:, a], op0=ALU.mult, op1=ALU.mult)
                last.then_inc(mixed[name], 1)
                eng.drain()

            def a_masks(i):
                if past_zero(i):
                    eng.wait_ge(s["o_done"], i)
                eng.wait_ge(s["lv_done"], i + 1)
                eng.tensor_tensor(AT[:, :, :], B[4][:, :].rearrange("p (n t) -> p n t", n=2 * NT),
                                  ident[:, :].unsqueeze(1).broadcast_to([P, 2 * NT, P]), ALU.mult)
                eng.drain()
                for l in range(LEVELS):
                    h, nb = 1 << l, P >> (l + 1)
                    bank, at = (B[5 + l // 2], (l % 2) * T) if l < 6 else (B[3], 0)
                    dst = AT[:, :, :].rearrange("p n (b two r) -> p n b two r", two=2, r=h)[:, :, :, 1, :]
                    mask = lmask[:, l, :].bitcast(U32).rearrange("p (b r) -> p b r", r=h)
                    for n in range(2 * NT):
                        eng.copy_predicated(dst[:, n], mask, bank[:, at + n * (P // 2):at + (n + 1) * (P // 2)]
                                            .rearrange("p (b r) -> p b r", r=h))
                    eng.drain()
                eng.tensor_copy(AToff[:, :, :], B[3][:, T:2 * T].rearrange("p (j t) -> p j t", j=2))
                eng.drain().then_inc(s["at_ready"], 1)

            def a_body(i, first):
                decays(i)
                if not first:
                    gated_out(s, i - 1, 4, ors_a, on_a, gate_a, "a_onorm", "A")
                eng.wait_ge(s["sig_ready"], i + 1)
                eng.tensor_tensor(gate_a[:, :], B[3][:, :], sig_a[:, :], ALU.mult).then_inc(s["gate_read"], 1)
                a_masks(i)

            pair_loop(a_body)
            gated_out(s, PAIRS - 1, 4, ors_a, on_a, gate_a, "a_onorm", "A")
            add_to_stream("OA", "F")
            stream_norm("F", [(hkvT, "kv_norm"), (hT, "b_norm")])

            s = sF
            eng.memset(fcum[:, :], 0.0)
            eng.memset(fneg[:, :], 0.0)
            eng.wait_ge(bias_in, 16)
            eng.wait_ge(s["fz_done"], 1)
            eng.tensor_scalar(fz[:, 0, :], B[5][0:HEADS, 0:T], fbias[:, 0:1], None, ALU.add)
            eng.drain()
            eng.tensor_scalar(fz[:, 4, :], fz[:, 0, :], 0.0, None, ALU.min)
            eng.drain()
            eng.scalar_tensor_tensor(out=fz[:, 1, :], in0=fz[:, 4, :], scalar=-2.0, in1=fz[:, 0, :], op0=ALU.mult,
                                     op1=ALU.add).then_inc(s["z_ready"], 1)
            eng.wait_ge(s["l_ready"], 1)
            eng.tensor_tensor(fz[:, 0, :], fz[:, 4, :], fz[:, 3, :], ALU.subtract)
            eng.drain()
            eng.tensor_tensor_scan(out=fcum[0:HEADS, :], data0=ones[0:HEADS, 0:1].broadcast_to([HEADS, T]), data1=fz[:, 0, :],
                                   initial=0.0, op0=ALU.mult, op1=ALU.add)
            eng.drain()
            eng.tensor_scalar(fneg[0:HEADS, :], fcum[0:HEADS, :], -1.0, None, ALU.mult)
            eng.drain()

            def softmax_scores(s, i, prob, nmax, rsum, rinv, mask):
                if past_zero(i * 2):
                    eng.wait_ge(s["pt_done"], i * 2)
                for j in range(2):
                    eng.wait_ge(s["s_done"], i * 2 + j + 1)
                    eng.tensor_tensor(prob[:, j, :], B[6 + j][:, 0:SC], mask[:, :], ALU.add)
                eng.drain()
                for j in range(2):
                    for t in range(NT):
                        last = eng.tensor_reduce(nmax[:, 2 * j + t:2 * j + t + 1], prob[:, j, t * P:t * P + (t + 1) * P],
                                                 AX.X, ALU.max, negate=True)
                last.then_inc(s["nmax_ready"], 1)
                eng.wait_ge(s["e_done"], i + 1)
                eng.reciprocal(rinv[:, :], rsum[:, :])
                eng.drain()
                for j in range(2):
                    for t in range(NT):
                        p = prob[:, j, t * P:t * P + (t + 1) * P]
                        last = eng.tensor_scalar(p, p, rinv[:, 2 * j + t:2 * j + t + 1], None, ALU.mult)
                last.then_inc(s["p_ready"], 1)

            def f_body(i, first):
                if past_zero(i * 2):
                    eng.wait_ge(s["s_done"], i * 2)
                for j in range(2):
                    eng.tensor_scalar(selF[:, j, :], fneg[:, :], ident[:, ds(i * 2 + j, 1)], None, ALU.mult)
                    last = eng.tensor_copy(selO[:, j, :], ident[:, ds(i * 2 + j, 1)].broadcast_to([P, T]))
                last.then_inc(s["sel_ready"], 1)
                eng.wait_ge(s["krs_ready"], i + 1)
                eng.scalar_tensor_tensor(out=kT_f[:, :, :].rearrange("p h t -> p (h t)"), in0=B[0][:, :],
                                         scalar=col("k_norm", 0), in1=krs[:, :], op0=ALU.mult, op1=ALU.mult).then_inc(s["kn_ready"], 1)
                eng.wait_ge(s["qrs_ready"], i + 1)
                eng.scalar_tensor_tensor(out=qT_f[:, :, :].rearrange("p h t -> p (h t)"), in0=B[1][:, :], scalar=qw[:, 0:1],
                                         in1=qrs[:, :], op0=ALU.mult, op1=ALU.mult).then_inc(s["qn_ready"], 1)
                if not first:
                    gated_out(s, i - 1, 5, ors_f, on_f, gate_f, "b_onorm", "F")
                eng.wait_ge(s["sig_ready"], i + 1)
                eng.tensor_tensor(gate_f[:, :], B[3][:, :], sig_f[:, :], ALU.mult).then_inc(s["gate_read"], 1)
                softmax_scores(s, i, prob_f, nmax_f, rsum_f, rinv_f, tri)

            pair_loop(f_body)
            gated_out(s, PAIRS - 1, 5, ors_f, on_f, gate_f, "b_onorm", "F")
            add_to_stream("OF", "C")
            stream_norm("C", [(hT, "mix")])

            s = sX
            eng.wait_ge(s["kw_ready"], 1)
            for t in range(NT):
                eng.tensor_reduce(kst[:, 0, t:t + 1], kw[:, t, 0:IDX_DIM], AX.X, ALU.add)
            eng.drain()
            eng.tensor_scalar(kst[:, 3, :], kst[:, 0, :], -1.0 / IDX_DIM, None, ALU.mult)
            eng.drain()
            for t in range(NT):
                eng.tensor_scalar(kc[:, t, :], kw[:, t, 0:IDX_DIM], kst[:, 3, t:t + 1], None, ALU.add)
                eng.tensor_scalar(kw[:, t, IDX_DIM:], kw[:, t, IDX_DIM:], float(IDX_HEADS) ** -0.5, None, ALU.mult)
            eng.drain().then_inc(s["kc_ready"], 1)
            eng.wait_ge(s["crs_ready"], 1)
            for c in range(RC):
                last = eng.scalar_tensor_tensor(out=ckvT[:, c, :], in0=B[c // 2][:, (c % 2) * T:(c % 2 + 1) * T],
                                                scalar=col("ckv", c), in1=crs[:, :], op0=ALU.mult, op1=ALU.mult)
                if c == 1:
                    last.then_inc(s["ckv_read"], 1)
            last.then_inc(s["ckv_ready"], 1)
            eng.wait_ge(s["krs_ready"], 1)
            for t in range(NT):
                for a in range(2):
                    last = eng.tensor_scalar(kdup[:, t, a, :], kc[:, t, :], kst[:, 2, t:t + 1], None, ALU.mult)
            last.then_inc(s["kn_ready"], 1)
            eng.memset(iscore[:, :], 0.0)
            eng.wait_ge(s["kt_done"], 1)
            eng.tensor_scalar(kiT[:, :], B[5][:, 0:T], col("idx_g", 0), col("idx_b", 0), ALU.mult, ALU.add).then_inc(s["kt_ready"], 1)
            for n in range(IDX_HEADS):
                eng.wait_ge(s["relu_ready"], n + 1)
                eng.drain()
                for t in range(NT):
                    a = slice(t * P, t * P + (t + 1) * P)
                    last = eng.scalar_tensor_tensor(out=iscore[:, a], in0=relu[:, n % 4, a], scalar=kw[:, t, IDX_DIM + n:IDX_DIM + n + 1],
                                                    in1=iscore[:, a], op0=ALU.mult, op1=ALU.add)
                last.then_inc(s["relu_used"], 1)
            eng.drain()
            eng.tensor_tensor(iscore[:, :], iscore[:, :], tri[:, :], ALU.add)
            eng.drain()
            with eng.Fori(0, TOPK // 8) as _:
                for t in range(NT):
                    eng.max(top8[:, t, :], iscore[:, t * P:t * P + (t + 1) * P])
                eng.drain()
                for t in range(NT):
                    a = slice(t * P, t * P + (t + 1) * P)
                    eng.match_replace(iscore[:, a], top8[:, t, :], iscore[:, a], TAKEN)
                eng.drain()
            eng.tensor_scalar(selmask[:, :], iscore[:, :], -3.2e38, NEG, ALU.is_gt, ALU.mult)
            eng.drain()
            eng.tensor_tensor(selmask[:, :], selmask[:, :], tri[:, :], ALU.add)
            eng.drain()

            s = sC

            def c_tail(i):
                eng.wait_ge(s["o_done"], i + 1)
                eng.wait_ge(s["asig_ready"], i + 1)
                eng.tensor_tensor(on_c[:, :], B[6][:, :], asig[:, :], ALU.mult).then_inc(s["o_read"], 1)
                eng.drain()
                eng.tensor_tensor(chunk(oT, i * 2, 2), on_c[:, :], mixr[:, :], ALU.add).then_inc(mixed["C"], 1)

            def c_body(i, first):
                eng.wait_ge(proj_done[0], i + (BASE["C"][0] + 1))
                if past_zero(i):
                    eng.wait_ge(s["rg_done"], i)
                for j in range(2):
                    eng.tensor_scalar(xc[:, j, :], B[0][:, j * T:(j + 1) * T], col("cw3", i * 2 + j), col("cb", i * 2 + j),
                                      ALU.mult, ALU.add)
                for d in (1, 2, 3):
                    eng.drain()
                    for j in range(2):
                        last = eng.scalar_tensor_tensor(out=xc[:, j, d:T], in0=B[0][:, j * T:(j + 1) * T - d],
                                                        scalar=col(f"cw{3 - d}", i * 2 + j), in1=xc[:, j, d:T],
                                                        op0=ALU.mult, op1=ALU.add)
                last.then_inc(s["xr_read"], 1)
                eng.drain().then_inc(s["xc_ready"], 1)
                eng.wait_ge(s["ri_read"], i + 1)
                for j in range(2):
                    last = eng.tensor_scalar(la[:, j * T:(j + 1) * T], rg[:, 0, j, :], rg_c[:, ds(i * 2 + j, 1)], None, ALU.mult)
                last.then_inc(s["la_ready"], 1)
                eng.wait_ge(s["ex_ready"], i + 1)
                eng.scalar_tensor_tensor(out=ub[:, 0, :], in0=ae[:, 1, :], scalar=1.0, in1=ae[:, 2, :], op0=ALU.add,
                                         op1=ALU.mult).then_inc(s["prod_ready"], 1)
                eng.tensor_tensor(ub[:, 1, :], rg[:, 1].rearrange("p j t -> p (j t)"), xc[:, :, :].rearrange("p j t -> p (j t)"), ALU.mult)
                eng.drain()
                eng.wait_ge(s["root_ready"], i + 1)
                eng.tensor_tensor(ub[:, 1, :], ub[:, 1, :], ub[:, 0, :], ALU.mult)
                eng.drain()
                for j in range(2):
                    a = slice(j * T, (j + 1) * T)
                    eng.tensor_tensor_scan(out=hs[:, a], data0=ae[:, 0, a], data1=ub[:, 1, a], initial=0.0, op0=ALU.mult, op1=ALU.add)
                if not first:
                    c_tail(i - 1)
                eng.drain()
                eng.wait_ge(s["rsig_ready"], i + 1)
                eng.tensor_tensor(mixr[:, :], hs[:, :], rsig[:, :], ALU.mult).then_inc(s["mix_ready"], 1)
                softmax_scores(s, i, prob_c, nmax_c, rsum_c, rinv_c, selmask)

            pair_loop(c_body)
            c_tail(PAIRS - 1)
            add_to_stream("OC", "Q")
            stream_norm("Q", [(hT, "ffn")])

            s = sQ
            eng.wait_ge(s["g_in"], 32)
            for t in range(NT):
                eng.wait_ge(s["trs_ready"], t + 1)
                last = eng.scalar_tensor_tensor(out=h_tok[:, t, :], in0=x_tok[:, t, :], scalar=tstat[:, 1, t:t + 1], in1=gffn[:, :],
                                                op0=ALU.mult, op1=ALU.mult)
            eng.drain()
            eng.wait_ge(consts_ready, 2)

            def top16(vals, inds, src, scratch):
                for n in range(len(src)):
                    eng.max(vals[n][:, 0:8], src[n])
                eng.drain()
                for n in range(len(src)):
                    eng.max_index(inds[n][:, 0:8], vals[n][:, 0:8], src[n])
                    eng.match_replace(scratch[n], vals[n][:, 0:8], src[n], TAKEN)
                eng.drain()
                for n in range(len(src)):
                    eng.max(vals[n][:, 8:16], scratch[n])
                eng.drain()
                for n in range(len(src)):
                    eng.max_index(inds[n][:, 8:16], vals[n][:, 8:16], scratch[n])
                eng.drain()

            def pick(n, table, where):
                k = [P, PEER_TOPK, PEER_TOPK]
                eng.tensor_tensor(onehot[:, n], where.unsqueeze(2).broadcast_to(k), iota16[:, :].unsqueeze(1).broadcast_to(k), ALU.is_equal)
                eng.drain()
                eng.tensor_tensor(onehot[:, n], onehot[:, n], table.unsqueeze(1).broadcast_to(k), ALU.mult)
                eng.drain()
                eng.tensor_reduce(epart[:, n, :], onehot[:, n], AX.X, ALU.add)

            def route(tile, h):
                eng.wait_ge(s["sc_ready"], h + 1)
                for n in range(2):
                    eng.tensor_copy(work[n][:, :], S12[:, tile, ds(h, 1), n * P:(n + 1) * P].rearrange("p o k -> p (o k)"))
                eng.drain()
                top16([vtop[:, 0, :], vtop[:, 1, :]], [itop[:, 0, :], itop[:, 1, :]], [work[0][:, :], work[1][:, :]],
                      [rest[0][:, :], rest[1][:, :]])
                k = [P, PEER_TOPK, PEER_TOPK]
                eng.tensor_scalar(itopf[:, 0, :], itop[:, 0, :], float(P), None, ALU.mult)
                eng.tensor_copy(itopf[:, 1, :], itop[:, 1, :])
                eng.tensor_tensor(cand[:, :].rearrange("p (a b) -> p a b", a=PEER_TOPK), vtop[:, 0, :].unsqueeze(2).broadcast_to(k),
                                  vtop[:, 1, :].unsqueeze(1).broadcast_to(k), ALU.add)
                eng.drain()
                top16([ctop[:, :]], [cpos[:, :]], [cand[:, :]], [cand2[:, :]])
                eng.tensor_scalar(cab[:, 0, :], cpos[:, :], 4, None, ALU.logical_shift_right)
                eng.tensor_scalar(cab[:, 1, :], cpos[:, :], PEER_TOPK - 1, None, ALU.bitwise_and)
                eng.drain()
                eng.tensor_copy(cabf[:, :, :], cab[:, :, :])
                eng.drain()
                for n in range(2):
                    pick(n, itopf[:, n, :], cabf[:, n, :])
                eng.drain()
                eng.tensor_tensor(expert[:, tile, ds(h * PEER_TOPK, PEER_TOPK)], epart[:, 0, :], epart[:, 1, :], ALU.add)
                eng.tensor_copy(tops[:, tile, ds(h, 1), :].rearrange("p o k -> p (o k)"), ctop[:, :])
                eng.drain().then_inc(s["idx0_ready"] if tile == 0 else s["idx1_ready"], 1)

            def gates(tile):
                k = [P, PEER_HEADS, PEER_TOPK]
                t_ = tops[:, tile]
                eng.tensor_copy(gsum[:, 0, :], t_[:, :, 0])
                eng.drain()
                eng.tensor_tensor(t_, t_, gsum[:, 0, :].unsqueeze(2).broadcast_to(k), ALU.subtract).then_inc(s["sub_ready"], 1)
                eng.wait_ge(s["gexp_ready"], tile + 1)
                eng.tensor_reduce(gsum[:, 0, :], t_, AX.X, ALU.add)
                eng.drain()
                eng.reciprocal(gsum[:, 1, :], gsum[:, 0, :])
                eng.drain()
                eng.tensor_tensor(t_, t_, gsum[:, 1, :].unsqueeze(2).broadcast_to(k), ALU.mult)
                eng.drain()

            def dots(tile, j):
                n = tile * (SLOTS_PER_TOKEN // GB) + j
                for b in range(GB):
                    eng.wait_ge(u_loaded[b], (n + 1) * 16)
                    if b == 0:
                        if past_zero(n):
                            eng.wait_ge(s["g_ready"], n)
                    eng.tensor_tensor_reduce(out=ubuf[b], in0=ubuf[b], in1=h_tok[:, tile, :], scale=1.0, scalar=0.0,
                                             op0=ALU.mult, op1=ALU.add, accum_out=z4[:, b:b + 1]).then_inc(s["dots_done"], 1)
                eng.drain().then_inc(s["z_ready"], 1)
                eng.wait_ge(s["g_ready"], n + 1)
                eng.tensor_tensor(act4[:, :], g4[:, :], tops[:, tile].rearrange("p h k -> p (h k)")[:, ds(j * GB, GB)], ALU.mult)
                eng.drain()
                for b in range(GB):
                    if past_zero((n - 1) * GB + b + 1):
                        eng.wait_ge(s["acc_done"], (n - 1) * GB + b + 1)
                    eng.tensor_scalar(diag[:, b, :], ident[:, :], act4[:, b:b + 1], None, ALU.mult).then_inc(s["diag_ready"], 1)

            with eng.Fori(0, PEER_HEADS) as h:
                route(0, h)
            gates(0)
            dots(0, 0)
            route(1, 0)
            with eng.Fori(1, PEER_HEADS) as j:
                dots(0, j)
                route(1, j)
            gates(1)
            with eng.Fori(PEER_HEADS, SLOTS_PER_TOKEN // GB) as j:
                dots(0, j)

            def finish(tile, dst):
                eng.wait_ge(s["fss_ready"], tile + 1)
                eng.tensor_reduce(tstat[:, 2, tile:tile + 1], fss[:, 4 * tile:4 * tile + 4], AX.X, ALU.add).then_inc(s["tss_ready"], 1)
                eng.wait_ge(s["frs_ready"], tile + 1)
                for c in range(4):
                    a = slice(c * 512, (c + 1) * 512)
                    last = eng.scalar_tensor_tensor(out=dst[:, a], in0=B[4 * tile + c][:, :], scalar=tstat[:, 3, tile:tile + 1],
                                                    in1=gfin[:, a], op0=ALU.mult, op1=ALU.mult)
                last.then_inc(s["fin_ready"], 1)

            dots(1, 0)
            dots(1, 1)
            finish(0, y_tok0)
            with eng.Fori(2, SLOTS_PER_TOKEN // GB) as j:
                dots(1, j)
            eng.drain()
            finish(1, y_tok1)


def kernel(**inputs):
    import numpy as np
    import concourse.bacc as bacc
    from concourse.bass_utils import run_bass_kernel_spmd

    a = {k: np.asarray(v) for k, v in inputs.items()}

    def wide(v):
        return np.reshape(v, (KC, P)).T

    pack = [wide(a[n][0]) for n in ("a_norm_w", "a_lb_logits", "a_out_norm_w")]
    pack += [wide(a["kv_norm_w"]), wide(a["b_norm_w"][0]), wide(a["b_out_norm_w"][0]), wide(a["norm_mix_g_2"][0])]
    pack += [wide(a["conv_w_2"][0, n]) for n in range(4)]
    pack += [wide(a[n][0]) for n in ("conv_b_2", "rg_ba_2", "rg_bx_2", "rg_lambda_2", "norm_ffn_g_2")]
    pack += [a["k_norm_w"].reshape(P, 1), a["b_q_norm_w"].reshape(P, 1), a["kv_norm_g_2"].reshape(RC, P).T]
    pack += [np.concatenate([a[n][0], a[n][0]]).reshape(P, 1) for n in ("idx_ln_g_2", "idx_ln_b_2")]
    arrays = {
        "x_fm": a["x"][0].T.reshape(KC, P, T).transpose(1, 0, 2),
        "prm_h": np.concatenate(pack, axis=1),
        "f_bias_h": a["kv_f_bias"].reshape(HEADS, 1),
        "w_in_a": a["a_w_in"][0], "w_out_a": a["a_w_out"][0], "w_kv": a["kv_w"], "w_in_b": a["b_w_in"][0],
        "w_out_b": a["b_w_out"][0], "w_in_c": a["w_in_2"][0], "rg_wa": a["rg_wa_2"][0], "rg_wx": a["rg_wx_2"][0],
        "w_uk": a["w_uk_2"][0], "w_uv": a["w_uv_2"][0], "w_out_c": a["w_o_2"][0], "w_q": a["peer_wq_2"][0],
        "keys1": a["peer_keys1_2"][0], "keys2": a["peer_keys2_2"][0], "peer_u": a["peer_u_2"][0], "peer_v": a["peer_v_2"][0],
        "g_ffn": a["norm_ffn_g_2"], "g_fin": a["norm_final_g_2"].reshape(1, D),
    }
    arrays = {k: np.ascontiguousarray(v) for k, v in arrays.items()}
    nc = bacc.Bacc("TRN2", target_bir_lowering=False, num_devices=1)
    aps = {k: nc.dram_tensor(k, v.shape, F32, kind="ExternalInput").ap() for k, v in arrays.items()}
    out = nc.dram_tensor("out", (T, D), F32, kind="ExternalOutput").ap()
    program(nc, out=out, **aps)
    r = run_bass_kernel_spmd(nc, [arrays], core_ids=[0])
    return r.results[0]["out"].reshape(1, T, D)
```

```python
from contextlib import ExitStack

import concourse.bass as bass
from concourse import mybir

ALU = mybir.AluOpType
ACT = mybir.ActivationFunctionType
AX = mybir.AxisListType
F32 = mybir.dt.float32
F32R = mybir.dt.float32r
I32 = mybir.dt.int32
U32 = mybir.dt.uint32
ds = bass.ds

P = 128
D = 2048
T = 256
KC = D // P
NT = T // P
HEADS = 16
PAIRS = HEADS // 2
G = 2 * P
W2 = 2 * T
EPS = 1e-6
HD_SCALE = float(P) ** -0.5
LEVELS = 7
SC = P + T
NEG = -1e30
TAKEN = -3.3e38
KV_RANK = 512
RC = KV_RANK // P
IDX_HEADS = 16
IDX_DIM = 64
TOPK = min(256, T // 4)
RG_C = 8.0
PEER_HEADS = 8
PEER_TOPK = 16
SLOTS_PER_TOKEN = PEER_HEADS * PEER_TOPK
GB = 4

PRM = {}
for _n in ("a_norm", "a_lb", "a_onorm", "kv_norm", "b_norm", "b_onorm", "mix", "cw0", "cw1", "cw2", "cw3",
           "cb", "ba", "bx", "lam", "ffn"):
    PRM[_n] = len(PRM) * KC
PRM["k_norm"] = 16 * KC
PRM["q_norm"] = PRM["k_norm"] + 1
PRM["ckv"] = PRM["q_norm"] + 1
PRM["idx_g"] = PRM["ckv"] + RC
PRM["idx_b"] = PRM["idx_g"] + 1
NPRM = PRM["idx_b"] + 1

UNITS = {"A": 64, "OA": 16, "FG": 1, "F": 64, "OF": 16, "X": 13, "C": 64, "OC": 16, "Q": 16}
BASE = {}
_n = 0
for _k, _v in UNITS.items():
    BASE[_k] = _n
    _n += _v
ALL_UNITS = _n
PER_PAIR = 8
RAW = 4
NORM_AT = {"A": 0, "F": 1, "C": 2, "Q": 3}
SPLIT_AT = {"A": 0, "F": 8, "C": 24, "Q": 32}
MIX_AT = {"A": 0, "F": PAIRS, "C": 2 * PAIRS}


def past_zero(value):
    return not isinstance(value, int) or value > 0


def unit(i, c, per_unit, more):
    return i * (PER_PAIR * per_unit) + (c * per_unit + more)


def program(nc, x_fm, prm_h, f_bias_h, w_in_a, w_out_a, w_fgate, w_kv, w_in_b, w_out_b, w_latent, w_ikey, w_iquery, w_in_c,
            rg_wa, rg_wx, w_uk, w_uv, w_out_c, w_q, keys1, keys2, peer_u, peer_v, g_ffn, g_fin, out):
    ctx = ExitStack()
    with ctx:
        def sb_in(stack, name, shape, dt=F32):
            return stack.enter_context(nc.sbuf_tensor(name, shape, dt))

        def sem(name):
            return ctx.enter_context(nc.semaphore(name))

        def sb(name, shape, dt=F32):
            return sb_in(ctx, name, shape, dt)

        xT = sb("xT", [P, KC, T])
        hh = sb("hh", [P, KC, T], F32R)
        hl = sb("hl", [P, KC, T], F32R)
        oT = sb("oT", [P, KC, T])
        raw = sb("raw", [P, RAW, KC * P])
        iota16 = sb("iota16", [P, PEER_TOPK])
        prm = sb("prm", [P, NPRM])
        fbias = sb("fbias", [HEADS, 1])
        ident = sb("ident", [P, P])
        ones = sb("ones", [P, P])
        eps = sb("eps", [P, 1])
        lb = sb("lb", [P, KC])
        omlb = sb("omlb", [P, KC])
        rg_c = sb("rg_c", [P, KC])
        qw = sb("qw", [P, 1])
        sp = sb("sp", [P, 8, KC])
        tri = sb("tri", [P, SC])
        rstd = sb("rstd", [P, T])
        sq = sb("sq", [P, 2, W2])
        wsets = ExitStack()
        wh = [sb_in(wsets, f"wh{n}", [P, KC, P], F32R) for n in range(2)]
        wl = [sb_in(wsets, f"wl{n}", [P, KC, P], F32R) for n in range(2)]
        B = [ctx.enter_context(nc.psum_tensor(f"bank{b}", [P, 512], F32)) for b in range(8)]

        w_loaded = [sem(f"w_loaded{s}") for s in range(RAW)]
        hi_ready = sem("hi_ready")
        lo_ready = sem("lo_ready")
        mm_done = sem("mm_done")
        pool_passed = sem("pool_passed")
        sp_passed = sem("sp_passed")
        params_in = sem("params_in")
        bias_in = sem("bias_in")
        x_in = sem("x_in")
        consts_ready = sem("consts_ready")
        lb_e_ready = sem("lb_e_ready")
        lam_e_ready = sem("lam_e_ready")
        lam_w_ready = sem("lam_w_ready")
        lam_l_ready = sem("lam_l_ready")

        x_ready = sem("x_ready")
        sq_ready = sem("sq_ready")
        ss_done = sem("ss_done")
        rstd_ready = sem("rstd_ready")
        hf_ready = sem("hf_ready")
        hh_ready = sem("hh_ready")
        hl_ready = sem("hl_ready")
        mixed = sem("mixed")
        oh_ready = sem("oh_ready")
        ol_ready = sem("ol_ready")

        def per_stage(stage, names):
            return {n: sem(f"{stage}_{n}") for n in names.split()}

        sA = per_stage("A", "fz_read qz_ready v_ready sig_ready gate_read f_ready lv_done at_ready o_done o_read "
                            "osq_ready oss_done ors_ready")
        sF = per_stage("F", "fz_read fzt_done z_ready l_ready ksq_ready kss_done krs_ready kn_ready "
                            "qsq_ready qss_done qrs_ready qn_ready v_ready sig_ready gate_read sel_ready s_done "
                            "nmax_ready e_done p_ready pt_done pt_ready o_done o_read osq_ready oss_done ors_ready")
        sX = per_stage("X", "ckv_read csq_ready css_done crs_ready ckv_ready kw_ready kc_ready krs_ready "
                            "kn_ready kt_done kt_ready qi_ready rel_done relu_ready relu_used")
        sC = per_stage("C", "small_in xr_read xc_ready rg_done ri_read la_ready ex_ready prod_ready root_ready q_ready "
                            "kv_done kT_ready v_ready rsig_ready asig_ready mix_ready s_done nmax_ready e_done "
                            "p_ready pt_done pt_ready o_done o_read")
        sQ = per_stage("Q", "keys_in kt_done kt_ready xtr_done xtok_ready g_in tss_ready trs_ready htok_ready "
                            "qp_ready sc_done sc_ready idx0_ready idx1_ready sub_ready gexp_ready z_ready "
                            "g_ready diag_ready idx_u_copied idx_v_copied dots_done acc_done fss_ready frs_ready fin_ready stored")
        u_loaded = [sem(f"u_loaded{b}") for b in range(GB)]
        v_loaded = [sem(f"v_loaded{b}") for b in range(GB)]

        m = ExitStack()
        f0 = sb_in(m, "f0", [P, W2])
        k0 = sb_in(m, "k0", [P, W2])
        q_a = sb_in(m, "q_a", [P, W2])
        QL = [sb_in(m, f"QL{n}", [P, W2]) for n in range(LEVELS + 1)]
        KL = [sb_in(m, f"KL{n}", [P, W2]) for n in range(LEVELS + 1)]
        TL = [sb_in(m, f"TL{n}", [P, W2 >> n]) for n in range(LEVELS)]
        lmask = sb_in(m, "lmask", [P, LEVELS, P // 2])
        AT = sb_in(m, "AT", [P, 2 * NT, P])
        AToff = sb_in(m, "AToff", [P, 2, P])
        v_a = sb_in(m, "v_a", [P, NT, G])
        osq_a = sb_in(m, "osq_a", [P, W2])
        ors_a = sb_in(m, "ors_a", [P, W2])
        on_a = sb_in(m, "on_a", [P, W2])
        sig_a = sb_in(m, "sig_a", [P, W2])
        gate_a = sb_in(m, "gate_a", [P, W2])
        m.close()
        m = ExitStack()
        kh = sb_in(m, "kh", [P, KC, T], F32R)
        kl = sb_in(m, "kl", [P, KC, T], F32R)
        fz_tok = sb_in(m, "fz_tok", [P, NT, HEADS])
        fcum = sb_in(m, "fcum", [P, T])
        fneg = sb_in(m, "fneg", [P, T])
        selF = sb_in(m, "selF", [P, 2, T])
        selO = sb_in(m, "selO", [P, 2, T])
        ksq = sb_in(m, "ksq", [P, W2])
        krs = sb_in(m, "krs", [P, W2])
        qsq = sb_in(m, "qsq", [P, W2])
        qrs = sb_in(m, "qrs", [P, W2])
        kT_f = sb_in(m, "kT_f", [P, 2, T])
        qT_f = sb_in(m, "qT_f", [P, 2, T])
        v_f = sb_in(m, "v_f", [P, NT, G])
        osq_f = sb_in(m, "osq_f", [P, W2])
        ors_f = sb_in(m, "ors_f", [P, W2])
        on_f = sb_in(m, "on_f", [P, W2])
        sig_f = sb_in(m, "sig_f", [P, W2])
        gate_f = sb_in(m, "gate_f", [P, W2])
        prob_f = sb_in(m, "prob_f", [P, 2, SC])
        probT_f = sb_in(m, "probT_f", [P, 2, SC])
        fz = [(prob_f if n < 3 else probT_f)[0:HEADS, :, :].rearrange("p a b -> p (a b)")[:, (n % 3) * T:(n % 3 + 1) * T]
              for n in range(5)]
        nmax_f = sb_in(m, "nmax_f", [P, 4])
        rsum_f = sb_in(m, "rsum_f", [P, 4])
        rinv_f = sb_in(m, "rinv_f", [P, 4])
        m.close()
        m = ExitStack()
        ckvT = sb_in(m, "ckvT", [P, RC, T])
        selmask = sb_in(m, "selmask", [P, SC])
        iscore = sb_in(m, "iscore", [P, SC])
        top8 = sb_in(m, "top8", [P, 2, 8])
        x = ExitStack()
        csq = sb_in(x, "csq", [P, RC, T])
        crs = sb_in(x, "crs", [P, T])
        kw = sb_in(x, "kw", [P, NT, IDX_DIM + IDX_HEADS])
        kc = sb_in(x, "kc", [P, NT, IDX_DIM])
        kdup = sb_in(x, "kdup", [P, NT, 2, IDX_DIM])
        kst = sb_in(x, "kst", [P, 4, NT])
        kiT = sb_in(x, "kiT", [P, T])
        qi = sb_in(x, "qi", [P, 2, W2])
        relu = sb_in(x, "relu", [P, 4, SC])
        x.close()
        uk = sb_in(m, "uk", [P, 2, RC, P])
        uv = sb_in(m, "uv", [P, RC, 2, P])
        wa = sb_in(m, "wa", [P, 2, P])
        wx = sb_in(m, "wx", [P, 2, P])
        xc = sb_in(m, "xc", [P, 2, T])
        rg = sb_in(m, "rg", [P, 2, 2, T])
        la = sb_in(m, "la", [P, W2])
        ae = sb_in(m, "ae", [P, 3, W2])
        ub = sb_in(m, "ub", [P, 2, W2])
        hs = sb_in(m, "hs", [P, W2])
        rsig = sb_in(m, "rsig", [P, W2])
        asig = sb_in(m, "asig", [P, W2])
        mixr = sb_in(m, "mixr", [P, W2])
        qT_c = sb_in(m, "qT_c", [P, 2, T])
        kT_c = sb_in(m, "kT_c", [P, 2, T])
        v_c = sb_in(m, "v_c", [P, NT, G])
        on_c = sb_in(m, "on_c", [P, W2])
        prob_c = sb_in(m, "prob_c", [P, 2, SC])
        probT_c = sb_in(m, "probT_c", [P, 2, SC])
        nmax_c = sb_in(m, "nmax_c", [P, 4])
        rsum_c = sb_in(m, "rsum_c", [P, 4])
        rinv_c = sb_in(m, "rinv_c", [P, 4])
        m.close()
        wsets.close()
        m = ExitStack()
        vrows = sb_in(m, "vrows", [P, GB, D])
        x_tok = sb_in(m, "x_tok", [P, NT, D])
        h_tok = sb_in(m, "h_tok", [P, NT, D])
        keys = sb_in(m, "keys", [P, 2, P])
        keysT = sb_in(m, "keysT", [P, 2, P])
        gffn = sb_in(m, "gffn", [P, D])
        gfin = sb_in(m, "gfin", [P, D])
        tstat = sb_in(m, "tstat", [P, 4, NT])
        qp = sb_in(m, "qp", [P, 2, 2, T])
        work = [sb_in(m, f"work{n}", [P, P]) for n in range(2)]
        rest = [sb_in(m, f"rest{n}", [P, P]) for n in range(2)]
        vtop = sb_in(m, "vtop", [P, 2, PEER_TOPK])
        itop = sb_in(m, "itop", [P, 2, PEER_TOPK], U32)
        itopf = sb_in(m, "itopf", [P, 2, PEER_TOPK])
        cand = sb_in(m, "cand", [P, PEER_TOPK * PEER_TOPK])
        cand2 = sb_in(m, "cand2", [P, PEER_TOPK * PEER_TOPK])
        ctop = sb_in(m, "ctop", [P, PEER_TOPK])
        cpos = sb_in(m, "cpos", [P, PEER_TOPK], U32)
        cab = sb_in(m, "cab", [P, 2, PEER_TOPK], U32)
        cabf = sb_in(m, "cabf", [P, 2, PEER_TOPK])
        onehot = sb_in(m, "onehot", [P, 2, PEER_TOPK, PEER_TOPK])
        epart = sb_in(m, "epart", [P, 2, PEER_TOPK])
        tops = sb_in(m, "tops", [P, NT, PEER_HEADS, PEER_TOPK])
        gsum = sb_in(m, "gsum", [P, 2, PEER_HEADS])
        expert = sb_in(m, "expert", [P, NT, SLOTS_PER_TOKEN], I32)
        idx_u = sb_in(m, "idx_u", [P, GB], I32)
        idx_v = sb_in(m, "idx_v", [P, GB], I32)
        z4 = sb_in(m, "z4", [P, GB])
        g4 = sb_in(m, "g4", [P, GB])
        act4 = sb_in(m, "act4", [P, GB])
        diag = sb_in(m, "diag", [P, GB, P])
        fss = sb_in(m, "fss", [P, 8])
        m.close()
        S12 = oT[:, :, :].rearrange("p (n h) t -> p n h t", n=NT)
        sq_scr = xT[:, 0:8, :].rearrange("p k t -> p (k t)")
        y_tok = [xT[:, 8 * n:8 * n + 8, :].rearrange("p k t -> p (k t)") for n in range(NT)]
        ubuf = [raw[:, b, :] for b in range(GB)]
        vbuf = [vrows[:, b, :] for b in range(GB)]

        def col(name, j):
            return prm[:, ds(j + PRM[name], 1)] if not isinstance(j, int) else prm[:, PRM[name] + j:PRM[name] + j + 1]

        def chunk(t, j, n=1):
            return t[:, ds(j, n), :].rearrange("p k t -> p (k t)")

        def halves(t, h):
            return t.rearrange("p (b two r) -> p b two r", two=2, r=h)

        def over(t, n):
            return t.unsqueeze(2).broadcast_to([P, t.shape[1], n])

        block = ctx.enter_context(nc.Block())

        @block.sync
        def _(eng):
            def load(i, c, src):
                if past_zero(unit(i, c, 2, 2 - 2 * RAW)):
                    eng.wait_ge(lo_ready, unit(i, c, 2, 2 - 2 * RAW))
                    eng.sem_inc(sp_passed, 1)
                eng.dma_start(raw[:, c % RAW, :], src).then_inc(w_loaded[c % RAW], 16)

            def one(w, n):
                return w[ds(n, 1)].rearrange("o p n -> p (o n)")

            def pairs(stage, sources, more=None):
                def body(i):
                    for r, (w, at) in enumerate(sources):
                        for j in range(2):
                            load(i, BASE[stage] + 2 * r + j, one(w, i * 2 + (at + j)))
                        if r == 1 and more is not None:
                            more(i)
                body(0)
                with eng.Fori(1, PAIRS) as i:
                    body(i)

            def row(stage, w, n, first=0):
                for c in range(n):
                    load(0, BASE[stage] + first + c, one(w, c))

            eng.dma_start(prm[:, :], prm_h).then_inc(params_in, 16)
            for c in range(4):
                eng.dma_start(xT[:, 4 * c:4 * c + 4, :], x_fm[:, 4 * c:4 * c + 4, :]).then_inc(x_in, 16)
            eng.dma_start(fbias[:, :], f_bias_h).then_inc(bias_in, 16)
            pairs("A", [(w_in_a, HEADS), (w_in_a, 0), (w_in_a, 2 * HEADS), (w_in_a, 3 * HEADS)])
            row("OA", w_out_a, KC)
            row("FG", w_fgate, 1)
            pairs("F", [(w_kv, 0), (w_in_b, 0), (w_kv, HEADS), (w_in_b, HEADS)])
            row("OF", w_out_b, KC)
            row("X", w_latent, RC)
            row("X", w_ikey, 1, RC)
            row("X", w_iquery, PEER_HEADS, RC + 1)

            def small(i):
                if past_zero(i * 2):
                    eng.wait_ge(sC["kv_done"], i * 2)
                    eng.sem_inc(sp_passed, 1)
                else:
                    eng.wait_ge(sX["relu_used"], IDX_HEADS)
                for j in range(2):
                    eng.dma_start(uk[:, j], w_uk[ds(i * 2 + j, 1)].rearrange("h (c p) d -> p (h c) d", p=P)).then_inc(sC["small_in"], 16)
                    eng.dma_start(uv[:, :, j], w_uv[ds(i * 2 + j, 1)].rearrange("h (c p) d -> p (h c) d", p=P)).then_inc(sC["small_in"], 16)
                for dst, src in ((wa, rg_wa), (wx, rg_wx)):
                    eng.dma_start(dst[:, :, :], src[ds(i * 2, 2)].rearrange("n c d -> c n d")).then_inc(sC["small_in"], 16)

            pairs("C", [(w_in_c, 0), (w_in_c, HEADS), (w_in_c, 2 * HEADS), (w_in_c, 3 * HEADS)], small)
            row("OC", w_out_c, KC)
            eng.wait_ge(mixed, MIX_AT["C"] + PAIRS)
            for n, k_ in enumerate((keys1, keys2)):
                eng.dma_start(keys[:, n, :], k_).then_inc(sQ["keys_in"], 16)
            eng.dma_start(gffn[:, :], g_ffn.broadcast_to([P, D])).then_inc(sQ["g_in"], 16)
            eng.dma_start(gfin[:, :], g_fin.broadcast_to([P, D])).then_inc(sQ["g_in"], 16)
            row("Q", w_q, KC)
            for tile in range(NT):
                eng.wait_ge(sQ["fin_ready"], tile + 1)
                eng.dma_start(out[tile * P:(tile + 1) * P, :], y_tok[tile]).then_inc(sQ["stored"], 16)
            eng.wait_ge(sQ["stored"], 16 * NT)

        @block.gpsimd
        def _(eng):
            eng.memset(ones[:, :], 1.0)
            eng.memset(eps[:, :], EPS)
            eng.memset(ident[:, :], 0.0)
            eng.memset(tri[:, :], 0.0)
            eng.memset(lmask[:, :, :], 1.0)
            eng.drain()
            eng.affine_select(out=ident[:, :], in_=ident[:, :], pattern=[[-1, P]], compare_op=ALU.not_equal, fill=1.0,
                              base=0, channel_multiplier=1)
            for a in (0, T):
                eng.affine_select(out=tri[:, a:a + P], in_=tri[:, a:a + P], pattern=[[-1, P]], compare_op=ALU.is_ge,
                                  fill=NEG, base=0, channel_multiplier=1)
            for l in range(LEVELS):
                h, nb = 1 << l, P >> (l + 1)
                v = lmask[:, l, :].rearrange("p (b r) -> p b r", r=h)
                eng.affine_select(out=v, in_=v, pattern=[[-2 * h, nb], [0, h]], compare_op=ALU.is_ge, fill=0.0,
                                  base=0, channel_multiplier=1)
            eng.drain()
            for l in range(LEVELS):
                h, nb = 1 << l, P >> (l + 1)
                v = lmask[:, l, :].rearrange("p (b r) -> p b r", r=h)
                last = eng.affine_select(out=v, in_=v, pattern=[[2 * h, nb], [0, h]], compare_op=ALU.is_ge, fill=0.0,
                                         base=h - 1, channel_multiplier=-1)
            eng.drain().then_inc(consts_ready, 1)

            eng.iota(iota16[:, :], pattern=[[1, PEER_TOPK]], base=0, channel_multiplier=0,
                     allow_small_or_imprecise_dtypes=True).then_inc(consts_ready, 1)

            def low_part(i, c):
                for half in range(2):
                    k = slice(half * KC // 2, (half + 1) * KC // 2)
                    eng.wait_ge(hi_ready, i * (2 * RAW) + (2 * c + half + 1))
                    eng.tensor_tensor(wl[c % 2][:, k, :], raw[:, c % RAW, :].rearrange("p (k n) -> p k n", k=KC)[:, k, :],
                                      wh[c % 2][:, k, :].bitcast(F32), ALU.subtract).then_inc(lo_ready, 1)

            with eng.Fori(0, ALL_UNITS // RAW) as i:
                for c in range(RAW):
                    low_part(i, c)
            for c in range(ALL_UNITS % RAW):
                low_part(ALL_UNITS // RAW, c)

            eng.wait_ge(mm_done, 2 * ALL_UNITS)

            def gather(idx, j, tile, table, bufs, used, copied, landed):
                n = tile * (SLOTS_PER_TOKEN // GB) + j
                for b in range(GB):
                    if past_zero((n - 1) * GB + b + 1):
                        eng.wait_ge(used, (n - 1) * GB + b + 1)
                    eng.tensor_copy(idx[:, b:b + 1], expert[:, tile, ds(j * GB + b, 1)]).then_inc(copied, 1)
                    eng.wait_ge(copied, n * GB + b + 1)
                    eng.sem_inc(pool_passed, 1)
                    eng.indirect_dma_start(out=bufs[b], out_offset=None, in_=table,
                                           in_offset=bass.IndirectOffsetOnAxis(ap=idx[:, b:b + 1], axis=0)
                                           ).then_inc(landed[b], 16)

            def gather_u(tile, j):
                gather(idx_u, j, tile, peer_u, ubuf, sQ["dots_done"], sQ["idx_u_copied"], u_loaded)

            def gather_v(tile, j):
                gather(idx_v, j, tile, peer_v, vbuf, sQ["acc_done"], sQ["idx_v_copied"], v_loaded)

            turns = SLOTS_PER_TOKEN // GB
            eng.wait_ge(sQ["idx0_ready"], PEER_HEADS)
            gather_u(0, 0)
            gather_u(0, 1)
            gather_v(0, 0)
            with eng.Fori(2, turns) as j:
                gather_u(0, j)
                gather_v(0, j - 1)
            eng.wait_ge(sQ["idx1_ready"], PEER_HEADS)
            gather_u(1, 0)
            gather_v(0, turns - 1)
            with eng.Fori(1, turns) as j:
                gather_u(1, j)
                gather_v(1, j - 1)
            gather_v(1, turns - 1)

        @block.tensor
        def _(eng):
            def product(i, c, out, high, low, fresh=None):
                h_, l_ = wh[c % 2], wl[c % 2]
                for half in range(2):
                    eng.wait_ge(lo_ready, unit(i, c, 2, half + 1))
                    for k in range(half * KC // 2, (half + 1) * KC // 2):
                        if fresh is not None and k % 2 == 0:
                            eng.wait_ge(fresh[0], fresh[1] + k // 2 + 1)
                        eng.matmul(out, h_[:, k, :], high[:, k, :], start=(k == 0), stop=False)
                        eng.matmul(out, h_[:, k, :], low[:, k, :], start=False, stop=False)
                        last = eng.matmul(out, l_[:, k, :], high[:, k, :], start=False, stop=(k == KC - 1))
                    last.then_inc(mm_done, 1)

            def project(stage, s, i, high, low, fresh=None):
                for j in range(2):
                    product(i, BASE[stage] + 2 * s + j, B[s][:, j * T:(j + 1) * T], high, low, fresh if j == 0 else None)

            def product_tok(i, c, out, high, low, n=P, fresh=None):
                h_, l_ = wh[c % 2], wl[c % 2]
                for half in range(2):
                    eng.wait_ge(lo_ready, unit(i, c, 2, half + 1))
                    for k in range(half * KC // 2, (half + 1) * KC // 2):
                        if fresh is not None and k % 2 == 0:
                            eng.wait_ge(fresh[0], fresh[1] + k // 2 + 1)
                        for t in range(NT):
                            tt = slice(t * P, (t + 1) * P)
                            eng.matmul(out[t], high[:, k, tt], h_[:, k, 0:n], start=(k == 0 and t == 0), stop=False,
                                       skip_group_check=True)
                            eng.matmul(out[t], high[:, k, tt], l_[:, k, 0:n], start=False, stop=False, skip_group_check=True)
                            last = eng.matmul(out[t], low[:, k, tt], h_[:, k, 0:n], start=False, stop=(k == KC - 1),
                                              skip_group_check=True)
                    last.then_inc(mm_done, 1)

            def project_tok(stage, s, i, high, low):
                for j in range(2):
                    product_tok(i, BASE[stage] + 2 * s + j, [B[s][:, t * G + j * P:t * G + (j + 1) * P] for t in range(NT)],
                                high, low)

            def norm_sum(name, g):
                eng.wait_ge(sq_ready, 8 * NORM_AT[name] + g + 1)
                for c in range(2):
                    last = eng.matmul(B[4][:, 0:T], ones[:, :], sq[:, g % 2, c * T:(c + 1) * T],
                                      start=(g == 0 and c == 0), stop=(g == KC // 2 - 1 and c == 1))
                last.then_inc(ss_done, 1)

            def out_projection(stage, mixer, name):
                for g in range(KC // 2):
                    if g >= 4:
                        eng.wait_ge(x_ready, 8 * (NORM_AT[name] - 1) + g - 3)
                    for j in range(2):
                        product(0, BASE[stage] + 2 * g + j, B[g % 4][:, j * T:(j + 1) * T], hh, hl,
                                (ol_ready, MIX_AT[mixer]) if g == 0 and j == 0 else None)
                    if g >= 1:
                        norm_sum(name, g - 1)
                norm_sum(name, KC // 2 - 1)

            def pair_loop(body):
                body(0, True)
                with eng.Fori(1, PAIRS) as i:
                    body(i, False)

            def head_sum(bank, src, done):
                eng.matmul(B[bank][:, :], ones[:, :], src[:, :], start=True, stop=True).then_inc(done, 1)

            def transpose_probs(prob, done):
                for j in range(2):
                    for a in range(3):
                        last = eng.transpose(B[6 + j][:, a * P:(a + 1) * P], prob[:, j, a * P:(a + 1) * P], ident[:, :])
                    last.then_inc(done, 1)

            def weigh_values(bank, v, probT, done):
                for j in range(2):
                    c = slice(j * P, (j + 1) * P)
                    o = j * T
                    eng.matmul(B[bank][:, o:o + P], v[:, 0, c], probT[:, j, 0:P], start=True, stop=True)
                    eng.matmul(B[bank][:, o + P:o + T], v[:, 0, c], probT[:, j, P:2 * P], start=True, stop=False)
                    last = eng.matmul(B[bank][:, o + P:o + T], v[:, 1, c], probT[:, j, 2 * P:3 * P], start=False, stop=True)
                last.then_inc(done, 1)

            eng.wait_ge(consts_ready, 1)
            for g in range(KC // 2):
                norm_sum("A", g)

            s = sA

            def a_values(i):
                eng.wait_ge(s["at_ready"], i + 1)
                eng.wait_ge(s["v_ready"], i + 1)
                for j in range(2):
                    c = slice(j * P, (j + 1) * P)
                    eng.matmul(B[4][:, j * T:j * T + P], v_a[:, 0, c], AT[:, 2 * j, :], start=True, stop=True)
                    eng.matmul(B[4][:, j * T + P:(j + 1) * T], v_a[:, 0, c], AToff[:, j, :], start=True, stop=False)
                    last = eng.matmul(B[4][:, j * T + P:(j + 1) * T], v_a[:, 1, c], AT[:, 2 * j + 1, :], start=False, stop=True)
                last.then_inc(s["o_done"], 1)

            def a_norm(i):
                eng.wait_ge(s["osq_ready"], i + 1)
                head_sum(5, osq_a, s["oss_done"])

            def a_levels(i):
                if past_zero(i):
                    eng.wait_ge(s["o_read"], i)
                    eng.wait_ge(s["ors_ready"], i)
                eng.wait_ge(s["f_ready"], i + 1)
                for j in range(2):
                    for t in range(NT):
                        a = j * T + t * P
                        eng.matmul(B[4][:, a:a + P], KL[0][:, a:a + P], q_a[:, a:a + P], start=True, stop=True)
                for l in range(LEVELS):
                    h = 1 << l
                    bank, at = (B[5 + l // 2], (l % 2) * T) if l < 6 else (B[3], 0)
                    if l == 6:
                        eng.wait_ge(s["gate_read"], i + 1)
                    for n in range(2 * NT):
                        last = eng.matmul(bank[:, at + n * (P // 2):at + (n + 1) * (P // 2)], KL[l][:, n * P:(n + 1) * P],
                                          halves(QL[l][:, n * P:(n + 1) * P], h)[:, :, 1, :], start=True, stop=True)
                for j in range(2):
                    last = eng.matmul(B[3][:, T + j * P:T + (j + 1) * P], KL[7][:, j * T:j * T + P],
                                      QL[7][:, j * T + P:(j + 1) * T], start=True, stop=True)
                last.then_inc(s["lv_done"], 1)

            def a_body(i, first):
                if past_zero(i):
                    eng.wait_ge(s["fz_read"], i)
                project("A", 0, i, hh, hl, (hl_ready, SPLIT_AT["A"]) if first else None)
                if not first:
                    a_values(i - 1)
                if past_zero(i):
                    eng.wait_ge(s["qz_ready"], i)
                project("A", 1, i, hh, hl)
                if not first:
                    a_norm(i - 1)
                if past_zero(i):
                    eng.wait_ge(s["v_ready"], i)
                project_tok("A", 2, i, hh, hl)
                if past_zero(i):
                    eng.wait_ge(s["at_ready"], i)
                project("A", 3, i, hh, hl)
                a_levels(i)

            pair_loop(a_body)
            a_values(PAIRS - 1)
            a_norm(PAIRS - 1)
            out_projection("OA", "A", "F")

            s = sF
            product_tok(0, BASE["FG"], [B[5][:, t * HEADS:(t + 1) * HEADS] for t in range(NT)], kh, kl, HEADS,
                        (hl_ready, SPLIT_AT["F"]))
            eng.wait_ge(s["fz_read"], 1)
            for t in range(NT):
                last = eng.transpose(B[5][0:HEADS, t * P:(t + 1) * P], fz_tok[:, t, :], ident[:, :])
            last.then_inc(s["fzt_done"], 1)

            def f_transpose(i):
                eng.wait_ge(s["p_ready"], i + 1)
                transpose_probs(prob_f, s["pt_done"])

            def f_values(i):
                eng.wait_ge(s["pt_ready"], i + 1)
                eng.wait_ge(s["v_ready"], i + 1)
                weigh_values(5, v_f, probT_f, s["o_done"])

            def f_norm(i):
                eng.wait_ge(s["osq_ready"], i + 1)
                head_sum(6, osq_f, s["oss_done"])

            def f_body(i, first):
                if past_zero(i):
                    eng.wait_ge(s["kn_ready"], i)
                project("F", 0, i, kh, kl)
                if not first:
                    f_transpose(i - 1)
                if past_zero(i):
                    eng.wait_ge(s["qn_ready"], i)
                project("F", 1, i, hh, hl, (hl_ready, SPLIT_AT["F"] + 8) if first else None)
                eng.wait_ge(s["ksq_ready"], i + 1)
                if past_zero(i):
                    eng.wait_ge(s["qrs_ready"], i)
                head_sum(4, ksq, s["kss_done"])
                if not first:
                    f_values(i - 1)
                if past_zero(i):
                    eng.wait_ge(s["v_ready"], i)
                project_tok("F", 2, i, kh, kl)
                eng.wait_ge(s["qsq_ready"], i + 1)
                eng.wait_ge(s["krs_ready"], i + 1)
                head_sum(4, qsq, s["qss_done"])
                if not first:
                    f_norm(i - 1)
                if past_zero(i):
                    eng.wait_ge(s["gate_read"], i)
                project("F", 3, i, hh, hl)
                eng.wait_ge(s["kn_ready"], i + 1)
                eng.wait_ge(s["qn_ready"], i + 1)
                eng.wait_ge(s["sel_ready"], i + 1)
                if past_zero(i):
                    eng.wait_ge(s["ors_ready"], i)
                for j in range(2):
                    for t in range(NT):
                        n = (t + 1) * P
                        o = B[6 + j][:, t * P:t * P + n]
                        tt = slice(t * P, (t + 1) * P)
                        eng.matmul(o, qT_f[:, j, tt], kT_f[:, j, 0:n], start=True, stop=False)
                        eng.matmul(o, ones[:, :], selF[:, j, 0:n], start=False, stop=False)
                        last = eng.matmul(o, fcum[:, tt], selO[:, j, 0:n], start=False, stop=True)
                    last.then_inc(s["s_done"], 1)

            pair_loop(f_body)
            f_transpose(PAIRS - 1)
            f_values(PAIRS - 1)
            f_norm(PAIRS - 1)
            out_projection("OF", "F", "C")

            s = sX
            u = BASE["X"]
            for c in range(RC):
                product(0, u + c, B[c // 2][:, (c % 2) * T:(c % 2 + 1) * T], hh, hl, (hl_ready, SPLIT_AT["C"]) if c == 0 else None)
            product_tok(0, u + RC, [B[2][:, t * (IDX_DIM + IDX_HEADS):(t + 1) * (IDX_DIM + IDX_HEADS)] for t in range(NT)],
                        hh, hl, IDX_DIM + IDX_HEADS)
            eng.wait_ge(s["csq_ready"], 1)
            for c in range(RC):
                last = eng.matmul(B[4][:, 0:T], ones[:, :], csq[:, c, :], start=(c == 0), stop=(c == RC - 1))
            last.then_inc(s["css_done"], 1)

            def index_scores(g):
                eng.wait_ge(s["qi_ready"], g + 1)
                for q in range(4):
                    n = 4 * g + q
                    b = 6 + n % 2
                    if past_zero(n - 1):
                        eng.wait_ge(s["relu_ready"], n - 1)
                    pr = slice(IDX_DIM * (q % 2), IDX_DIM * (q % 2 + 1))
                    for t in range(NT):
                        a = (q // 2) * T + t * P
                        last = eng.matmul(B[b][:, t * P:t * P + (t + 1) * P], qi[pr, g % 2, a:a + P], kiT[pr, 0:(t + 1) * P],
                                          start=True, stop=True)
                    last.then_inc(s["rel_done"], 1)

            for g in range(4):
                bank = 3 if g % 2 == 0 else 0
                if g == 1:
                    eng.wait_ge(s["ckv_read"], 1)
                if past_zero(g - 1):
                    eng.wait_ge(s["qi_ready"], g - 1)
                for j in range(2):
                    product(0, u + RC + 1 + 2 * g + j, B[bank][:, j * T:(j + 1) * T], hh, hl)
                if g == 0:
                    eng.wait_ge(s["kn_ready"], 1)
                    for t in range(NT):
                        last = eng.transpose(B[5][:, t * P:(t + 1) * P], kdup[:, t].rearrange("p a d -> p (a d)"), ident[:, :])
                    last.then_inc(s["kt_done"], 1)
                if g == 1:
                    eng.wait_ge(s["kt_ready"], 1)
                if g >= 1:
                    index_scores(g - 1)
            index_scores(3)
            eng.wait_ge(s["relu_ready"], IDX_HEADS)

            s = sC
            eng.wait_ge(sX["ckv_ready"], 1)

            def c_transpose(i):
                eng.wait_ge(s["p_ready"], i + 1)
                transpose_probs(prob_c, s["pt_done"])

            def c_values(i):
                eng.wait_ge(s["pt_ready"], i + 1)
                eng.wait_ge(s["v_ready"], i + 1)
                weigh_values(6, v_c, probT_c, s["o_done"])

            def c_body(i, first):
                if past_zero(i):
                    eng.wait_ge(s["xr_read"], i)
                project("C", 0, i, hh, hl)
                if not first:
                    c_transpose(i - 1)
                if past_zero(i):
                    eng.wait_ge(s["q_ready"], i)
                project("C", 1, i, hh, hl)
                eng.wait_ge(s["small_in"], (i + 1) * 96)
                eng.wait_ge(s["xc_ready"], i + 1)
                if past_zero(i):
                    eng.wait_ge(s["kT_ready"], i)
                    eng.wait_ge(s["v_ready"], i)
                for n, w in enumerate((wa, wx)):
                    for j in range(2):
                        last = eng.matmul(B[4 + n][:, j * T:(j + 1) * T], w[:, j, :], xc[:, j, :], start=True, stop=True)
                last.then_inc(s["rg_done"], 1)
                if not first:
                    c_values(i - 1)
                if past_zero(i):
                    eng.wait_ge(s["mix_ready"], i)
                project("C", 2, i, hh, hl)
                eng.wait_ge(s["ri_read"], i + 1)
                for j in range(2):
                    for c in range(RC):
                        last = eng.matmul(B[4][:, j * T:(j + 1) * T], uk[:, j, c, :], ckvT[:, c, :],
                                          start=(c == 0), stop=(c == RC - 1))
                last.then_inc(s["kv_done"], 1)
                for t in range(NT):
                    for c in range(RC):
                        last = eng.matmul(B[5][:, t * G:(t + 1) * G], ckvT[:, c, t * P:(t + 1) * P],
                                          uv[:, c].rearrange("p h d -> p (h d)"), start=(c == 0), stop=(c == RC - 1))
                last.then_inc(s["kv_done"], 1)
                if past_zero(i):
                    eng.wait_ge(s["asig_ready"], i)
                project("C", 3, i, hh, hl)
                eng.wait_ge(s["kT_ready"], i + 1)
                eng.wait_ge(s["q_ready"], i + 1)
                if past_zero(i):
                    eng.wait_ge(s["o_read"], i)
                for j in range(2):
                    for t in range(NT):
                        n = (t + 1) * P
                        last = eng.matmul(B[6 + j][:, t * P:t * P + n], qT_c[:, j, t * P:(t + 1) * P], kT_c[:, j, 0:n],
                                          start=True, stop=True)
                    last.then_inc(s["s_done"], 1)

            pair_loop(c_body)
            c_transpose(PAIRS - 1)
            c_values(PAIRS - 1)
            out_projection("OC", "C", "Q")

            s = sQ
            eng.wait_ge(s["keys_in"], 32)
            for n in range(2):
                last = eng.transpose(B[5][:, n * P:(n + 1) * P], keys[:, n, :], ident[:, :])
            last.then_inc(s["kt_done"], 1)
            for n in range(2 * 4):
                t, quarter = n // 4, n % 4
                b = 6 + n % 2
                if past_zero(n - 1):
                    eng.wait_ge(s["xtok_ready"], n - 1)
                for c in range(4):
                    last = eng.transpose(B[b][:, c * P:(c + 1) * P], xT[:, 4 * quarter + c, t * P:(t + 1) * P], ident[:, :])
                last.then_inc(s["xtr_done"], 1)

            def key_scores(g):
                eng.wait_ge(s["qp_ready"], g + 1)
                if g == 0:
                    eng.wait_ge(s["kt_ready"], 1)
                if past_zero(g - 1):
                    eng.wait_ge(s["sc_ready"], g - 1)
                for t in range(NT):
                    for n in range(2):
                        last = eng.matmul(B[4 + g % 2][:, (2 * t + n) * P:(2 * t + n + 1) * P],
                                          qp[:, g % 2, n, t * P:(t + 1) * P], keysT[:, n, :], start=True, stop=True)
                last.then_inc(s["sc_done"], 1)

            for g in range(PEER_HEADS):
                if past_zero(g - 3):
                    eng.wait_ge(s["qp_ready"], g - 3)
                for j in range(2):
                    product(0, BASE["Q"] + 2 * g + j, B[g % 4][:, j * T:(j + 1) * T], hh, hl,
                            (hl_ready, SPLIT_AT["Q"]) if g == 0 and j == 0 else None)
                if g >= 1:
                    key_scores(g - 1)
            key_scores(PEER_HEADS - 1)

            def accumulate(tile, j, final):
                n = tile * (SLOTS_PER_TOKEN // GB) + j
                for b in range(GB):
                    eng.wait_ge(s["diag_ready"], n * GB + b + 1)
                    eng.wait_ge(v_loaded[b], (n + 1) * 16)
                    for c in range(4):
                        last = eng.matmul(B[4 * tile + c][:, :], diag[:, b, :], vbuf[b][:, c * 512:(c + 1) * 512],
                                          start=False, stop=(final and b == GB - 1), skip_group_check=True)
                    last.then_inc(s["acc_done"], 1)

            eng.wait_ge(s["xtok_ready"], 8)
            eng.wait_ge(s["sc_ready"], PEER_HEADS)
            for tile in range(NT):
                for c in range(4):
                    eng.matmul(B[4 * tile + c][:, :], ident[:, :], x_tok[:, tile, c * 512:(c + 1) * 512],
                               start=True, stop=False, skip_group_check=True)
                with eng.Fori(0, SLOTS_PER_TOKEN // GB - 1) as j:
                    accumulate(tile, j, False)
                accumulate(tile, SLOTS_PER_TOKEN // GB - 1, True)

        @block.scalar
        def _(eng):
            def rsqrt(out, src, scale):
                eng.activation(out, src, ACT.Ln, bias=eps[0:out.shape[0], 0:1], scale=scale)
                eng.drain()
                return eng.activation(out, out, ACT.Exp, scale=-0.5)

            def high_part(i, c):
                eng.wait_ge(w_loaded[c % RAW], i * (PER_PAIR // RAW * 16) + (c // RAW + 1) * 16)
                for half in range(2):
                    k = slice(half * KC // 2, (half + 1) * KC // 2)
                    if past_zero(unit(i, c, 2, half - 3)):
                        eng.wait_ge(mm_done, unit(i, c, 2, half - 3))
                    eng.activation(wh[c % 2][:, k, :], raw[:, c % RAW, :].rearrange("p (k n) -> p k n", k=KC)[:, k, :],
                                   ACT.Copy).then_inc(hi_ready, 1)

            def square_chunks(name, g):
                n = 8 * NORM_AT[name]
                if name != "A":
                    eng.wait_ge(x_ready, n - 8 + g + 1)
                if past_zero(g - 1):
                    eng.wait_ge(ss_done, n + g - 1)
                eng.activation(sq[:, g % 2, :], chunk(xT, 2 * g, 2), ACT.Square).then_inc(sq_ready, 1)

            def stream_norm(name, outs):
                eng.wait_ge(ss_done, 8 * (NORM_AT[name] + 1))
                rsqrt(rstd[:, :], B[4][:, 0:T], 1.0 / D).then_inc(rstd_ready, 1)
                for n, dst in enumerate(outs):
                    for g in range(KC // 2):
                        eng.wait_ge(hf_ready, SPLIT_AT[name] + 8 * n + g + 1)
                        eng.activation(chunk(dst, 2 * g, 2), chunk(oT, 2 * g, 2), ACT.Copy).then_inc(hh_ready, 1)

            def outputs_high(name, first, count):
                eng.wait_ge(mm_done, 2 * (BASE[name] + 64))
                for c in range(first, first + count):
                    eng.wait_ge(mixed, MIX_AT[name] + c + 1)
                    eng.activation(chunk(hh, 2 * c, 2), chunk(oT, 2 * c, 2), ACT.Copy).then_inc(oh_ready, 1)

            def after(stage, i, c):
                return unit(i, BASE[stage] + c, 2, 2)

            def out_stage(stage, name):
                for g in range(KC // 2):
                    high_part(0, BASE[stage] + 2 * g + 2)
                    high_part(0, BASE[stage] + 2 * g + 3)
                    square_chunks(name, g)

            def pair_loop(body):
                body(0, True)
                with eng.Fori(1, PAIRS) as i:
                    body(i, False)

            eng.wait_ge(consts_ready, 1)
            eng.wait_ge(x_in, 64)
            for g in range(KC // 2):
                square_chunks("A", g)
            eng.wait_ge(lb_e_ready, 1)
            eng.activation(sp[:, 1, :], sp[:, 0, :], ACT.Exp).then_inc(lb_e_ready, 1)
            eng.wait_ge(lam_e_ready, 1)
            eng.activation(sp[:, 5, :], sp[:, 4, :], ACT.Exp, scale=-1.0).then_inc(lam_e_ready, 1)
            eng.wait_ge(lam_w_ready, 1)
            eng.activation(sp[:, 7, :], sp[:, 6, :], ACT.Ln).then_inc(lam_l_ready, 1)
            high_part(0, 0)
            high_part(0, 1)
            stream_norm("A", [hh])

            s = sA

            def a_body(i, first):
                high_part(i, 2)
                eng.wait_ge(mm_done, after("A", i, 1))
                if past_zero(i):
                    eng.wait_ge(s["f_ready"], i)
                eng.activation(f0[:, :], B[0][:, :], ACT.Sigmoid)
                eng.activation(k0[:, :], B[0][:, :], ACT.Sigmoid, scale=-1.0).then_inc(s["fz_read"], 1)
                high_part(i, 3)
                if not first:
                    eng.wait_ge(s["o_done"], i)
                    eng.activation(osq_a[:, :], B[4][:, :], ACT.Square).then_inc(s["osq_ready"], 1)
                high_part(i, 4)
                eng.wait_ge(mm_done, after("A", i, 3))
                if past_zero(i):
                    eng.wait_ge(s["lv_done"], i)
                eng.activation(q_a[:, :], B[1][:, :], ACT.Copy).then_inc(s["qz_ready"], 1)
                high_part(i, 5)
                if not first:
                    a_rstd(i - 1)
                high_part(i, 6)
                eng.wait_ge(mm_done, after("A", i, 5))
                if past_zero(i):
                    eng.wait_ge(s["o_done"], i)
                eng.activation(v_a[:, :, :].rearrange("p t g -> p (t g)"), B[2][:, :], ACT.Copy).then_inc(s["v_ready"], 1)
                high_part(i, 7)
                high_part(i, 8)
                eng.wait_ge(mm_done, after("A", i, 7))
                if past_zero(i):
                    eng.wait_ge(s["gate_read"], i)
                eng.activation(sig_a[:, :], B[3][:, :], ACT.Sigmoid).then_inc(s["sig_ready"], 1)
                high_part(i, 9)

            def a_rstd(i):
                eng.wait_ge(s["oss_done"], i + 1)
                if past_zero(i):
                    eng.wait_ge(s["o_read"], i)
                rsqrt(ors_a[:, :], B[5][:, :], 1.0 / P).then_inc(s["ors_ready"], 1)

            pair_loop(a_body)
            outputs_high("A", 0, PAIRS - 1)
            eng.wait_ge(s["o_done"], PAIRS)
            eng.activation(osq_a[:, :], B[4][:, :], ACT.Square).then_inc(s["osq_ready"], 1)
            a_rstd(PAIRS - 1)
            outputs_high("A", PAIRS - 1, 1)
            out_stage("OA", "F")
            stream_norm("F", [kh, hh])

            s = sF
            high_part(0, BASE["FG"] + 2)
            eng.wait_ge(mm_done, 2 * (BASE["FG"] + 1))
            eng.activation(fz_tok[:, :, :].rearrange("p t h -> p (t h)"), B[5][:, 0:NT * HEADS], ACT.Copy).then_inc(s["fz_read"], 1)
            eng.wait_ge(s["z_ready"], 1)
            eng.activation(fz[2], fz[1], ACT.Exp, scale=-1.0)
            eng.drain()
            eng.activation(fz[3], fz[2], ACT.Ln, bias=ones[0:HEADS, 0:1]).then_inc(s["l_ready"], 1)

            def softmax_exp(s, i, prob, nmax, rsum):
                eng.wait_ge(s["nmax_ready"], i + 1)
                for j in range(2):
                    for t in range(NT):
                        p = prob[:, j, t * P:t * P + (t + 1) * P]
                        last = eng.activation(p, p, ACT.Exp, bias=nmax[:, 2 * j + t:2 * j + t + 1],
                                              accum_out=rsum[:, 2 * j + t:2 * j + t + 1])
                last.then_inc(s["e_done"], 1)

            def copy_probs(s, i, probT):
                if past_zero(i):
                    eng.wait_ge(s["o_done"], i)
                for j in range(2):
                    eng.wait_ge(s["pt_done"], i * 2 + j + 1)
                    last = eng.activation(probT[:, j, :], B[6 + j][:, 0:SC], ACT.Copy)
                last.then_inc(s["pt_ready"], 1)

            def f_square_out(i):
                eng.wait_ge(s["o_done"], i + 1)
                eng.activation(osq_f[:, :], B[5][:, :], ACT.Square).then_inc(s["osq_ready"], 1)

            def f_rstd_out(i):
                eng.wait_ge(s["oss_done"], i + 1)
                if past_zero(i):
                    eng.wait_ge(s["o_read"], i)
                rsqrt(ors_f[:, :], B[6][:, :], 1.0 / P).then_inc(s["ors_ready"], 1)

            def f_body(i, first):
                u = BASE["F"]
                high_part(i, u + 2)
                eng.wait_ge(mm_done, after("F", i, 1))
                eng.activation(ksq[:, :], B[0][:, :], ACT.Square).then_inc(s["ksq_ready"], 1)
                high_part(i, u + 3)
                if not first:
                    copy_probs(s, i - 1, probT_f)
                high_part(i, u + 4)
                eng.wait_ge(mm_done, after("F", i, 3))
                eng.activation(qsq[:, :], B[1][:, :], ACT.Square).then_inc(s["qsq_ready"], 1)
                eng.wait_ge(s["kss_done"], i + 1)
                if past_zero(i):
                    eng.wait_ge(s["kn_ready"], i)
                rsqrt(krs[:, :], B[4][:, :], 1.0 / P).then_inc(s["krs_ready"], 1)
                high_part(i, u + 5)
                if not first:
                    f_square_out(i - 1)
                high_part(i, u + 6)
                eng.wait_ge(mm_done, after("F", i, 5))
                if past_zero(i):
                    eng.wait_ge(s["o_done"], i)
                eng.activation(v_f[:, :, :].rearrange("p t g -> p (t g)"), B[2][:, :], ACT.Copy).then_inc(s["v_ready"], 1)
                high_part(i, u + 7)
                eng.wait_ge(s["qss_done"], i + 1)
                if past_zero(i):
                    eng.wait_ge(s["qn_ready"], i)
                rsqrt(qrs[:, :], B[4][:, :], 1.0 / P).then_inc(s["qrs_ready"], 1)
                if not first:
                    f_rstd_out(i - 1)
                high_part(i, u + 8)
                eng.wait_ge(mm_done, after("F", i, 7))
                if past_zero(i):
                    eng.wait_ge(s["gate_read"], i)
                eng.activation(sig_f[:, :], B[3][:, :], ACT.Sigmoid).then_inc(s["sig_ready"], 1)
                high_part(i, u + 9)
                softmax_exp(s, i, prob_f, nmax_f, rsum_f)

            pair_loop(f_body)
            copy_probs(s, PAIRS - 1, probT_f)
            outputs_high("F", 0, PAIRS - 1)
            f_square_out(PAIRS - 1)
            f_rstd_out(PAIRS - 1)
            outputs_high("F", PAIRS - 1, 1)
            out_stage("OF", "C")
            stream_norm("C", [hh])

            s = sX
            u = BASE["X"]
            for n in range(2):
                high_part(0, u + 2 * n + 2)
                eng.wait_ge(mm_done, 2 * (u + 2 * n + 2))
                eng.activation(csq[:, 2 * n:2 * n + 2, :].rearrange("p c t -> p (c t)"), B[n][:, :], ACT.Square)
                high_part(0, u + 2 * n + 3)
            eng.drain().then_inc(s["csq_ready"], 1)
            high_part(0, u + 6)
            eng.wait_ge(mm_done, 2 * (u + RC + 1))
            eng.activation(kw[:, :, :].rearrange("p t n -> p (t n)"), B[2][:, 0:NT * (IDX_DIM + IDX_HEADS)],
                           ACT.Copy).then_inc(s["kw_ready"], 1)
            eng.wait_ge(s["css_done"], 1)
            rsqrt(crs[:, :], B[4][:, 0:T], 1.0 / KV_RANK).then_inc(s["crs_ready"], 1)
            eng.wait_ge(s["kc_ready"], 1)
            for t in range(NT):
                eng.activation(kdup[:, t, 0, :], kc[:, t, :], ACT.Square, accum_out=kst[:, 1, t:t + 1])
            eng.drain()
            rsqrt(kst[:, 2, :], kst[:, 1, :], 1.0 / IDX_DIM).then_inc(s["krs_ready"], 1)

            def index_relu(g):
                for q in range(4):
                    n = 4 * g + q
                    eng.wait_ge(s["rel_done"], n + 1)
                    if past_zero(n - 3):
                        eng.wait_ge(s["relu_used"], n - 3)
                    eng.activation(relu[:, n % 4, :], B[6 + n % 2][:, 0:SC], ACT.Relu).then_inc(s["relu_ready"], 1)

            for g in range(4):
                high_part(0, u + RC + 1 + 2 * g + 2)
                high_part(0, u + RC + 1 + 2 * g + 3)
                eng.wait_ge(mm_done, 2 * (u + RC + 1 + 2 * g + 2))
                eng.activation(qi[:, g % 2, :], B[3 if g % 2 == 0 else 0][:, :], ACT.Copy,
                               scale=float(IDX_DIM) ** -0.5).then_inc(s["qi_ready"], 1)
                if g >= 1:
                    index_relu(g - 1)
            index_relu(3)

            s = sC

            def c_body(i, first):
                u = BASE["C"]
                high_part(i, u + 2)
                if not first:
                    copy_probs(s, i - 1, probT_c)
                high_part(i, u + 3)
                high_part(i, u + 4)
                eng.wait_ge(mm_done, after("C", i, 3))
                if past_zero(i):
                    eng.wait_ge(s["s_done"], i * 2)
                eng.activation(qT_c[:, :, :].rearrange("p h t -> p (h t)"), B[1][:, :], ACT.Copy,
                               scale=HD_SCALE).then_inc(s["q_ready"], 1)
                eng.wait_ge(s["rg_done"], i + 1)
                if past_zero(i):
                    eng.wait_ge(s["mix_ready"], i)
                for n, b in enumerate(("ba", "bx")):
                    for j in range(2):
                        last = eng.activation(rg[:, n, j, :], B[4 + n][:, j * T:(j + 1) * T], ACT.Sigmoid,
                                              bias=col(b, i * 2 + j))
                last.then_inc(s["ri_read"], 1)
                high_part(i, u + 5)
                eng.wait_ge(s["la_ready"], i + 1)
                eng.activation(ae[:, 0, :], la[:, :], ACT.Exp)
                eng.activation(ae[:, 1, :], la[:, :], ACT.Exp, scale=2.0)
                eng.activation(ae[:, 2, :], la[:, :], ACT.Tanh, scale=-1.0).then_inc(s["ex_ready"], 1)
                high_part(i, u + 6)
                eng.wait_ge(s["prod_ready"], i + 1)
                eng.activation(ub[:, 0, :], ub[:, 0, :], ACT.Sqrt).then_inc(s["root_ready"], 1)
                eng.wait_ge(mm_done, after("C", i, 5))
                eng.activation(rsig[:, :], B[2][:, :], ACT.Sigmoid).then_inc(s["rsig_ready"], 1)
                high_part(i, u + 7)
                eng.wait_ge(s["kv_done"], i * 2 + 1)
                eng.activation(kT_c[:, :, :].rearrange("p h t -> p (h t)"), B[4][:, :], ACT.Copy).then_inc(s["kT_ready"], 1)
                eng.wait_ge(s["kv_done"], i * 2 + 2)
                if past_zero(i):
                    eng.wait_ge(s["o_done"], i)
                eng.activation(v_c[:, :, :].rearrange("p t g -> p (t g)"), B[5][:, :], ACT.Copy).then_inc(s["v_ready"], 1)
                high_part(i, u + 8)
                eng.wait_ge(mm_done, after("C", i, 7))
                if past_zero(i):
                    eng.wait_ge(s["o_read"], i)
                eng.activation(asig[:, :], B[3][:, :], ACT.Sigmoid).then_inc(s["asig_ready"], 1)
                high_part(i, u + 9)
                softmax_exp(s, i, prob_c, nmax_c, rsum_c)

            pair_loop(c_body)
            copy_probs(s, PAIRS - 1, probT_c)
            outputs_high("C", 0, PAIRS)
            out_stage("OC", "Q")
            stream_norm("Q", [hh])

            s = sQ
            eng.wait_ge(s["kt_done"], 1)
            eng.activation(keysT[:, :, :].rearrange("p n k -> p (n k)"), B[5][:, 0:2 * P], ACT.Copy).then_inc(s["kt_ready"], 1)
            for n in range(8):
                t, quarter = n // 4, n % 4
                eng.wait_ge(s["xtr_done"], n + 1)
                eng.activation(x_tok[:, t, quarter * 512:(quarter + 1) * 512], B[6 + n % 2][:, :], ACT.Copy).then_inc(s["xtok_ready"], 1)
            eng.drain()

            def evacuate(g):
                for c in (2 * g + 2, 2 * g + 3):
                    if c < UNITS["Q"]:
                        high_part(0, BASE["Q"] + c)
                eng.wait_ge(mm_done, 2 * (BASE["Q"] + 2 * g + 2))
                if past_zero(g - 1):
                    eng.wait_ge(s["sc_done"], g - 1)
                eng.activation(qp[:, g % 2, :, :].rearrange("p n t -> p (n t)"), B[g % 4][:, :], ACT.Copy).then_inc(s["qp_ready"], 1)

            def keep_scores(g):
                eng.wait_ge(s["sc_done"], g + 1)
                eng.activation(S12[:, :, g, :], B[4 + g % 2][:, :].rearrange("p (t n) -> p t n", t=NT), ACT.Copy).then_inc(s["sc_ready"], 1)

            for g in range(PEER_HEADS):
                evacuate(g)
                if g >= 1:
                    keep_scores(g - 1)
                if g < NT:
                    eng.activation(sq_scr, x_tok[:, g, :], ACT.Square, accum_out=tstat[:, 0, g:g + 1])
                    eng.drain()
                    rsqrt(tstat[:, 1, g:g + 1], tstat[:, 0, g:g + 1], 1.0 / D).then_inc(s["trs_ready"], 1)
            keep_scores(PEER_HEADS - 1)

            def gate_exp(tile):
                eng.wait_ge(s["sub_ready"], tile + 1)
                t_ = tops[:, tile].rearrange("p h k -> p (h k)")
                eng.activation(t_, t_, ACT.Exp).then_inc(s["gexp_ready"], 1)

            def gelu(tile, j):
                n = tile * (SLOTS_PER_TOKEN // GB) + j
                eng.wait_ge(s["z_ready"], n + 1)
                eng.activation(g4[:, :], z4[:, :], ACT.Gelu).then_inc(s["g_ready"], 1)

            gate_exp(0)
            with eng.Fori(0, PEER_HEADS) as j:
                gelu(0, j)
            gate_exp(1)
            with eng.Fori(PEER_HEADS, SLOTS_PER_TOKEN // GB) as j:
                gelu(0, j)

            def final_norm(tile):
                eng.wait_ge(s["acc_done"], (tile + 1) * SLOTS_PER_TOKEN)
                for c in range(4):
                    eng.activation(x_tok[:, tile, c * 512:(c + 1) * 512], B[4 * tile + c][:, :], ACT.Square,
                                   accum_out=fss[:, 4 * tile + c:4 * tile + c + 1])
                eng.drain().then_inc(s["fss_ready"], 1)
                eng.wait_ge(s["tss_ready"], tile + 1)
                rsqrt(tstat[:, 3, tile:tile + 1], tstat[:, 2, tile:tile + 1], 1.0 / D).then_inc(s["frs_ready"], 1)

            gelu(1, 0)
            gelu(1, 1)
            final_norm(0)
            with eng.Fori(2, SLOTS_PER_TOKEN // GB) as j:
                gelu(1, j)
            final_norm(1)

        @block.vector
        def _(eng):
            def stream_norm(name, outs):
                eng.wait_ge(rstd_ready, NORM_AT[name] + 1)
                for n, (dst, high, weight) in enumerate(outs):
                    for g in range(KC // 2 + 1):
                        if g < KC // 2:
                            for c in (2 * g, 2 * g + 1):
                                last = eng.scalar_tensor_tensor(out=oT[:, c, :], in0=xT[:, c, :], scalar=col(weight, c),
                                                                in1=rstd[:, :], op0=ALU.mult, op1=ALU.mult)
                            last.then_inc(hf_ready, 1)
                        if g >= 1:
                            eng.wait_ge(hh_ready, SPLIT_AT[name] + 8 * n + g)
                            eng.tensor_tensor(chunk(dst, 2 * g - 2, 2), chunk(oT, 2 * g - 2, 2),
                                              chunk(high, 2 * g - 2, 2).bitcast(F32), ALU.subtract).then_inc(hl_ready, 1)
                    eng.drain()

            def outputs_low(name, first, count):
                for c in range(first, first + count):
                    eng.wait_ge(oh_ready, MIX_AT[name] + c + 1)
                    eng.tensor_tensor(chunk(hl, 2 * c, 2), chunk(oT, 2 * c, 2), chunk(hh, 2 * c, 2).bitcast(F32),
                                      ALU.subtract).then_inc(ol_ready, 1)

            def add_to_stream(stage, name):
                for g in range(KC // 2):
                    eng.wait_ge(mm_done, 2 * (BASE[stage] + 2 * g + 2))
                    eng.tensor_tensor(chunk(xT, 2 * g, 2), B[g % 4][:, :], chunk(xT, 2 * g, 2), ALU.add).then_inc(x_ready, 1)

            def pair_loop(body):
                body(0, True)
                with eng.Fori(1, PAIRS) as i:
                    body(i, False)

            eng.wait_ge(params_in, 16)
            lbl = prm[:, PRM["a_lb"]:PRM["a_lb"] + KC]
            eng.tensor_tensor(sp[:, 0, :], lbl, lbl, ALU.subtract).then_inc(lb_e_ready, 1)
            lam = prm[:, PRM["lam"]:PRM["lam"] + KC]
            eng.tensor_scalar(sp[:, 3, :], lam, -1.0, 0.0, ALU.mult, ALU.max)
            eng.drain()
            eng.scalar_tensor_tensor(out=sp[:, 4, :], in0=sp[:, 3, :], scalar=2.0, in1=lam, op0=ALU.mult,
                                     op1=ALU.add).then_inc(lam_e_ready, 1)
            eng.tensor_scalar(qw[:, :], prm[:, PRM["q_norm"]:PRM["q_norm"] + 1], HD_SCALE, None, ALU.mult)
            for n in range(1, LEVELS + 1):
                eng.memset(KL[n][:, :], 0.0)
            eng.wait_ge(x_in, 64)
            eng.wait_ge(lb_e_ready, 2)
            eng.reciprocal(sp[:, 2, :], sp[:, 1, :])
            eng.drain()
            eng.tensor_tensor(sp[:, 0, :], sp[:, 1, :], sp[:, 2, :], ALU.mult)
            eng.drain()
            eng.tensor_tensor(lb[:, :], sp[:, 0, :], sp[:, 0, :], ALU.subtract)
            eng.drain()
            eng.tensor_scalar(omlb[:, :], lb[:, :], -1.0, 1.0, ALU.mult, ALU.add)
            eng.wait_ge(lam_e_ready, 2)
            eng.tensor_scalar(sp[:, 6, :], sp[:, 5, :], 1.0, None, ALU.add)
            eng.drain().then_inc(lam_w_ready, 1)
            eng.tensor_scalar(sp[:, 0, :], sp[:, 6, :], 1.0, None, ALU.is_equal)
            eng.drain()
            eng.scalar_tensor_tensor(out=sp[:, 1, :], in0=sp[:, 6, :], scalar=-1.0, in1=sp[:, 0, :], op0=ALU.add, op1=ALU.add)
            eng.drain()
            eng.reciprocal(sp[:, 2, :], sp[:, 1, :])
            eng.wait_ge(lam_l_ready, 1)
            eng.drain()
            eng.tensor_tensor(sp[:, 1, :], sp[:, 7, :], sp[:, 2, :], ALU.mult)
            eng.drain()
            eng.tensor_tensor(sp[:, 1, :], sp[:, 1, :], sp[:, 0, :], ALU.add)
            eng.drain()
            eng.tensor_tensor(sp[:, 1, :], sp[:, 1, :], sp[:, 5, :], ALU.mult)
            eng.drain()
            eng.tensor_tensor(sp[:, 1, :], sp[:, 1, :], sp[:, 3, :], ALU.add)
            eng.drain()
            eng.tensor_scalar(rg_c[:, :], sp[:, 1, :], -RG_C, None, ALU.mult)
            stream_norm("A", [(hl, hh, "a_norm")])

            s = sA
            eng.wait_ge(consts_ready, 1)

            def decays(i):
                eng.wait_ge(s["fz_read"], i + 1)
                if past_zero(i):
                    eng.wait_ge(s["lv_done"], i)
                for j in range(2):
                    a = slice(j * T, (j + 1) * T)
                    eng.tensor_scalar(TL[0][:, a], f0[:, a], omlb[:, ds(i * 2 + j, 1)], lb[:, ds(i * 2 + j, 1)], ALU.mult, ALU.add)
                    eng.tensor_scalar(KL[0][:, a], k0[:, a], omlb[:, ds(i * 2 + j, 1)], None, ALU.mult)
                eng.drain()
                eng.wait_ge(s["qz_ready"], i + 1)
                eng.tensor_tensor(QL[0][:, :], q_a[:, :], TL[0][:, :], ALU.mult)
                eng.drain()
                for l in range(LEVELS):
                    h = 1 << l
                    seg = TL[l][:, :].rearrange("p (b two) -> p b two", two=2)
                    q0, q1 = halves(QL[l][:, :], h), halves(QL[l + 1][:, :], h)
                    k0_, k1_ = halves(KL[l][:, :], h), halves(KL[l + 1][:, :], h)
                    eng.tensor_tensor(q1[:, :, 1, :], q0[:, :, 1, :], over(seg[:, :, 0], h), ALU.mult)
                    eng.tensor_tensor(k1_[:, :, 0, :], k0_[:, :, 0, :], over(seg[:, :, 1], h), ALU.mult)
                    eng.tensor_copy(q1[:, :, 0, :], q0[:, :, 0, :])
                    last = eng.tensor_copy(k1_[:, :, 1, :], k0_[:, :, 1, :])
                    if l < LEVELS - 1:
                        eng.tensor_tensor(TL[l + 1][:, :], seg[:, :, 0], seg[:, :, 1], ALU.mult)
                        eng.drain()
                    else:
                        last.then_inc(s["f_ready"], 1)

            def gated_out(s, i, bank, ors, on, gate, weight, name):
                eng.wait_ge(s["ors_ready"], i + 1)
                eng.tensor_tensor(on[:, :], B[bank][:, :], ors[:, :], ALU.mult).then_inc(s["o_read"], 1)
                eng.drain()
                for j in range(2):
                    a = slice(j * T, (j + 1) * T)
                    last = eng.scalar_tensor_tensor(out=chunk(oT, i * 2 + j), in0=on[:, a], scalar=col(weight, i * 2 + j),
                                                    in1=gate[:, a], op0=ALU.mult, op1=ALU.mult)
                last.then_inc(mixed, 1)
                eng.drain()

            def a_masks(i):
                if past_zero(i):
                    eng.wait_ge(s["o_done"], i)
                eng.wait_ge(s["lv_done"], i + 1)
                eng.tensor_tensor(AT[:, :, :], B[4][:, :].rearrange("p (n t) -> p n t", n=2 * NT),
                                  ident[:, :].unsqueeze(1).broadcast_to([P, 2 * NT, P]), ALU.mult)
                eng.drain()
                for l in range(LEVELS):
                    h, nb = 1 << l, P >> (l + 1)
                    bank, at = (B[5 + l // 2], (l % 2) * T) if l < 6 else (B[3], 0)
                    dst = AT[:, :, :].rearrange("p n (b two r) -> p n b two r", two=2, r=h)[:, :, :, 1, :]
                    mask = lmask[:, l, :].bitcast(U32).rearrange("p (b r) -> p b r", r=h)
                    for n in range(2 * NT):
                        eng.copy_predicated(dst[:, n], mask, bank[:, at + n * (P // 2):at + (n + 1) * (P // 2)]
                                            .rearrange("p (b r) -> p b r", r=h))
                    eng.drain()
                eng.tensor_copy(AToff[:, :, :], B[3][:, T:2 * T].rearrange("p (j t) -> p j t", j=2))
                eng.drain().then_inc(s["at_ready"], 1)

            def a_body(i, first):
                decays(i)
                if not first:
                    gated_out(s, i - 1, 4, ors_a, on_a, gate_a, "a_onorm", "A")
                eng.wait_ge(s["sig_ready"], i + 1)
                eng.tensor_tensor(gate_a[:, :], B[3][:, :], sig_a[:, :], ALU.mult).then_inc(s["gate_read"], 1)
                a_masks(i)

            pair_loop(a_body)
            outputs_low("A", 0, PAIRS - 1)
            gated_out(s, PAIRS - 1, 4, ors_a, on_a, gate_a, "a_onorm", "A")
            outputs_low("A", PAIRS - 1, 1)
            add_to_stream("OA", "F")
            stream_norm("F", [(kl, kh, "kv_norm"), (hl, hh, "b_norm")])

            s = sF
            eng.memset(fcum[:, :], 0.0)
            eng.memset(fneg[:, :], 0.0)
            eng.wait_ge(bias_in, 16)
            eng.wait_ge(s["fzt_done"], 1)
            eng.tensor_scalar(fz[0], B[5][0:HEADS, 0:T], fbias[:, 0:1], None, ALU.add)
            eng.drain()
            eng.tensor_scalar(fz[4], fz[0], 0.0, None, ALU.min)
            eng.drain()
            eng.scalar_tensor_tensor(out=fz[1], in0=fz[4], scalar=-2.0, in1=fz[0], op0=ALU.mult,
                                     op1=ALU.add).then_inc(s["z_ready"], 1)
            eng.wait_ge(s["l_ready"], 1)
            eng.tensor_tensor(fz[0], fz[4], fz[3], ALU.subtract)
            eng.drain()
            eng.tensor_tensor_scan(out=fcum[0:HEADS, :], data0=ones[0:HEADS, 0:1].broadcast_to([HEADS, T]), data1=fz[0],
                                   initial=0.0, op0=ALU.mult, op1=ALU.add)
            eng.drain()
            eng.tensor_scalar(fneg[0:HEADS, :], fcum[0:HEADS, :], -1.0, None, ALU.mult)
            eng.drain()

            def softmax_scores(s, i, prob, nmax, rsum, rinv, mask):
                if past_zero(i * 2):
                    eng.wait_ge(s["pt_done"], i * 2)
                for j in range(2):
                    eng.wait_ge(s["s_done"], i * 2 + j + 1)
                    eng.tensor_tensor(prob[:, j, :], B[6 + j][:, 0:SC], mask[:, :], ALU.add)
                eng.drain()
                for j in range(2):
                    for t in range(NT):
                        last = eng.tensor_reduce(nmax[:, 2 * j + t:2 * j + t + 1], prob[:, j, t * P:t * P + (t + 1) * P],
                                                 AX.X, ALU.max, negate=True)
                last.then_inc(s["nmax_ready"], 1)
                eng.wait_ge(s["e_done"], i + 1)
                eng.reciprocal(rinv[:, :], rsum[:, :])
                eng.drain()
                for j in range(2):
                    for t in range(NT):
                        p = prob[:, j, t * P:t * P + (t + 1) * P]
                        last = eng.tensor_scalar(p, p, rinv[:, 2 * j + t:2 * j + t + 1], None, ALU.mult)
                last.then_inc(s["p_ready"], 1)

            def f_body(i, first):
                if past_zero(i * 2):
                    eng.wait_ge(s["s_done"], i * 2)
                for j in range(2):
                    eng.tensor_scalar(selF[:, j, :], fneg[:, :], ident[:, ds(i * 2 + j, 1)], None, ALU.mult)
                    last = eng.tensor_copy(selO[:, j, :], ident[:, ds(i * 2 + j, 1)].broadcast_to([P, T]))
                last.then_inc(s["sel_ready"], 1)
                eng.wait_ge(s["krs_ready"], i + 1)
                eng.scalar_tensor_tensor(out=kT_f[:, :, :].rearrange("p h t -> p (h t)"), in0=B[0][:, :],
                                         scalar=col("k_norm", 0), in1=krs[:, :], op0=ALU.mult, op1=ALU.mult).then_inc(s["kn_ready"], 1)
                eng.wait_ge(s["qrs_ready"], i + 1)
                eng.scalar_tensor_tensor(out=qT_f[:, :, :].rearrange("p h t -> p (h t)"), in0=B[1][:, :], scalar=qw[:, 0:1],
                                         in1=qrs[:, :], op0=ALU.mult, op1=ALU.mult).then_inc(s["qn_ready"], 1)
                if not first:
                    gated_out(s, i - 1, 5, ors_f, on_f, gate_f, "b_onorm", "F")
                eng.wait_ge(s["sig_ready"], i + 1)
                eng.tensor_tensor(gate_f[:, :], B[3][:, :], sig_f[:, :], ALU.mult).then_inc(s["gate_read"], 1)
                softmax_scores(s, i, prob_f, nmax_f, rsum_f, rinv_f, tri)

            pair_loop(f_body)
            outputs_low("F", 0, PAIRS - 1)
            gated_out(s, PAIRS - 1, 5, ors_f, on_f, gate_f, "b_onorm", "F")
            outputs_low("F", PAIRS - 1, 1)
            add_to_stream("OF", "C")
            stream_norm("C", [(hl, hh, "mix")])

            s = sX
            eng.wait_ge(s["kw_ready"], 1)
            for t in range(NT):
                eng.tensor_reduce(kst[:, 0, t:t + 1], kw[:, t, 0:IDX_DIM], AX.X, ALU.add)
            eng.drain()
            eng.tensor_scalar(kst[:, 3, :], kst[:, 0, :], -1.0 / IDX_DIM, None, ALU.mult)
            eng.drain()
            for t in range(NT):
                eng.tensor_scalar(kc[:, t, :], kw[:, t, 0:IDX_DIM], kst[:, 3, t:t + 1], None, ALU.add)
                eng.tensor_scalar(kw[:, t, IDX_DIM:], kw[:, t, IDX_DIM:], float(IDX_HEADS) ** -0.5, None, ALU.mult)
            eng.drain().then_inc(s["kc_ready"], 1)
            eng.wait_ge(s["crs_ready"], 1)
            for c in range(RC):
                last = eng.scalar_tensor_tensor(out=ckvT[:, c, :], in0=B[c // 2][:, (c % 2) * T:(c % 2 + 1) * T],
                                                scalar=col("ckv", c), in1=crs[:, :], op0=ALU.mult, op1=ALU.mult)
                if c == 1:
                    last.then_inc(s["ckv_read"], 1)
            last.then_inc(s["ckv_ready"], 1)
            eng.wait_ge(s["krs_ready"], 1)
            for t in range(NT):
                for a in range(2):
                    last = eng.tensor_scalar(kdup[:, t, a, :], kc[:, t, :], kst[:, 2, t:t + 1], None, ALU.mult)
            last.then_inc(s["kn_ready"], 1)
            eng.memset(iscore[:, :], 0.0)
            eng.wait_ge(s["kt_done"], 1)
            eng.tensor_scalar(kiT[:, :], B[5][:, 0:T], col("idx_g", 0), col("idx_b", 0), ALU.mult, ALU.add).then_inc(s["kt_ready"], 1)
            for n in range(IDX_HEADS):
                eng.wait_ge(s["relu_ready"], n + 1)
                eng.drain()
                for t in range(NT):
                    a = slice(t * P, t * P + (t + 1) * P)
                    last = eng.scalar_tensor_tensor(out=iscore[:, a], in0=relu[:, n % 4, a], scalar=kw[:, t, IDX_DIM + n:IDX_DIM + n + 1],
                                                    in1=iscore[:, a], op0=ALU.mult, op1=ALU.add)
                last.then_inc(s["relu_used"], 1)
            eng.drain()
            eng.tensor_tensor(iscore[:, :], iscore[:, :], tri[:, :], ALU.add)
            eng.drain()
            with eng.Fori(0, TOPK // 8) as _:
                for t in range(NT):
                    eng.max(top8[:, t, :], iscore[:, t * P:t * P + (t + 1) * P])
                eng.drain()
                for t in range(NT):
                    a = slice(t * P, t * P + (t + 1) * P)
                    eng.match_replace(iscore[:, a], top8[:, t, :], iscore[:, a], TAKEN)
                eng.drain()
            eng.tensor_scalar(selmask[:, :], iscore[:, :], -3.2e38, NEG, ALU.is_gt, ALU.mult)
            eng.drain()
            eng.tensor_tensor(selmask[:, :], selmask[:, :], tri[:, :], ALU.add)
            eng.drain()

            s = sC

            def c_tail(i):
                eng.wait_ge(s["o_done"], i + 1)
                eng.wait_ge(s["asig_ready"], i + 1)
                eng.tensor_tensor(on_c[:, :], B[6][:, :], asig[:, :], ALU.mult).then_inc(s["o_read"], 1)
                eng.drain()
                eng.tensor_tensor(chunk(oT, i * 2, 2), on_c[:, :], mixr[:, :], ALU.add).then_inc(mixed, 1)

            def c_body(i, first):
                eng.wait_ge(mm_done, unit(i, BASE["C"] + 1, 2, 2))
                if past_zero(i):
                    eng.wait_ge(s["rg_done"], i)
                for j in range(2):
                    eng.tensor_scalar(xc[:, j, :], B[0][:, j * T:(j + 1) * T], col("cw3", i * 2 + j), col("cb", i * 2 + j),
                                      ALU.mult, ALU.add)
                for d in (1, 2, 3):
                    eng.drain()
                    for j in range(2):
                        last = eng.scalar_tensor_tensor(out=xc[:, j, d:T], in0=B[0][:, j * T:(j + 1) * T - d],
                                                        scalar=col(f"cw{3 - d}", i * 2 + j), in1=xc[:, j, d:T],
                                                        op0=ALU.mult, op1=ALU.add)
                last.then_inc(s["xr_read"], 1)
                eng.drain().then_inc(s["xc_ready"], 1)
                eng.wait_ge(s["ri_read"], i + 1)
                for j in range(2):
                    last = eng.tensor_scalar(la[:, j * T:(j + 1) * T], rg[:, 0, j, :], rg_c[:, ds(i * 2 + j, 1)], None, ALU.mult)
                last.then_inc(s["la_ready"], 1)
                eng.wait_ge(s["ex_ready"], i + 1)
                eng.scalar_tensor_tensor(out=ub[:, 0, :], in0=ae[:, 1, :], scalar=1.0, in1=ae[:, 2, :], op0=ALU.add,
                                         op1=ALU.mult).then_inc(s["prod_ready"], 1)
                eng.tensor_tensor(ub[:, 1, :], rg[:, 1].rearrange("p j t -> p (j t)"), xc[:, :, :].rearrange("p j t -> p (j t)"), ALU.mult)
                eng.drain()
                eng.wait_ge(s["root_ready"], i + 1)
                eng.tensor_tensor(ub[:, 1, :], ub[:, 1, :], ub[:, 0, :], ALU.mult)
                eng.drain()
                for j in range(2):
                    a = slice(j * T, (j + 1) * T)
                    eng.tensor_tensor_scan(out=hs[:, a], data0=ae[:, 0, a], data1=ub[:, 1, a], initial=0.0, op0=ALU.mult, op1=ALU.add)
                if not first:
                    c_tail(i - 1)
                eng.drain()
                eng.wait_ge(s["rsig_ready"], i + 1)
                eng.tensor_tensor(mixr[:, :], hs[:, :], rsig[:, :], ALU.mult).then_inc(s["mix_ready"], 1)
                softmax_scores(s, i, prob_c, nmax_c, rsum_c, rinv_c, selmask)

            pair_loop(c_body)
            outputs_low("C", 0, PAIRS - 1)
            c_tail(PAIRS - 1)
            outputs_low("C", PAIRS - 1, 1)
            add_to_stream("OC", "Q")
            stream_norm("Q", [(hl, hh, "ffn")])

            s = sQ
            eng.wait_ge(s["g_in"], 32)
            for t in range(NT):
                eng.wait_ge(s["trs_ready"], t + 1)
                last = eng.scalar_tensor_tensor(out=h_tok[:, t, :], in0=x_tok[:, t, :], scalar=tstat[:, 1, t:t + 1], in1=gffn[:, :],
                                                op0=ALU.mult, op1=ALU.mult)
            eng.drain()
            eng.wait_ge(consts_ready, 2)

            def top16(vals, inds, src, scratch):
                for n in range(len(src)):
                    eng.max(vals[n][:, 0:8], src[n])
                eng.drain()
                for n in range(len(src)):
                    eng.max_index(inds[n][:, 0:8], vals[n][:, 0:8], src[n])
                    eng.match_replace(scratch[n], vals[n][:, 0:8], src[n], TAKEN)
                eng.drain()
                for n in range(len(src)):
                    eng.max(vals[n][:, 8:16], scratch[n])
                eng.drain()
                for n in range(len(src)):
                    eng.max_index(inds[n][:, 8:16], vals[n][:, 8:16], scratch[n])
                eng.drain()

            def pick(n, table, where):
                k = [P, PEER_TOPK, PEER_TOPK]
                eng.tensor_tensor(onehot[:, n], where.unsqueeze(2).broadcast_to(k), iota16[:, :].unsqueeze(1).broadcast_to(k), ALU.is_equal)
                eng.drain()
                eng.tensor_tensor(onehot[:, n], onehot[:, n], table.unsqueeze(1).broadcast_to(k), ALU.mult)
                eng.drain()
                eng.tensor_reduce(epart[:, n, :], onehot[:, n], AX.X, ALU.add)

            def route(tile, h):
                eng.wait_ge(s["sc_ready"], h + 1)
                for n in range(2):
                    eng.tensor_copy(work[n][:, :], S12[:, tile, ds(h, 1), n * P:(n + 1) * P].rearrange("p o k -> p (o k)"))
                eng.drain()
                top16([vtop[:, 0, :], vtop[:, 1, :]], [itop[:, 0, :], itop[:, 1, :]], [work[0][:, :], work[1][:, :]],
                      [rest[0][:, :], rest[1][:, :]])
                k = [P, PEER_TOPK, PEER_TOPK]
                eng.tensor_scalar(itopf[:, 0, :], itop[:, 0, :], float(P), None, ALU.mult)
                eng.tensor_copy(itopf[:, 1, :], itop[:, 1, :])
                eng.tensor_tensor(cand[:, :].rearrange("p (a b) -> p a b", a=PEER_TOPK), vtop[:, 0, :].unsqueeze(2).broadcast_to(k),
                                  vtop[:, 1, :].unsqueeze(1).broadcast_to(k), ALU.add)
                eng.drain()
                top16([ctop[:, :]], [cpos[:, :]], [cand[:, :]], [cand2[:, :]])
                eng.tensor_scalar(cab[:, 0, :], cpos[:, :], 4, None, ALU.logical_shift_right)
                eng.tensor_scalar(cab[:, 1, :], cpos[:, :], PEER_TOPK - 1, None, ALU.bitwise_and)
                eng.drain()
                eng.tensor_copy(cabf[:, :, :], cab[:, :, :])
                eng.drain()
                for n in range(2):
                    pick(n, itopf[:, n, :], cabf[:, n, :])
                eng.drain()
                eng.tensor_tensor(expert[:, tile, ds(h * PEER_TOPK, PEER_TOPK)], epart[:, 0, :], epart[:, 1, :], ALU.add)
                eng.tensor_copy(tops[:, tile, ds(h, 1), :].rearrange("p o k -> p (o k)"), ctop[:, :])
                eng.drain().then_inc(s["idx0_ready"] if tile == 0 else s["idx1_ready"], 1)

            def gates(tile):
                k = [P, PEER_HEADS, PEER_TOPK]
                t_ = tops[:, tile]
                eng.tensor_copy(gsum[:, 0, :], t_[:, :, 0])
                eng.drain()
                eng.tensor_tensor(t_, t_, gsum[:, 0, :].unsqueeze(2).broadcast_to(k), ALU.subtract).then_inc(s["sub_ready"], 1)
                eng.wait_ge(s["gexp_ready"], tile + 1)
                eng.tensor_reduce(gsum[:, 0, :], t_, AX.X, ALU.add)
                eng.drain()
                eng.reciprocal(gsum[:, 1, :], gsum[:, 0, :])
                eng.drain()
                eng.tensor_tensor(t_, t_, gsum[:, 1, :].unsqueeze(2).broadcast_to(k), ALU.mult)
                eng.drain()

            def dots(tile, j):
                n = tile * (SLOTS_PER_TOKEN // GB) + j
                for b in range(GB):
                    eng.wait_ge(u_loaded[b], (n + 1) * 16)
                    if b == 0:
                        if past_zero(n):
                            eng.wait_ge(s["g_ready"], n)
                    eng.tensor_tensor_reduce(out=ubuf[b], in0=ubuf[b], in1=h_tok[:, tile, :], scale=1.0, scalar=0.0,
                                             op0=ALU.mult, op1=ALU.add, accum_out=z4[:, b:b + 1]).then_inc(s["dots_done"], 1)
                eng.drain().then_inc(s["z_ready"], 1)
                eng.wait_ge(s["g_ready"], n + 1)
                eng.tensor_tensor(act4[:, :], g4[:, :], tops[:, tile].rearrange("p h k -> p (h k)")[:, ds(j * GB, GB)], ALU.mult)
                eng.drain()
                for b in range(GB):
                    if past_zero((n - 1) * GB + b + 1):
                        eng.wait_ge(s["acc_done"], (n - 1) * GB + b + 1)
                    eng.tensor_scalar(diag[:, b, :], ident[:, :], act4[:, b:b + 1], None, ALU.mult).then_inc(s["diag_ready"], 1)

            with eng.Fori(0, PEER_HEADS) as h:
                route(0, h)
            gates(0)
            dots(0, 0)
            route(1, 0)
            with eng.Fori(1, PEER_HEADS) as j:
                dots(0, j)
                route(1, j)
            gates(1)
            with eng.Fori(PEER_HEADS, SLOTS_PER_TOKEN // GB) as j:
                dots(0, j)

            def finish(tile, dst):
                eng.wait_ge(s["fss_ready"], tile + 1)
                eng.tensor_reduce(tstat[:, 2, tile:tile + 1], fss[:, 4 * tile:4 * tile + 4], AX.X, ALU.add).then_inc(s["tss_ready"], 1)
                eng.wait_ge(s["frs_ready"], tile + 1)
                for c in range(4):
                    a = slice(c * 512, (c + 1) * 512)
                    last = eng.scalar_tensor_tensor(out=dst[:, a], in0=B[4 * tile + c][:, :], scalar=tstat[:, 3, tile:tile + 1],
                                                    in1=gfin[:, a], op0=ALU.mult, op1=ALU.mult)
                last.then_inc(s["fin_ready"], 1)

            dots(1, 0)
            dots(1, 1)
            finish(0, y_tok[0])
            with eng.Fori(2, SLOTS_PER_TOKEN // GB) as j:
                dots(1, j)
            eng.drain()
            finish(1, y_tok[1])


def kernel(**inputs):
    import numpy as np
    import concourse.bacc as bacc
    from concourse.bass_utils import run_bass_kernel_spmd

    a = {k: np.asarray(v) for k, v in inputs.items()}

    def units(w):
        n = -(-w.shape[1] // P)
        w = np.pad(w, ((0, 0), (0, n * P - w.shape[1])))
        return w.reshape(KC, P, n, P).transpose(2, 1, 0, 3).reshape(n, P, KC * P)

    def wide(v):
        return np.reshape(v, (KC, P)).T

    pack = [wide(a[n][0]) for n in ("a_norm_w", "a_lb_logits", "a_out_norm_w")]
    pack += [wide(a["kv_norm_w"]), wide(a["b_norm_w"][0]), wide(a["b_out_norm_w"][0]), wide(a["norm_mix_g_2"][0])]
    pack += [wide(a["conv_w_2"][0, n]) for n in range(4)]
    pack += [wide(a[n][0]) for n in ("conv_b_2", "rg_ba_2", "rg_bx_2", "rg_lambda_2", "norm_ffn_g_2")]
    pack += [a["k_norm_w"].reshape(P, 1), a["b_q_norm_w"].reshape(P, 1), a["kv_norm_g_2"].reshape(RC, P).T]
    pack += [np.concatenate([a[n][0], a[n][0]]).reshape(P, 1) for n in ("idx_ln_g_2", "idx_ln_b_2")]
    w_c = a["w_in_2"][0]
    i_q = 2 * D + KV_RANK
    i_k = i_q + IDX_HEADS * IDX_DIM
    i_g = i_k + IDX_DIM + IDX_HEADS
    arrays = {
        "x_fm": a["x"][0].T.reshape(KC, P, T).transpose(1, 0, 2),
        "prm_h": np.concatenate(pack, axis=1),
        "f_bias_h": a["kv_f_bias"].reshape(HEADS, 1),
        "w_in_a": units(a["a_w_in"][0]), "w_out_a": units(a["a_w_out"][0]),
        "w_fgate": units(a["kv_w"][:, 2 * D:]), "w_kv": units(a["kv_w"][:, 0:2 * D]),
        "w_in_b": units(a["b_w_in"][0]), "w_out_b": units(a["b_w_out"][0]),
        "w_latent": units(w_c[:, 2 * D:i_q]), "w_ikey": units(w_c[:, i_k:i_g]), "w_iquery": units(w_c[:, i_q:i_k]),
        "w_in_c": np.concatenate([units(w_c[:, c:c + D]) for c in (0, D, i_g, i_g + D)]),
        "rg_wa": a["rg_wa_2"][0], "rg_wx": a["rg_wx_2"][0],
        "w_uk": a["w_uk_2"][0], "w_uv": a["w_uv_2"][0], "w_out_c": units(a["w_o_2"][0]), "w_q": units(a["peer_wq_2"][0]),
        "keys1": a["peer_keys1_2"][0], "keys2": a["peer_keys2_2"][0], "peer_u": a["peer_u_2"][0], "peer_v": a["peer_v_2"][0],
        "g_ffn": a["norm_ffn_g_2"], "g_fin": a["norm_final_g_2"].reshape(1, D),
    }
    arrays = {k: np.ascontiguousarray(v) for k, v in arrays.items()}
    nc = bacc.Bacc("TRN2", target_bir_lowering=False, num_devices=1)
    aps = {k: nc.dram_tensor(k, v.shape, F32, kind="ExternalInput").ap() for k, v in arrays.items()}
    out = nc.dram_tensor("out", (T, D), F32, kind="ExternalOutput").ap()
    program(nc, out=out, **aps)
    r = run_bass_kernel_spmd(nc, [arrays], core_ids=[0])
    return r.results[0]["out"].reshape(1, T, D)
```

```python
from contextlib import ExitStack

import concourse.bass as bass
from concourse import mybir

ALU = mybir.AluOpType
ACT = mybir.ActivationFunctionType
AX = mybir.AxisListType
F32 = mybir.dt.float32
F32R = mybir.dt.float32r
F16 = mybir.dt.float16
U32 = mybir.dt.uint32
ds = bass.ds

P = 128
D = 2048
T = 256
KC = D // P
NT = T // P
HEADS = 16
PAIRS = HEADS // 2
G = 2 * P
W2 = 2 * T
EPS = 1e-6
HD_SCALE = float(P) ** -0.5
LEVELS = 7
SC = P + T
NEG = -1e30
TAKEN = -3.3e38
KV_RANK = 512
RC = KV_RANK // P
IDX_HEADS = 16
IDX_DIM = 64
TOPK = min(256, T // 4)
RG_C = 8.0
PEER_HEADS = 8
PEER_TOPK = 16
SLOTS_PER_TOKEN = PEER_HEADS * PEER_TOPK
BJ = 32
BLOCKS = P // BJ
TG = T // BJ
G_SCALE = 2.0 ** 14
FH = KC // 2

PRM = {}
for _n in ("a_norm", "a_lb", "a_onorm", "kv_norm", "b_norm", "b_onorm", "mix", "cw0", "cw1", "cw2", "cw3",
           "cb", "ba", "bx", "lam", "ffn", "fin"):
    PRM[_n] = len(PRM) * KC
PRM["k_norm"] = 17 * KC
PRM["q_norm"] = PRM["k_norm"] + 1
PRM["ckv"] = PRM["q_norm"] + 1
PRM["idx_g"] = PRM["ckv"] + RC
PRM["idx_b"] = PRM["idx_g"] + 1
NPRM = PRM["idx_b"] + 1

UNITS = {"A": 64, "OA": 16, "FG": 1, "F": 64, "OF": 16, "X": 13, "C": 64, "OC": 16, "Q": 16,
         "U0": 32, "U1": 32, "V0": 32, "U2": 32, "V1": 32, "U3": 32, "V2": 32, "V3": 32}
BASE = {}
_n = 0
for _k, _v in UNITS.items():
    BASE[_k] = _n
    _n += _v
ALL_UNITS = _n
PEER_ORDER = [(_k[0], int(_k[1])) for _k in UNITS if _k[0] in "UV"]
PER_PAIR = 8
RAW = 4
NORM_AT = {"A": 0, "F": 1, "C": 2, "Q": 3}
SPLIT_AT = {"A": 0, "F": 8, "C": 24, "Q": 32}
MIX_AT = {"A": 0, "F": PAIRS, "C": 2 * PAIRS}


def past_zero(value):
    return not isinstance(value, int) or value > 0


def unit(i, c, per_unit, more):
    return i * (PER_PAIR * per_unit) + (c * per_unit + more)


def program(nc, x_fm, prm_h, f_bias_h, w_in_a, w_out_a, w_fgate, w_kv, w_in_b, w_out_b, w_latent, w_ikey, w_iquery, w_in_c,
            rg_wa, rg_wx, w_uk, w_uv, w_out_c, w_q, keys1, keys2, peer_u, peer_v, out):
    ctx = ExitStack()
    with ctx:
        def sb_in(stack, name, shape, dt=F32):
            return stack.enter_context(nc.sbuf_tensor(name, shape, dt))

        def sem(name):
            return ctx.enter_context(nc.semaphore(name))

        def sb(name, shape, dt=F32):
            return sb_in(ctx, name, shape, dt)

        xT = sb("xT", [P, KC, T])
        hh = sb("hh", [P, KC, T], F32R)
        hl = sb("hl", [P, KC, T], F32R)
        raw = sb("raw", [P, RAW, KC * P])
        iota = sb("iota", [P, P])
        prm = sb("prm", [P, NPRM])
        fbias = sb("fbias", [HEADS, 1])
        ident = sb("ident", [P, P])
        ones = sb("ones", [P, P])
        eps = sb("eps", [P, 1])
        lb = sb("lb", [P, KC])
        omlb = sb("omlb", [P, KC])
        rg_c = sb("rg_c", [P, KC])
        qw = sb("qw", [P, 1])
        tri = sb("tri", [P, SC])
        rstd = sb("rstd", [P, T])
        wh = [sb(f"wh{n}", [P, KC, P], F32R) for n in range(2)]
        wl = [sb(f"wl{n}", [P, KC, P], F32R) for n in range(2)]
        layers = ExitStack()
        oT = sb_in(layers, "oT", [P, KC, T])
        sq = sb_in(layers, "sq", [P, 2, W2])
        vf = sq[:, 1, :].rearrange("p (j t) -> p j t", j=2)
        kw_fm = sq[:, 1, 0:T]
        sp = sb_in(layers, "sp", [P, 8, KC])
        B = [ctx.enter_context(nc.psum_tensor(f"bank{b}", [P, 512], F32)) for b in range(8)]

        w_loaded = [sem(f"w_loaded{s}") for s in range(RAW)]
        hi_ready = sem("hi_ready")
        lo_ready = sem("lo_ready")
        mm_done = sem("mm_done")
        sp_passed = sem("sp_passed")
        params_in = sem("params_in")
        bias_in = sem("bias_in")
        x_in = [sem(f"x_in{c}") for c in range(4)]
        consts_ready = sem("consts_ready")
        lb_e_ready = sem("lb_e_ready")
        lam_e_ready = sem("lam_e_ready")
        lam_w_ready = sem("lam_w_ready")
        lam_l_ready = sem("lam_l_ready")

        x_ready = sem("x_ready")
        sq_ready = sem("sq_ready")
        ss_done = sem("ss_done")
        rstd_ready = sem("rstd_ready")
        hf_ready = sem("hf_ready")
        hh_ready = sem("hh_ready")
        hl_ready = sem("hl_ready")
        mixed = sem("mixed")
        oh_ready = sem("oh_ready")
        ol_ready = sem("ol_ready")

        def per_stage(stage, names):
            return {n: sem(f"{stage}_{n}") for n in names.split()}

        sA = per_stage("A", "fz_read qz_ready vf_ready vt_done v_ready sig_ready gate_read f_ready lv_done at_ready o_done o_read "
                            "osq_ready oss_done ors_ready")
        sF = per_stage("F", "z_ready l_ready ksq_ready kss_done krs_ready kn_ready "
                            "qsq_ready qss_done qrs_ready qn_ready vf_ready vt_done v_ready sig_ready gate_read sel_ready s_done "
                            "nmax_ready e_done p_ready pt_done pt_ready o_done o_read osq_ready oss_done ors_ready")
        sX = per_stage("X", "ckv_read csq_ready css_done crs_ready ckv_ready kwf_ready kwt_done kw_ready kc_ready krs_ready "
                            "kn_ready kt_done kt_ready qi_ready rel_done relu_ready relu_used")
        sC = per_stage("C", "small_in xr_read xc_ready rg_done ri_read la_ready ex_ready prod_ready root_ready q_ready "
                            "kv_done kT_ready v_ready rsig_ready asig_ready mix_ready s_done nmax_ready e_done "
                            "p_ready pt_done pt_ready o_done o_read")
        sQ = per_stage("Q", "keys_in kt_done kt_ready qp_ready sc_done sc_ready sub_ready gexp_ready routed rt_done "
                            "slots_ready z_read pairs_ready g_done g_read gated ah_ready al_ready x_added "
                            "zsq_ready zss_done zrs_ready y_ready stored")

        m = ExitStack()
        f0 = sb_in(m, "f0", [P, W2])
        k0 = sb_in(m, "k0", [P, W2])
        q_a = sb_in(m, "q_a", [P, W2])
        QL = [sb_in(m, f"QL{n}", [P, W2]) for n in range(LEVELS + 1)]
        KL = [sb_in(m, f"KL{n}", [P, W2]) for n in range(LEVELS + 1)]
        TL = [sb_in(m, f"TL{n}", [P, W2 >> n]) for n in range(LEVELS)]
        lmask = sb_in(m, "lmask", [P, LEVELS, P // 2])
        AT = sb_in(m, "AT", [P, 2 * NT, P])
        AToff = sb_in(m, "AToff", [P, 2, P])
        v_a = sb_in(m, "v_a", [P, NT, G])
        osq_a = sb_in(m, "osq_a", [P, W2])
        ors_a = sb_in(m, "ors_a", [P, W2])
        on_a = sb_in(m, "on_a", [P, W2])
        sig_a = sb_in(m, "sig_a", [P, W2])
        gate_a = sb_in(m, "gate_a", [P, W2])
        m.close()
        m = ExitStack()
        kh = sb_in(m, "kh", [P, KC, T], F32R)
        kl = sb_in(m, "kl", [P, KC, T], F32R)
        fcum = sb_in(m, "fcum", [P, T])
        fneg = sb_in(m, "fneg", [P, T])
        selF = sb_in(m, "selF", [P, 2, T])
        selO = sb_in(m, "selO", [P, 2, T])
        ksq = sb_in(m, "ksq", [P, W2])
        krs = sb_in(m, "krs", [P, W2])
        qsq = sb_in(m, "qsq", [P, W2])
        qrs = sb_in(m, "qrs", [P, W2])
        kT_f = sb_in(m, "kT_f", [P, 2, T])
        qT_f = sb_in(m, "qT_f", [P, 2, T])
        v_f = sb_in(m, "v_f", [P, NT, G])
        osq_f = sb_in(m, "osq_f", [P, W2])
        ors_f = sb_in(m, "ors_f", [P, W2])
        on_f = sb_in(m, "on_f", [P, W2])
        sig_f = sb_in(m, "sig_f", [P, W2])
        gate_f = sb_in(m, "gate_f", [P, W2])
        prob_f = sb_in(m, "prob_f", [P, 2, SC])
        probT_f = sb_in(m, "probT_f", [P, 2, SC])
        fz = [(prob_f if n < 3 else probT_f)[0:HEADS, :, :].rearrange("p a b -> p (a b)")[:, (n % 3) * T:(n % 3 + 1) * T]
              for n in range(5)]
        nmax_f = sb_in(m, "nmax_f", [P, 4])
        rsum_f = sb_in(m, "rsum_f", [P, 4])
        rinv_f = sb_in(m, "rinv_f", [P, 4])
        m.close()
        m = ExitStack()
        ckvT = sb_in(m, "ckvT", [P, RC, T])
        selmask = sb_in(m, "selmask", [P, SC])
        iscore = sb_in(m, "iscore", [P, SC])
        top8 = sb_in(m, "top8", [P, 2, 8])
        x = ExitStack()
        csq = sb_in(x, "csq", [P, RC, T])
        crs = sb_in(x, "crs", [P, T])
        kw = sb_in(x, "kw", [P, NT, IDX_DIM + IDX_HEADS])
        kc = sb_in(x, "kc", [P, NT, IDX_DIM])
        kdup = sb_in(x, "kdup", [P, NT, 2, IDX_DIM])
        kst = sb_in(x, "kst", [P, 4, NT])
        kiT = sb_in(x, "kiT", [P, T])
        qi = sb_in(x, "qi", [P, 2, W2])
        relu = sb_in(x, "relu", [P, 4, SC])
        x.close()
        uk = sb_in(m, "uk", [P, 2, RC, P])
        uv = sb_in(m, "uv", [P, RC, 2, P])
        wa = sb_in(m, "wa", [P, 2, P])
        wx = sb_in(m, "wx", [P, 2, P])
        xc = sb_in(m, "xc", [P, 2, T])
        rg = sb_in(m, "rg", [P, 2, 2, T])
        la = sb_in(m, "la", [P, W2])
        ae = sb_in(m, "ae", [P, 3, W2])
        ub = sb_in(m, "ub", [P, 2, W2])
        hs = sb_in(m, "hs", [P, W2])
        rsig = sb_in(m, "rsig", [P, W2])
        asig = sb_in(m, "asig", [P, W2])
        mixr = sb_in(m, "mixr", [P, W2])
        qT_c = sb_in(m, "qT_c", [P, 2, T])
        kT_c = sb_in(m, "kT_c", [P, 2, T])
        v_c = sb_in(m, "v_c", [P, NT, G])
        on_c = sb_in(m, "on_c", [P, W2])
        prob_c = sb_in(m, "prob_c", [P, 2, SC])
        probT_c = sb_in(m, "probT_c", [P, 2, SC])
        nmax_c = sb_in(m, "nmax_c", [P, 4])
        rsum_c = sb_in(m, "rsum_c", [P, 4])
        rinv_c = sb_in(m, "rinv_c", [P, 4])
        m.close()
        layers.close()
        m = ExitStack()
        act = sb_in(m, "act", [P, BJ, T])
        r = ExitStack()
        S12 = sb_in(r, "S12", [P, NT, PEER_HEADS, 2 * P])
        keys = sb_in(r, "keys", [P, 2, P])
        keysT = sb_in(r, "keysT", [P, 2, P])
        qp = sb_in(r, "qp", [P, 2, 2, T])
        work = [sb_in(r, f"work{n}", [P, P]) for n in range(4)]
        rest = [sb_in(r, f"rest{n}", [P, P]) for n in range(4)]
        vtop = sb_in(r, "vtop", [P, 4, PEER_TOPK])
        itop = sb_in(r, "itop", [P, 4, PEER_TOPK], U32)
        itopf = sb_in(r, "itopf", [P, 4, PEER_TOPK])
        epart = sb_in(r, "epart", [P, 4, PEER_TOPK])
        cand = sb_in(r, "cand", [P, NT, PEER_TOPK * PEER_TOPK])
        ctop = sb_in(r, "ctop", [P, NT, PEER_TOPK])
        cpos = sb_in(r, "cpos", [P, NT, PEER_TOPK], U32)
        cab = sb_in(r, "cab", [P, NT, 2, PEER_TOPK], U32)
        cabf = sb_in(r, "cabf", [P, NT, 2, PEER_TOPK])
        onehot = sb_in(r, "onehot", [P, 4, PEER_TOPK, PEER_TOPK])
        cand2 = [onehot[:, t].rearrange("p a b -> p (a b)") for t in range(NT)]
        tops = sb_in(r, "tops", [P, NT, PEER_HEADS, PEER_TOPK])
        place = sb_in(r, "place", [P, NT, 2, SLOTS_PER_TOKEN])
        gsum = sb_in(r, "gsum", [P, 2, PEER_HEADS])
        r.close()
        act_odd = sb_in(m, "act_odd", [P, BJ, T])
        acts = [act, act_odd]
        hot_a = [sb_in(m, f"hot_a{n}", [P, TG, P], F16) for n in range(2)]
        hot_b = sb_in(m, "hot_b", [P, TG, BJ])
        gates_b = [sb_in(m, f"gates_b{n}", [P, TG, 2, BJ], F16) for n in range(2)]
        gsums = sb_in(m, "gsums", [P, TG, BJ])
        ah = [sb_in(m, f"ah{n}", [P, 2, T], F32R) for n in range(2)]
        al = [sb_in(m, f"al{n}", [P, 2, T], F32R) for n in range(2)]
        slotT = sb_in(m, "slotT", [P, 2, T])
        gT = sb_in(m, "gT", [P, T, 2], F16)
        m.close()
        y = act[:, 0:KC, :]
        zsq = act[:, KC:2 * KC, :].rearrange("p (n k) t -> p n (k t)", k=2)

        def col(name, j):
            return prm[:, ds(j + PRM[name], 1)] if not isinstance(j, int) else prm[:, PRM[name] + j:PRM[name] + j + 1]

        def chunk(t, j, n=1):
            return t[:, ds(j, n), :].rearrange("p k t -> p (k t)")

        def halves(t, h):
            return t.rearrange("p (b two r) -> p b two r", two=2, r=h)

        def over(t, n):
            return t.unsqueeze(2).broadcast_to([P, t.shape[1], n])

        block = ctx.enter_context(nc.Block())

        @block.sync
        def _(eng):
            def load(i, c, src):
                if past_zero(unit(i, c, 2, 2 - 2 * RAW)):
                    eng.wait_ge(lo_ready, unit(i, c, 2, 2 - 2 * RAW))
                    eng.sem_inc(sp_passed, 1)
                eng.dma_start(raw[:, c % RAW, :], src).then_inc(w_loaded[c % RAW], 16)

            def one(w, n):
                return w[ds(n, 1)].rearrange("o p n -> p (o n)")

            def pairs(stage, sources, more=None):
                def body(i):
                    for r, (w, at) in enumerate(sources):
                        for j in range(2):
                            load(i, BASE[stage] + 2 * r + j, one(w, i * 2 + (at + j)))
                        if r == 1 and more is not None:
                            more(i)
                body(0)
                with eng.Fori(1, PAIRS) as i:
                    body(i)

            def row(stage, w, n, first=0):
                for c in range(n):
                    load(0, BASE[stage] + first + c, one(w, c))

            eng.dma_start(prm[:, :], prm_h).then_inc(params_in, 16)
            for c in range(4):
                eng.dma_start(xT[:, 4 * c:4 * c + 4, :], x_fm[:, 4 * c:4 * c + 4, :]).then_inc(x_in[c], 16)
            eng.dma_start(fbias[:, :], f_bias_h).then_inc(bias_in, 16)
            pairs("A", [(w_in_a, HEADS), (w_in_a, 0), (w_in_a, 2 * HEADS), (w_in_a, 3 * HEADS)])
            row("OA", w_out_a, KC)
            row("FG", w_fgate, 1)
            pairs("F", [(w_kv, 0), (w_in_b, 0), (w_kv, HEADS), (w_in_b, HEADS)])
            row("OF", w_out_b, KC)
            row("X", w_latent, RC)
            row("X", w_ikey, 1, RC)
            row("X", w_iquery, PEER_HEADS, RC + 1)

            def small(i):
                if past_zero(i * 2):
                    eng.wait_ge(sC["kv_done"], i * 2)
                    eng.sem_inc(sp_passed, 1)
                else:
                    eng.wait_ge(sX["relu_used"], IDX_HEADS)
                for j in range(2):
                    eng.dma_start(uk[:, j], w_uk[ds(i * 2 + j, 1)].rearrange("h (c p) d -> p (h c) d", p=P)).then_inc(sC["small_in"], 16)
                    eng.dma_start(uv[:, :, j], w_uv[ds(i * 2 + j, 1)].rearrange("h (c p) d -> p (h c) d", p=P)).then_inc(sC["small_in"], 16)
                for dst, src in ((wa, rg_wa), (wx, rg_wx)):
                    eng.dma_start(dst[:, :, :], src[ds(i * 2, 2)].rearrange("n c d -> c n d")).then_inc(sC["small_in"], 16)

            pairs("C", [(w_in_c, 0), (w_in_c, HEADS), (w_in_c, 2 * HEADS), (w_in_c, 3 * HEADS)], small)
            row("OC", w_out_c, KC)
            eng.wait_ge(mixed, MIX_AT["C"] + PAIRS)
            for n, k_ in enumerate((keys1, keys2)):
                eng.dma_start(keys[:, n, :], k_).then_inc(sQ["keys_in"], 16)
            row("Q", w_q, KC)

            def block_of(name, table, b):
                with eng.Fori(0, BJ // PER_PAIR) as i:
                    for c in range(PER_PAIR):
                        load(i, BASE[f"{name}{b}"] + c, one(table, i * PER_PAIR + (b * BJ + c)))

            for name, b in PEER_ORDER:
                block_of(name, peer_u if name == "U" else peer_v, b)
            for c in range(FH):
                eng.wait_ge(sQ["y_ready"], c + 1)
                eng.dma_start(out[:, 2 * c:2 * c + 2, :], y[:, 2 * c:2 * c + 2, :]).then_inc(sQ["stored"], 16)
            eng.wait_ge(sQ["stored"], 16 * FH)

        @block.gpsimd
        def _(eng):
            eng.memset(ones[:, :], 1.0)
            eng.memset(eps[:, :], EPS)
            eng.memset(ident[:, :], 0.0)
            eng.memset(tri[:, :], 0.0)
            eng.memset(lmask[:, :, :], 1.0)
            eng.drain()
            eng.affine_select(out=ident[:, :], in_=ident[:, :], pattern=[[-1, P]], compare_op=ALU.not_equal, fill=1.0,
                              base=0, channel_multiplier=1)
            for a in (0, T):
                eng.affine_select(out=tri[:, a:a + P], in_=tri[:, a:a + P], pattern=[[-1, P]], compare_op=ALU.is_ge,
                                  fill=NEG, base=0, channel_multiplier=1)
            for l in range(LEVELS):
                h, nb = 1 << l, P >> (l + 1)
                v = lmask[:, l, :].rearrange("p (b r) -> p b r", r=h)
                eng.affine_select(out=v, in_=v, pattern=[[-2 * h, nb], [0, h]], compare_op=ALU.is_ge, fill=0.0,
                                  base=0, channel_multiplier=1)
            eng.drain()
            for l in range(LEVELS):
                h, nb = 1 << l, P >> (l + 1)
                v = lmask[:, l, :].rearrange("p (b r) -> p b r", r=h)
                last = eng.affine_select(out=v, in_=v, pattern=[[2 * h, nb], [0, h]], compare_op=ALU.is_ge, fill=0.0,
                                         base=h - 1, channel_multiplier=-1)
            eng.drain().then_inc(consts_ready, 1)

            eng.iota(iota[:, :], pattern=[[1, P]], base=0, channel_multiplier=0,
                     allow_small_or_imprecise_dtypes=True).then_inc(consts_ready, 1)

            def low_part(i, c):
                for half in range(2):
                    k = slice(half * KC // 2, (half + 1) * KC // 2)
                    eng.wait_ge(hi_ready, i * (2 * RAW) + (2 * c + half + 1))
                    eng.tensor_tensor(wl[c % 2][:, k, :], raw[:, c % RAW, :].rearrange("p (k n) -> p k n", k=KC)[:, k, :],
                                      wh[c % 2][:, k, :].bitcast(F32), ALU.subtract).then_inc(lo_ready, 1)

            with eng.Fori(0, ALL_UNITS // RAW) as i:
                for c in range(RAW):
                    low_part(i, c)
            for c in range(ALL_UNITS % RAW):
                low_part(ALL_UNITS // RAW, c)

        @block.tensor
        def _(eng):
            def product(i, c, out, high, low, fresh=None):
                h_, l_ = wh[c % 2], wl[c % 2]
                for half in range(2):
                    eng.wait_ge(lo_ready, unit(i, c, 2, half + 1))
                    for k in range(half * KC // 2, (half + 1) * KC // 2):
                        if fresh is not None and k % 2 == 0:
                            eng.wait_ge(fresh[0], fresh[1] + k // 2 + 1)
                        eng.matmul(out, h_[:, k, :], high[:, k, :], start=(k == 0), stop=False)
                        eng.matmul(out, h_[:, k, :], low[:, k, :], start=False, stop=False)
                        last = eng.matmul(out, l_[:, k, :], high[:, k, :], start=False, stop=(k == KC - 1))
                    last.then_inc(mm_done, 1)

            def project(stage, s, i, high, low, fresh=None):
                for j in range(2):
                    product(i, BASE[stage] + 2 * s + j, B[s][:, j * T:(j + 1) * T], high, low, fresh if j == 0 else None)

            def transpose_values(s, i):
                eng.wait_ge(s["vf_ready"], i + 1)
                for t in range(NT):
                    for j in range(2):
                        last = eng.transpose(B[2][:, t * G + j * P:t * G + (j + 1) * P], vf[:, j, t * P:(t + 1) * P], ident[:, :])
                last.then_inc(s["vt_done"], 1)

            def norm_sum(name, g):
                eng.wait_ge(sq_ready, 8 * NORM_AT[name] + g + 1)
                for c in range(2):
                    last = eng.matmul(B[4][:, 0:T], ones[:, :], sq[:, g % 2, c * T:(c + 1) * T],
                                      start=(g == 0 and c == 0), stop=(g == KC // 2 - 1 and c == 1))
                last.then_inc(ss_done, 1)

            def out_projection(stage, mixer, name):
                for g in range(KC // 2):
                    if g >= 4:
                        eng.wait_ge(x_ready, 8 * (NORM_AT[name] - 1) + g - 3)
                    for j in range(2):
                        product(0, BASE[stage] + 2 * g + j, B[g % 4][:, j * T:(j + 1) * T], hh, hl,
                                (ol_ready, MIX_AT[mixer]) if g == 0 and j == 0 else None)
                    if g >= 1:
                        norm_sum(name, g - 1)
                norm_sum(name, KC // 2 - 1)

            def pair_loop(body):
                body(0, True)
                with eng.Fori(1, PAIRS) as i:
                    body(i, False)

            def head_sum(bank, src, done):
                eng.matmul(B[bank][:, :], ones[:, :], src[:, :], start=True, stop=True).then_inc(done, 1)

            def transpose_probs(prob, done):
                for j in range(2):
                    for a in range(3):
                        last = eng.transpose(B[6 + j][:, a * P:(a + 1) * P], prob[:, j, a * P:(a + 1) * P], ident[:, :])
                    last.then_inc(done, 1)

            def weigh_values(bank, v, probT, done):
                for j in range(2):
                    c = slice(j * P, (j + 1) * P)
                    o = j * T
                    eng.matmul(B[bank][:, o:o + P], v[:, 0, c], probT[:, j, 0:P], start=True, stop=True)
                    eng.matmul(B[bank][:, o + P:o + T], v[:, 0, c], probT[:, j, P:2 * P], start=True, stop=False)
                    last = eng.matmul(B[bank][:, o + P:o + T], v[:, 1, c], probT[:, j, 2 * P:3 * P], start=False, stop=True)
                last.then_inc(done, 1)

            eng.wait_ge(consts_ready, 1)
            for g in range(KC // 2):
                norm_sum("A", g)

            s = sA

            def a_values(i):
                eng.wait_ge(s["at_ready"], i + 1)
                eng.wait_ge(s["v_ready"], i + 1)
                for j in range(2):
                    c = slice(j * P, (j + 1) * P)
                    eng.matmul(B[4][:, j * T:j * T + P], v_a[:, 0, c], AT[:, 2 * j, :], start=True, stop=True)
                    eng.matmul(B[4][:, j * T + P:(j + 1) * T], v_a[:, 0, c], AToff[:, j, :], start=True, stop=False)
                    last = eng.matmul(B[4][:, j * T + P:(j + 1) * T], v_a[:, 1, c], AT[:, 2 * j + 1, :], start=False, stop=True)
                last.then_inc(s["o_done"], 1)

            def a_norm(i):
                eng.wait_ge(s["osq_ready"], i + 1)
                head_sum(5, osq_a, s["oss_done"])

            def a_levels(i):
                if past_zero(i):
                    eng.wait_ge(s["o_read"], i)
                    eng.wait_ge(s["ors_ready"], i)
                eng.wait_ge(s["f_ready"], i + 1)
                for j in range(2):
                    for t in range(NT):
                        a = j * T + t * P
                        eng.matmul(B[4][:, a:a + P], KL[0][:, a:a + P], q_a[:, a:a + P], start=True, stop=True)
                for l in range(LEVELS):
                    h = 1 << l
                    bank, at = (B[5 + l // 2], (l % 2) * T) if l < 6 else (B[3], 0)
                    if l == 6:
                        eng.wait_ge(s["gate_read"], i + 1)
                    for n in range(2 * NT):
                        last = eng.matmul(bank[:, at + n * (P // 2):at + (n + 1) * (P // 2)], KL[l][:, n * P:(n + 1) * P],
                                          halves(QL[l][:, n * P:(n + 1) * P], h)[:, :, 1, :], start=True, stop=True)
                for j in range(2):
                    last = eng.matmul(B[3][:, T + j * P:T + (j + 1) * P], KL[7][:, j * T:j * T + P],
                                      QL[7][:, j * T + P:(j + 1) * T], start=True, stop=True)
                last.then_inc(s["lv_done"], 1)

            def a_body(i, first):
                if past_zero(i):
                    eng.wait_ge(s["fz_read"], i)
                project("A", 0, i, hh, hl, (hl_ready, SPLIT_AT["A"]) if first else None)
                if not first:
                    a_values(i - 1)
                if past_zero(i):
                    eng.wait_ge(s["qz_ready"], i)
                project("A", 1, i, hh, hl)
                if not first:
                    a_norm(i - 1)
                if past_zero(i):
                    eng.wait_ge(s["v_ready"], i)
                project("A", 2, i, hh, hl)
                if past_zero(i):
                    eng.wait_ge(s["at_ready"], i)
                project("A", 3, i, hh, hl)
                transpose_values(s, i)
                a_levels(i)

            pair_loop(a_body)
            a_values(PAIRS - 1)
            a_norm(PAIRS - 1)
            out_projection("OA", "A", "F")

            s = sF
            product(0, BASE["FG"], B[5][:, 0:T], kh, kl, (hl_ready, SPLIT_AT["F"]))

            def f_transpose(i):
                eng.wait_ge(s["p_ready"], i + 1)
                transpose_probs(prob_f, s["pt_done"])

            def f_values(i):
                eng.wait_ge(s["pt_ready"], i + 1)
                eng.wait_ge(s["v_ready"], i + 1)
                weigh_values(5, v_f, probT_f, s["o_done"])

            def f_norm(i):
                eng.wait_ge(s["osq_ready"], i + 1)
                head_sum(6, osq_f, s["oss_done"])

            def f_body(i, first):
                if past_zero(i):
                    eng.wait_ge(s["kn_ready"], i)
                project("F", 0, i, kh, kl)
                if not first:
                    f_transpose(i - 1)
                if past_zero(i):
                    eng.wait_ge(s["qn_ready"], i)
                project("F", 1, i, hh, hl, (hl_ready, SPLIT_AT["F"] + 8) if first else None)
                eng.wait_ge(s["ksq_ready"], i + 1)
                if past_zero(i):
                    eng.wait_ge(s["qrs_ready"], i)
                head_sum(4, ksq, s["kss_done"])
                if not first:
                    f_values(i - 1)
                if past_zero(i):
                    eng.wait_ge(s["v_ready"], i)
                project("F", 2, i, kh, kl)
                eng.wait_ge(s["qsq_ready"], i + 1)
                eng.wait_ge(s["krs_ready"], i + 1)
                head_sum(4, qsq, s["qss_done"])
                if not first:
                    f_norm(i - 1)
                if past_zero(i):
                    eng.wait_ge(s["gate_read"], i)
                project("F", 3, i, hh, hl)
                transpose_values(s, i)
                eng.wait_ge(s["kn_ready"], i + 1)
                eng.wait_ge(s["qn_ready"], i + 1)
                eng.wait_ge(s["sel_ready"], i + 1)
                if past_zero(i):
                    eng.wait_ge(s["ors_ready"], i)
                for j in range(2):
                    for t in range(NT):
                        n = (t + 1) * P
                        o = B[6 + j][:, t * P:t * P + n]
                        tt = slice(t * P, (t + 1) * P)
                        eng.matmul(o, qT_f[:, j, tt], kT_f[:, j, 0:n], start=True, stop=False)
                        eng.matmul(o, ones[:, :], selF[:, j, 0:n], start=False, stop=False)
                        last = eng.matmul(o, fcum[:, tt], selO[:, j, 0:n], start=False, stop=True)
                    last.then_inc(s["s_done"], 1)

            pair_loop(f_body)
            f_transpose(PAIRS - 1)
            f_values(PAIRS - 1)
            f_norm(PAIRS - 1)
            out_projection("OF", "F", "C")

            s = sX
            u = BASE["X"]
            for c in range(RC):
                product(0, u + c, B[c // 2][:, (c % 2) * T:(c % 2 + 1) * T], hh, hl, (hl_ready, SPLIT_AT["C"]) if c == 0 else None)
            product(0, u + RC, B[2][:, 0:T], hh, hl)
            eng.wait_ge(s["csq_ready"], 1)
            for c in range(RC):
                last = eng.matmul(B[4][:, 0:T], ones[:, :], csq[:, c, :], start=(c == 0), stop=(c == RC - 1))
            last.then_inc(s["css_done"], 1)
            eng.wait_ge(s["kwf_ready"], 1)
            for t in range(NT):
                last = eng.transpose(B[5][:, t * P:(t + 1) * P], kw_fm[:, t * P:(t + 1) * P], ident[:, :])
            last.then_inc(s["kwt_done"], 1)

            def index_scores(g):
                eng.wait_ge(s["qi_ready"], g + 1)
                for q in range(4):
                    n = 4 * g + q
                    b = 6 + n % 2
                    if past_zero(n - 1):
                        eng.wait_ge(s["relu_ready"], n - 1)
                    pr = slice(IDX_DIM * (q % 2), IDX_DIM * (q % 2 + 1))
                    for t in range(NT):
                        a = (q // 2) * T + t * P
                        last = eng.matmul(B[b][:, t * P:t * P + (t + 1) * P], qi[pr, g % 2, a:a + P], kiT[pr, 0:(t + 1) * P],
                                          start=True, stop=True)
                    last.then_inc(s["rel_done"], 1)

            for g in range(4):
                bank = 3 if g % 2 == 0 else 0
                if g == 1:
                    eng.wait_ge(s["ckv_read"], 1)
                if past_zero(g - 1):
                    eng.wait_ge(s["qi_ready"], g - 1)
                for j in range(2):
                    product(0, u + RC + 1 + 2 * g + j, B[bank][:, j * T:(j + 1) * T], hh, hl)
                if g == 0:
                    eng.wait_ge(s["kn_ready"], 1)
                    for t in range(NT):
                        last = eng.transpose(B[5][:, t * P:(t + 1) * P], kdup[:, t].rearrange("p a d -> p (a d)"), ident[:, :])
                    last.then_inc(s["kt_done"], 1)
                if g == 1:
                    eng.wait_ge(s["kt_ready"], 1)
                if g >= 1:
                    index_scores(g - 1)
            index_scores(3)
            eng.wait_ge(s["relu_ready"], IDX_HEADS)

            s = sC
            eng.wait_ge(sX["ckv_ready"], 1)

            def c_transpose(i):
                eng.wait_ge(s["p_ready"], i + 1)
                transpose_probs(prob_c, s["pt_done"])

            def c_values(i):
                eng.wait_ge(s["pt_ready"], i + 1)
                eng.wait_ge(s["v_ready"], i + 1)
                weigh_values(6, v_c, probT_c, s["o_done"])

            def c_body(i, first):
                if past_zero(i):
                    eng.wait_ge(s["xr_read"], i)
                project("C", 0, i, hh, hl)
                if not first:
                    c_transpose(i - 1)
                if past_zero(i):
                    eng.wait_ge(s["q_ready"], i)
                project("C", 1, i, hh, hl)
                eng.wait_ge(s["small_in"], (i + 1) * 96)
                eng.wait_ge(s["xc_ready"], i + 1)
                if past_zero(i):
                    eng.wait_ge(s["kT_ready"], i)
                    eng.wait_ge(s["v_ready"], i)
                for n, w in enumerate((wa, wx)):
                    for j in range(2):
                        last = eng.matmul(B[4 + n][:, j * T:(j + 1) * T], w[:, j, :], xc[:, j, :], start=True, stop=True)
                last.then_inc(s["rg_done"], 1)
                if not first:
                    c_values(i - 1)
                if past_zero(i):
                    eng.wait_ge(s["mix_ready"], i)
                project("C", 2, i, hh, hl)
                eng.wait_ge(s["ri_read"], i + 1)
                for j in range(2):
                    for c in range(RC):
                        last = eng.matmul(B[4][:, j * T:(j + 1) * T], uk[:, j, c, :], ckvT[:, c, :],
                                          start=(c == 0), stop=(c == RC - 1))
                last.then_inc(s["kv_done"], 1)
                for t in range(NT):
                    for c in range(RC):
                        last = eng.matmul(B[5][:, t * G:(t + 1) * G], ckvT[:, c, t * P:(t + 1) * P],
                                          uv[:, c].rearrange("p h d -> p (h d)"), start=(c == 0), stop=(c == RC - 1))
                last.then_inc(s["kv_done"], 1)
                if past_zero(i):
                    eng.wait_ge(s["asig_ready"], i)
                project("C", 3, i, hh, hl)
                eng.wait_ge(s["kT_ready"], i + 1)
                eng.wait_ge(s["q_ready"], i + 1)
                if past_zero(i):
                    eng.wait_ge(s["o_read"], i)
                for j in range(2):
                    for t in range(NT):
                        n = (t + 1) * P
                        last = eng.matmul(B[6 + j][:, t * P:t * P + n], qT_c[:, j, t * P:(t + 1) * P], kT_c[:, j, 0:n],
                                          start=True, stop=True)
                    last.then_inc(s["s_done"], 1)

            pair_loop(c_body)
            c_transpose(PAIRS - 1)
            c_values(PAIRS - 1)
            out_projection("OC", "C", "Q")

            s = sQ
            eng.wait_ge(s["keys_in"], 32)
            for n in range(2):
                last = eng.transpose(B[6][:, n * P:(n + 1) * P], keys[:, n, :], ident[:, :])
            last.then_inc(s["kt_done"], 1)

            def key_scores(g):
                eng.wait_ge(s["qp_ready"], g + 1)
                if g == 0:
                    eng.wait_ge(s["kt_ready"], 1)
                if past_zero(g - 1):
                    eng.wait_ge(s["sc_ready"], g - 1)
                for t in range(NT):
                    for n in range(2):
                        last = eng.matmul(B[4 + g % 2][:, (2 * t + n) * P:(2 * t + n + 1) * P],
                                          qp[:, g % 2, n, t * P:(t + 1) * P], keysT[:, n, :], start=True, stop=True)
                last.then_inc(s["sc_done"], 1)

            for g in range(PEER_HEADS):
                if past_zero(g - 3):
                    eng.wait_ge(s["qp_ready"], g - 3)
                for j in range(2):
                    product(0, BASE["Q"] + 2 * g + j, B[g % 4][:, j * T:(j + 1) * T], hh, hl,
                            (hl_ready, SPLIT_AT["Q"]) if g == 0 and j == 0 else None)
                if g >= 1:
                    key_scores(g - 1)
            key_scores(PEER_HEADS - 1)

            def spread(b, i, c):
                n = i * PER_PAIR + (b * BJ + c)
                eng.wait_ge(s["pairs_ready"], n + 1)
                if past_zero(n - 1):
                    eng.wait_ge(s["g_read"], n - 1)
                for t in range(TG):
                    last = eng.matmul(B[6 + c % 2][:, t * 2 * BJ:(t + 1) * 2 * BJ], hot_a[c % 2][:, t, :],
                                      gates_b[c % 2][:, t].rearrange("p n b -> p (n b)"), start=True, stop=True)
                last.then_inc(s["g_done"], 1)

            def dots(b, i, c):
                n = i * PER_PAIR + (b * BJ + c)
                if past_zero(n - 1):
                    eng.wait_ge(s["z_read"], n - 1)
                product(i, BASE[f"U{b}"] + c, B[4 + c % 2][:, 0:T], hh, hl)

            def u_block(b):
                def body(i):
                    for c in range(PER_PAIR):
                        if b == 0 and c < 2 and isinstance(i, int):
                            eng.wait_ge(s["sc_ready"], PEER_HEADS - 1 + c)
                        if b >= 1:
                            spread(b - 1, i, c)
                        dots(b, i, c)
                body(0)
                with eng.Fori(1, BJ // PER_PAIR) as i:
                    body(i)

            def final_sums(first, end):
                for g in range(first, end):
                    eng.wait_ge(s["zsq_ready"], g + 1)
                    for c in range(2):
                        last = eng.matmul(B[4][:, 0:T], ones[:, :], zsq[:, g, c * T:(c + 1) * T],
                                          start=(g == 0 and c == 0), stop=(g == FH - 1 and c == 1))
                    last.then_inc(s["zss_done"], 1)

            def v_block(b):
                def half(f):
                    for c in range(BJ // 2):
                        k0_ = BASE[f"V{b}"] + c
                        if b == BLOCKS - 2:
                            spread(BLOCKS - 1, f * 2, c)
                        eng.wait_ge(s["al_ready"], f * (BJ // 2) + (b * BJ + c + 1))
                        for j in range(2):
                            eng.wait_ge(lo_ready, unit(f * 2, k0_, 2, j + 1))
                            for k in range(FH):
                                if c == 0 and j == 0 and k % 2 == 0 and past_zero(f * 4 + (8 * b - 4 + k // 2 + 1)):
                                    eng.wait_ge(s["x_added"], f * 4 + (8 * b - 4 + k // 2 + 1))
                                o = B[k // 2][:, (k % 2) * T:(k % 2 + 1) * T]
                                h_, l_ = wh[k0_ % 2][:, j * FH + k, :], wl[k0_ % 2][:, j * FH + k, :]
                                final = c == BJ // 2 - 1 and j == 1
                                eng.matmul(o, h_, ah[c % 2][:, j, :], start=(c == 0 and j == 0 and k % 2 == 0), stop=False,
                                           skip_group_check=True)
                                eng.matmul(o, h_, al[c % 2][:, j, :], start=False, stop=False, skip_group_check=True)
                                last = eng.matmul(o, l_, ah[c % 2][:, j, :], start=False, stop=final, skip_group_check=True)
                            last.then_inc(mm_done, 1)
                        if b == BLOCKS - 1 and f == 1 and c == PER_PAIR:
                            final_sums(0, FH // 2)

                if b in (0, BLOCKS - 1):
                    half(0)
                    half(1)
                else:
                    with eng.Fori(0, 2) as f:
                        half(f)

            u_block(0)
            eng.wait_ge(s["routed"], 1)
            for t in range(NT):
                for n in range(2):
                    eng.transpose(B[6 + t][:, n * P:(n + 1) * P], place[:, t, n, :], ident[:, :])
                last = eng.transpose(B[6 + t][:, 2 * P:3 * P], tops[:, t].rearrange("p h k -> p (h k)"), ident[:, :])
            last.then_inc(s["rt_done"], 1)
            eng.wait_ge(s["slots_ready"], 1)
            u_block(1)
            v_block(0)
            u_block(2)
            v_block(1)
            u_block(3)
            v_block(2)
            v_block(3)
            final_sums(FH // 2, FH)

        @block.scalar
        def _(eng):
            def rsqrt(out, src, scale):
                eng.activation(out, src, ACT.Ln, bias=eps[0:out.shape[0], 0:1], scale=scale)
                eng.drain()
                return eng.activation(out, out, ACT.Exp, scale=-0.5)

            def high_part(i, c):
                eng.wait_ge(w_loaded[c % RAW], i * (PER_PAIR // RAW * 16) + (c // RAW + 1) * 16)
                for half in range(2):
                    k = slice(half * KC // 2, (half + 1) * KC // 2)
                    if past_zero(unit(i, c, 2, half - 3)):
                        eng.wait_ge(mm_done, unit(i, c, 2, half - 3))
                    eng.activation(wh[c % 2][:, k, :], raw[:, c % RAW, :].rearrange("p (k n) -> p k n", k=KC)[:, k, :],
                                   ACT.Copy).then_inc(hi_ready, 1)

            def square_chunks(name, g):
                n = 8 * NORM_AT[name]
                if name != "A":
                    eng.wait_ge(x_ready, n - 8 + g + 1)
                if past_zero(g - 1):
                    eng.wait_ge(ss_done, n + g - 1)
                eng.activation(sq[:, g % 2, :], chunk(xT, 2 * g, 2), ACT.Square).then_inc(sq_ready, 1)

            def stream_norm(name, outs):
                eng.wait_ge(ss_done, 8 * (NORM_AT[name] + 1))
                rsqrt(rstd[:, :], B[4][:, 0:T], 1.0 / D).then_inc(rstd_ready, 1)
                for n, dst in enumerate(outs):
                    for g in range(KC // 2):
                        if n == 1 and g == 6:
                            high_part(0, BASE["FG"] + 2)
                        eng.wait_ge(hf_ready, SPLIT_AT[name] + 8 * n + g + 1)
                        eng.activation(chunk(dst, 2 * g, 2), chunk(oT, 2 * g, 2), ACT.Copy).then_inc(hh_ready, 1)

            def outputs_high(name, first, count):
                eng.wait_ge(mm_done, 2 * (BASE[name] + 64))
                for c in range(first, first + count):
                    eng.wait_ge(mixed, MIX_AT[name] + c + 1)
                    eng.activation(chunk(hh, 2 * c, 2), chunk(oT, 2 * c, 2), ACT.Copy).then_inc(oh_ready, 1)

            def after(stage, i, c):
                return unit(i, BASE[stage] + c, 2, 2)

            def out_stage(stage, name):
                for g in range(KC // 2):
                    high_part(0, BASE[stage] + 2 * g + 2)
                    high_part(0, BASE[stage] + 2 * g + 3)
                    square_chunks(name, g)

            def pair_loop(body):
                body(0, True)
                with eng.Fori(1, PAIRS) as i:
                    body(i, False)

            eng.wait_ge(consts_ready, 1)
            for g in range(KC // 2):
                eng.wait_ge(x_in[g // 2], 16)
                square_chunks("A", g)
            eng.wait_ge(lb_e_ready, 1)
            eng.activation(sp[:, 1, :], sp[:, 0, :], ACT.Exp).then_inc(lb_e_ready, 1)
            eng.wait_ge(lam_e_ready, 1)
            eng.activation(sp[:, 5, :], sp[:, 4, :], ACT.Exp, scale=-1.0).then_inc(lam_e_ready, 1)
            eng.wait_ge(lam_w_ready, 1)
            eng.activation(sp[:, 7, :], sp[:, 6, :], ACT.Ln).then_inc(lam_l_ready, 1)
            high_part(0, 0)
            high_part(0, 1)
            stream_norm("A", [hh])

            def keep_values(s, i):
                eng.activation(vf[:, :, :].rearrange("p j t -> p (j t)"), B[2][:, :], ACT.Copy).then_inc(s["vf_ready"], 1)

            def keep_values_tok(s, i, v):
                if past_zero(i):
                    eng.wait_ge(s["o_done"], i)
                eng.wait_ge(s["vt_done"], i + 1)
                eng.activation(v[:, :, :].rearrange("p t g -> p (t g)"), B[2][:, :], ACT.Copy).then_inc(s["v_ready"], 1)

            s = sA

            def a_body(i, first):
                high_part(i, 2)
                eng.wait_ge(mm_done, after("A", i, 1))
                if past_zero(i):
                    eng.wait_ge(s["f_ready"], i)
                eng.activation(f0[:, :], B[0][:, :], ACT.Sigmoid)
                eng.activation(k0[:, :], B[0][:, :], ACT.Sigmoid, scale=-1.0).then_inc(s["fz_read"], 1)
                high_part(i, 3)
                if not first:
                    eng.wait_ge(s["o_done"], i)
                    eng.activation(osq_a[:, :], B[4][:, :], ACT.Square).then_inc(s["osq_ready"], 1)
                high_part(i, 4)
                eng.wait_ge(mm_done, after("A", i, 3))
                if past_zero(i):
                    eng.wait_ge(s["lv_done"], i)
                eng.activation(q_a[:, :], B[1][:, :], ACT.Copy).then_inc(s["qz_ready"], 1)
                high_part(i, 5)
                if not first:
                    a_rstd(i - 1)
                high_part(i, 6)
                eng.wait_ge(mm_done, after("A", i, 5))
                keep_values(s, i)
                high_part(i, 7)
                high_part(i, 8)
                eng.wait_ge(mm_done, after("A", i, 7))
                if past_zero(i):
                    eng.wait_ge(s["gate_read"], i)
                eng.activation(sig_a[:, :], B[3][:, :], ACT.Sigmoid).then_inc(s["sig_ready"], 1)
                keep_values_tok(s, i, v_a)
                high_part(i, 9)

            def a_rstd(i):
                eng.wait_ge(s["oss_done"], i + 1)
                if past_zero(i):
                    eng.wait_ge(s["o_read"], i)
                rsqrt(ors_a[:, :], B[5][:, :], 1.0 / P).then_inc(s["ors_ready"], 1)

            pair_loop(a_body)
            outputs_high("A", 0, PAIRS - 1)
            eng.wait_ge(s["o_done"], PAIRS)
            eng.activation(osq_a[:, :], B[4][:, :], ACT.Square).then_inc(s["osq_ready"], 1)
            a_rstd(PAIRS - 1)
            outputs_high("A", PAIRS - 1, 1)
            out_stage("OA", "F")
            stream_norm("F", [kh, hh])

            s = sF
            eng.wait_ge(s["z_ready"], 1)
            eng.activation(fz[2], fz[1], ACT.Exp, scale=-1.0)
            eng.drain()
            eng.activation(fz[3], fz[2], ACT.Ln, bias=ones[0:HEADS, 0:1]).then_inc(s["l_ready"], 1)

            def softmax_exp(s, i, prob, nmax, rsum):
                eng.wait_ge(s["nmax_ready"], i + 1)
                for j in range(2):
                    for t in range(NT):
                        p = prob[:, j, t * P:t * P + (t + 1) * P]
                        last = eng.activation(p, p, ACT.Exp, bias=nmax[:, 2 * j + t:2 * j + t + 1],
                                              accum_out=rsum[:, 2 * j + t:2 * j + t + 1])
                last.then_inc(s["e_done"], 1)

            def copy_probs(s, i, probT):
                if past_zero(i):
                    eng.wait_ge(s["o_done"], i)
                for j in range(2):
                    eng.wait_ge(s["pt_done"], i * 2 + j + 1)
                    last = eng.activation(probT[:, j, :], B[6 + j][:, 0:SC], ACT.Copy)
                last.then_inc(s["pt_ready"], 1)

            def f_square_out(i):
                eng.wait_ge(s["o_done"], i + 1)
                eng.activation(osq_f[:, :], B[5][:, :], ACT.Square).then_inc(s["osq_ready"], 1)

            def f_rstd_out(i):
                eng.wait_ge(s["oss_done"], i + 1)
                if past_zero(i):
                    eng.wait_ge(s["o_read"], i)
                rsqrt(ors_f[:, :], B[6][:, :], 1.0 / P).then_inc(s["ors_ready"], 1)

            def f_body(i, first):
                u = BASE["F"]
                high_part(i, u + 2)
                eng.wait_ge(mm_done, after("F", i, 1))
                eng.activation(ksq[:, :], B[0][:, :], ACT.Square).then_inc(s["ksq_ready"], 1)
                high_part(i, u + 3)
                if not first:
                    copy_probs(s, i - 1, probT_f)
                high_part(i, u + 4)
                eng.wait_ge(mm_done, after("F", i, 3))
                eng.activation(qsq[:, :], B[1][:, :], ACT.Square).then_inc(s["qsq_ready"], 1)
                eng.wait_ge(s["kss_done"], i + 1)
                if past_zero(i):
                    eng.wait_ge(s["kn_ready"], i)
                rsqrt(krs[:, :], B[4][:, :], 1.0 / P).then_inc(s["krs_ready"], 1)
                high_part(i, u + 5)
                if not first:
                    f_square_out(i - 1)
                high_part(i, u + 6)
                eng.wait_ge(mm_done, after("F", i, 5))
                keep_values(s, i)
                high_part(i, u + 7)
                eng.wait_ge(s["qss_done"], i + 1)
                if past_zero(i):
                    eng.wait_ge(s["qn_ready"], i)
                rsqrt(qrs[:, :], B[4][:, :], 1.0 / P).then_inc(s["qrs_ready"], 1)
                if not first:
                    f_rstd_out(i - 1)
                high_part(i, u + 8)
                eng.wait_ge(mm_done, after("F", i, 7))
                if past_zero(i):
                    eng.wait_ge(s["gate_read"], i)
                eng.activation(sig_f[:, :], B[3][:, :], ACT.Sigmoid).then_inc(s["sig_ready"], 1)
                keep_values_tok(s, i, v_f)
                high_part(i, u + 9)
                softmax_exp(s, i, prob_f, nmax_f, rsum_f)

            pair_loop(f_body)
            copy_probs(s, PAIRS - 1, probT_f)
            outputs_high("F", 0, PAIRS - 1)
            f_square_out(PAIRS - 1)
            f_rstd_out(PAIRS - 1)
            outputs_high("F", PAIRS - 1, 1)
            out_stage("OF", "C")
            stream_norm("C", [hh])

            s = sX
            u = BASE["X"]
            for n in range(2):
                high_part(0, u + 2 * n + 2)
                eng.wait_ge(mm_done, 2 * (u + 2 * n + 2))
                eng.activation(csq[:, 2 * n:2 * n + 2, :].rearrange("p c t -> p (c t)"), B[n][:, :], ACT.Square)
                high_part(0, u + 2 * n + 3)
            eng.drain().then_inc(s["csq_ready"], 1)
            high_part(0, u + 6)
            eng.wait_ge(mm_done, 2 * (u + RC + 1))
            eng.activation(kw_fm, B[2][:, 0:T], ACT.Copy).then_inc(s["kwf_ready"], 1)
            eng.wait_ge(s["kwt_done"], 1)
            eng.activation(kw[:, :, :], B[5][:, 0:NT * P].rearrange("p (t n) -> p t n", t=NT)[:, :, 0:IDX_DIM + IDX_HEADS],
                           ACT.Copy).then_inc(s["kw_ready"], 1)
            eng.wait_ge(s["css_done"], 1)
            rsqrt(crs[:, :], B[4][:, 0:T], 1.0 / KV_RANK).then_inc(s["crs_ready"], 1)
            eng.wait_ge(s["kc_ready"], 1)
            for t in range(NT):
                eng.activation(kdup[:, t, 0, :], kc[:, t, :], ACT.Square, accum_out=kst[:, 1, t:t + 1])
            eng.drain()
            rsqrt(kst[:, 2, :], kst[:, 1, :], 1.0 / IDX_DIM).then_inc(s["krs_ready"], 1)

            def index_relu(g):
                for q in range(4):
                    n = 4 * g + q
                    eng.wait_ge(s["rel_done"], n + 1)
                    if past_zero(n - 3):
                        eng.wait_ge(s["relu_used"], n - 3)
                    eng.activation(relu[:, n % 4, :], B[6 + n % 2][:, 0:SC], ACT.Relu).then_inc(s["relu_ready"], 1)

            for g in range(4):
                high_part(0, u + RC + 1 + 2 * g + 2)
                high_part(0, u + RC + 1 + 2 * g + 3)
                eng.wait_ge(mm_done, 2 * (u + RC + 1 + 2 * g + 2))
                eng.activation(qi[:, g % 2, :], B[3 if g % 2 == 0 else 0][:, :], ACT.Copy,
                               scale=float(IDX_DIM) ** -0.5).then_inc(s["qi_ready"], 1)
                if g >= 1:
                    index_relu(g - 1)
            index_relu(3)

            s = sC

            def c_body(i, first):
                u = BASE["C"]
                high_part(i, u + 2)
                if not first:
                    copy_probs(s, i - 1, probT_c)
                high_part(i, u + 3)
                high_part(i, u + 4)
                eng.wait_ge(mm_done, after("C", i, 3))
                if past_zero(i):
                    eng.wait_ge(s["s_done"], i * 2)
                eng.activation(qT_c[:, :, :].rearrange("p h t -> p (h t)"), B[1][:, :], ACT.Copy,
                               scale=HD_SCALE).then_inc(s["q_ready"], 1)
                eng.wait_ge(s["rg_done"], i + 1)
                if past_zero(i):
                    eng.wait_ge(s["mix_ready"], i)
                for n, b in enumerate(("ba", "bx")):
                    for j in range(2):
                        last = eng.activation(rg[:, n, j, :], B[4 + n][:, j * T:(j + 1) * T], ACT.Sigmoid,
                                              bias=col(b, i * 2 + j))
                last.then_inc(s["ri_read"], 1)
                high_part(i, u + 5)
                eng.wait_ge(s["la_ready"], i + 1)
                eng.activation(ae[:, 0, :], la[:, :], ACT.Exp)
                eng.activation(ae[:, 1, :], la[:, :], ACT.Exp, scale=2.0)
                eng.activation(ae[:, 2, :], la[:, :], ACT.Tanh, scale=-1.0).then_inc(s["ex_ready"], 1)
                high_part(i, u + 6)
                eng.wait_ge(s["prod_ready"], i + 1)
                eng.activation(ub[:, 0, :], ub[:, 0, :], ACT.Sqrt).then_inc(s["root_ready"], 1)
                eng.wait_ge(mm_done, after("C", i, 5))
                eng.activation(rsig[:, :], B[2][:, :], ACT.Sigmoid).then_inc(s["rsig_ready"], 1)
                high_part(i, u + 7)
                eng.wait_ge(s["kv_done"], i * 2 + 1)
                eng.activation(kT_c[:, :, :].rearrange("p h t -> p (h t)"), B[4][:, :], ACT.Copy).then_inc(s["kT_ready"], 1)
                eng.wait_ge(s["kv_done"], i * 2 + 2)
                if past_zero(i):
                    eng.wait_ge(s["o_done"], i)
                eng.activation(v_c[:, :, :].rearrange("p t g -> p (t g)"), B[5][:, :], ACT.Copy).then_inc(s["v_ready"], 1)
                high_part(i, u + 8)
                eng.wait_ge(mm_done, after("C", i, 7))
                if past_zero(i):
                    eng.wait_ge(s["o_read"], i)
                eng.activation(asig[:, :], B[3][:, :], ACT.Sigmoid).then_inc(s["asig_ready"], 1)
                high_part(i, u + 9)
                softmax_exp(s, i, prob_c, nmax_c, rsum_c)

            pair_loop(c_body)
            copy_probs(s, PAIRS - 1, probT_c)
            outputs_high("C", 0, PAIRS)
            out_stage("OC", "Q")
            stream_norm("Q", [hh])

            s = sQ
            eng.wait_ge(s["kt_done"], 1)
            eng.activation(keysT[:, :, :].rearrange("p n k -> p (n k)"), B[6][:, 0:2 * P], ACT.Copy).then_inc(s["kt_ready"], 1)

            def evacuate(g):
                high_part(0, BASE["Q"] + 2 * g + 2)
                high_part(0, BASE["Q"] + 2 * g + 3)
                eng.wait_ge(mm_done, 2 * (BASE["Q"] + 2 * g + 2))
                if past_zero(g - 1):
                    eng.wait_ge(s["sc_done"], g - 1)
                eng.activation(qp[:, g % 2, :, :].rearrange("p n t -> p (n t)"), B[g % 4][:, :], ACT.Copy).then_inc(s["qp_ready"], 1)

            def keep_scores(g):
                eng.wait_ge(s["sc_done"], g + 1)
                eng.activation(S12[:, :, g, :], B[4 + g % 2][:, :].rearrange("p (t n) -> p t n", t=NT), ACT.Copy).then_inc(s["sc_ready"], 1)

            for g in range(PEER_HEADS):
                evacuate(g)
                if g >= 1:
                    keep_scores(g - 1)
            keep_scores(PEER_HEADS - 1)

            def gate_exp(tile):
                eng.wait_ge(s["sub_ready"], tile + 1)
                t_ = tops[:, tile].rearrange("p h k -> p (h k)")
                eng.activation(t_, t_, ACT.Exp).then_inc(s["gexp_ready"], 1)

            def gelus(b, i):
                for c in range(PER_PAIR):
                    high_part(i, BASE[f"U{b}"] + c + 2)
                    eng.wait_ge(mm_done, unit(i, BASE[f"U{b}"] + c, 2, 2))
                    eng.activation(acts[b % 2][:, ds(i * PER_PAIR + c, 1), :].rearrange("p o t -> p (o t)"),
                                   B[4 + c % 2][:, 0:T], ACT.Gelu).then_inc(s["z_read"], 1)

            def act_high(b, f, c):
                eng.wait_ge(mm_done, unit(f * 2, BASE[f"V{b}"] + c, 2, -2))
                eng.activation(ah[c % 2][:, :, :], acts[b % 2][:, 2 * c:2 * c + 2, :], ACT.Copy).then_inc(s["ah_ready"], 1)

            def final_squares(first, end):
                for g in range(first, end):
                    eng.wait_ge(s["x_added"], 8 * BLOCKS - 8 + g + 1)
                    eng.activation(zsq[:, g, :], chunk(xT, 2 * g, 2), ACT.Square).then_inc(s["zsq_ready"], 1)

            def v_highs(b):
                eng.wait_ge(s["gated"], (b + 1) * BJ)

                def half(f, highs):
                    act_high(b, f, 0)
                    act_high(b, f, 1)
                    for c in range(BJ // 2):
                        if c < highs:
                            high_part(f * 2, BASE[f"V{b}"] + c + 2)
                        if c < BJ // 2 - 2:
                            act_high(b, f, c + 2)
                        if b == BLOCKS - 1 and highs < BJ // 2 and c == 4:
                            final_squares(0, FH // 2)

                if b < BLOCKS - 1:
                    with eng.Fori(0, 2) as f:
                        half(f, BJ // 2)
                else:
                    half(0, BJ // 2)
                    half(1, BJ // 2 - 2)

            with eng.Fori(0, 3) as i:
                gelus(0, i)
            gate_exp(0)
            gate_exp(1)
            gelus(0, 3)
            for name, b in PEER_ORDER[1:]:
                if name == "U":
                    with eng.Fori(0, BJ // PER_PAIR) as i:
                        gelus(b, i)
                else:
                    v_highs(b)
            final_squares(FH // 2, FH)
            eng.wait_ge(s["zss_done"], FH)
            rsqrt(rstd[:, :], B[4][:, 0:T], 1.0 / D).then_inc(s["zrs_ready"], 1)

        @block.vector
        def _(eng):
            def stream_norm(name, outs):
                eng.wait_ge(rstd_ready, NORM_AT[name] + 1)
                for n, (dst, high, weight) in enumerate(outs):
                    for g in range(KC // 2 + 1):
                        if g < KC // 2:
                            for c in (2 * g, 2 * g + 1):
                                last = eng.scalar_tensor_tensor(out=oT[:, c, :], in0=xT[:, c, :], scalar=col(weight, c),
                                                                in1=rstd[:, :], op0=ALU.mult, op1=ALU.mult)
                            last.then_inc(hf_ready, 1)
                        if g >= 1:
                            eng.wait_ge(hh_ready, SPLIT_AT[name] + 8 * n + g)
                            eng.tensor_tensor(chunk(dst, 2 * g - 2, 2), chunk(oT, 2 * g - 2, 2),
                                              chunk(high, 2 * g - 2, 2).bitcast(F32), ALU.subtract).then_inc(hl_ready, 1)
                    eng.drain()

            def outputs_low(name, first, count):
                for c in range(first, first + count):
                    eng.wait_ge(oh_ready, MIX_AT[name] + c + 1)
                    eng.tensor_tensor(chunk(hl, 2 * c, 2), chunk(oT, 2 * c, 2), chunk(hh, 2 * c, 2).bitcast(F32),
                                      ALU.subtract).then_inc(ol_ready, 1)

            def add_to_stream(stage, name):
                for g in range(KC // 2):
                    eng.wait_ge(mm_done, 2 * (BASE[stage] + 2 * g + 2))
                    eng.tensor_tensor(chunk(xT, 2 * g, 2), B[g % 4][:, :], chunk(xT, 2 * g, 2), ALU.add).then_inc(x_ready, 1)

            def pair_loop(body):
                body(0, True)
                with eng.Fori(1, PAIRS) as i:
                    body(i, False)

            eng.wait_ge(params_in, 16)
            lbl = prm[:, PRM["a_lb"]:PRM["a_lb"] + KC]
            eng.tensor_tensor(sp[:, 0, :], lbl, lbl, ALU.subtract).then_inc(lb_e_ready, 1)
            lam = prm[:, PRM["lam"]:PRM["lam"] + KC]
            eng.tensor_scalar(sp[:, 3, :], lam, -1.0, 0.0, ALU.mult, ALU.max)
            eng.drain()
            eng.scalar_tensor_tensor(out=sp[:, 4, :], in0=sp[:, 3, :], scalar=2.0, in1=lam, op0=ALU.mult,
                                     op1=ALU.add).then_inc(lam_e_ready, 1)
            eng.tensor_scalar(qw[:, :], prm[:, PRM["q_norm"]:PRM["q_norm"] + 1], HD_SCALE, None, ALU.mult)
            for n in range(1, LEVELS + 1):
                eng.memset(KL[n][:, :], 0.0)
            for c in range(4):
                eng.wait_ge(x_in[c], 16)
            eng.wait_ge(lb_e_ready, 2)
            eng.reciprocal(sp[:, 2, :], sp[:, 1, :])
            eng.drain()
            eng.tensor_tensor(sp[:, 0, :], sp[:, 1, :], sp[:, 2, :], ALU.mult)
            eng.drain()
            eng.tensor_tensor(lb[:, :], sp[:, 0, :], sp[:, 0, :], ALU.subtract)
            eng.drain()
            eng.tensor_scalar(omlb[:, :], lb[:, :], -1.0, 1.0, ALU.mult, ALU.add)
            eng.wait_ge(lam_e_ready, 2)
            eng.tensor_scalar(sp[:, 6, :], sp[:, 5, :], 1.0, None, ALU.add)
            eng.drain().then_inc(lam_w_ready, 1)
            eng.tensor_scalar(sp[:, 0, :], sp[:, 6, :], 1.0, None, ALU.is_equal)
            eng.drain()
            eng.scalar_tensor_tensor(out=sp[:, 1, :], in0=sp[:, 6, :], scalar=-1.0, in1=sp[:, 0, :], op0=ALU.add, op1=ALU.add)
            eng.drain()
            eng.reciprocal(sp[:, 2, :], sp[:, 1, :])
            eng.wait_ge(lam_l_ready, 1)
            eng.drain()
            eng.tensor_tensor(sp[:, 1, :], sp[:, 7, :], sp[:, 2, :], ALU.mult)
            eng.drain()
            eng.tensor_tensor(sp[:, 1, :], sp[:, 1, :], sp[:, 0, :], ALU.add)
            eng.drain()
            eng.tensor_tensor(sp[:, 1, :], sp[:, 1, :], sp[:, 5, :], ALU.mult)
            eng.drain()
            eng.tensor_tensor(sp[:, 1, :], sp[:, 1, :], sp[:, 3, :], ALU.add)
            eng.drain()
            eng.tensor_scalar(rg_c[:, :], sp[:, 1, :], -RG_C, None, ALU.mult)
            stream_norm("A", [(hl, hh, "a_norm")])

            s = sA
            eng.wait_ge(consts_ready, 1)

            def decays(i):
                eng.wait_ge(s["fz_read"], i + 1)
                if past_zero(i):
                    eng.wait_ge(s["lv_done"], i)
                for j in range(2):
                    a = slice(j * T, (j + 1) * T)
                    eng.tensor_scalar(TL[0][:, a], f0[:, a], omlb[:, ds(i * 2 + j, 1)], lb[:, ds(i * 2 + j, 1)], ALU.mult, ALU.add)
                    eng.tensor_scalar(KL[0][:, a], k0[:, a], omlb[:, ds(i * 2 + j, 1)], None, ALU.mult)
                eng.drain()
                eng.wait_ge(s["qz_ready"], i + 1)
                eng.tensor_tensor(QL[0][:, :], q_a[:, :], TL[0][:, :], ALU.mult)
                eng.drain()
                for l in range(LEVELS):
                    h = 1 << l
                    seg = TL[l][:, :].rearrange("p (b two) -> p b two", two=2)
                    q0, q1 = halves(QL[l][:, :], h), halves(QL[l + 1][:, :], h)
                    k0_, k1_ = halves(KL[l][:, :], h), halves(KL[l + 1][:, :], h)
                    eng.tensor_tensor(q1[:, :, 1, :], q0[:, :, 1, :], over(seg[:, :, 0], h), ALU.mult)
                    eng.tensor_tensor(k1_[:, :, 0, :], k0_[:, :, 0, :], over(seg[:, :, 1], h), ALU.mult)
                    eng.tensor_copy(q1[:, :, 0, :], q0[:, :, 0, :])
                    last = eng.tensor_copy(k1_[:, :, 1, :], k0_[:, :, 1, :])
                    if l < LEVELS - 1:
                        eng.tensor_tensor(TL[l + 1][:, :], seg[:, :, 0], seg[:, :, 1], ALU.mult)
                        eng.drain()
                    else:
                        last.then_inc(s["f_ready"], 1)

            def gated_out(s, i, bank, ors, on, gate, weight, name):
                eng.wait_ge(s["ors_ready"], i + 1)
                eng.tensor_tensor(on[:, :], B[bank][:, :], ors[:, :], ALU.mult).then_inc(s["o_read"], 1)
                eng.drain()
                for j in range(2):
                    a = slice(j * T, (j + 1) * T)
                    last = eng.scalar_tensor_tensor(out=chunk(oT, i * 2 + j), in0=on[:, a], scalar=col(weight, i * 2 + j),
                                                    in1=gate[:, a], op0=ALU.mult, op1=ALU.mult)
                last.then_inc(mixed, 1)
                eng.drain()

            def a_masks(i):
                if past_zero(i):
                    eng.wait_ge(s["o_done"], i)
                eng.wait_ge(s["lv_done"], i + 1)
                eng.tensor_tensor(AT[:, :, :], B[4][:, :].rearrange("p (n t) -> p n t", n=2 * NT),
                                  ident[:, :].unsqueeze(1).broadcast_to([P, 2 * NT, P]), ALU.mult)
                eng.drain()
                for l in range(LEVELS):
                    h, nb = 1 << l, P >> (l + 1)
                    bank, at = (B[5 + l // 2], (l % 2) * T) if l < 6 else (B[3], 0)
                    dst = AT[:, :, :].rearrange("p n (b two r) -> p n b two r", two=2, r=h)[:, :, :, 1, :]
                    mask = lmask[:, l, :].bitcast(U32).rearrange("p (b r) -> p b r", r=h)
                    for n in range(2 * NT):
                        eng.copy_predicated(dst[:, n], mask, bank[:, at + n * (P // 2):at + (n + 1) * (P // 2)]
                                            .rearrange("p (b r) -> p b r", r=h))
                    eng.drain()
                eng.tensor_copy(AToff[:, :, :], B[3][:, T:2 * T].rearrange("p (j t) -> p j t", j=2))
                eng.drain().then_inc(s["at_ready"], 1)

            def a_body(i, first):
                decays(i)
                if not first:
                    gated_out(s, i - 1, 4, ors_a, on_a, gate_a, "a_onorm", "A")
                eng.wait_ge(s["sig_ready"], i + 1)
                eng.tensor_tensor(gate_a[:, :], B[3][:, :], sig_a[:, :], ALU.mult).then_inc(s["gate_read"], 1)
                a_masks(i)

            pair_loop(a_body)
            outputs_low("A", 0, PAIRS - 1)
            gated_out(s, PAIRS - 1, 4, ors_a, on_a, gate_a, "a_onorm", "A")
            outputs_low("A", PAIRS - 1, 1)
            add_to_stream("OA", "F")
            stream_norm("F", [(kl, kh, "kv_norm"), (hl, hh, "b_norm")])

            s = sF
            eng.memset(fcum[:, :], 0.0)
            eng.memset(fneg[:, :], 0.0)
            eng.wait_ge(bias_in, 16)
            eng.wait_ge(mm_done, 2 * (BASE["FG"] + 1))
            eng.tensor_scalar(fz[0], B[5][0:HEADS, 0:T], fbias[:, 0:1], None, ALU.add)
            eng.drain()
            eng.tensor_scalar(fz[4], fz[0], 0.0, None, ALU.min)
            eng.drain()
            eng.scalar_tensor_tensor(out=fz[1], in0=fz[4], scalar=-2.0, in1=fz[0], op0=ALU.mult,
                                     op1=ALU.add).then_inc(s["z_ready"], 1)
            eng.wait_ge(s["l_ready"], 1)
            eng.tensor_tensor(fz[0], fz[4], fz[3], ALU.subtract)
            eng.drain()
            eng.tensor_tensor_scan(out=fcum[0:HEADS, :], data0=ones[0:HEADS, 0:1].broadcast_to([HEADS, T]), data1=fz[0],
                                   initial=0.0, op0=ALU.mult, op1=ALU.add)
            eng.drain()
            eng.tensor_scalar(fneg[0:HEADS, :], fcum[0:HEADS, :], -1.0, None, ALU.mult)
            eng.drain()

            def softmax_scores(s, i, prob, nmax, rsum, rinv, mask):
                if past_zero(i * 2):
                    eng.wait_ge(s["pt_done"], i * 2)
                for j in range(2):
                    eng.wait_ge(s["s_done"], i * 2 + j + 1)
                    eng.tensor_tensor(prob[:, j, :], B[6 + j][:, 0:SC], mask[:, :], ALU.add)
                eng.drain()
                for j in range(2):
                    for t in range(NT):
                        last = eng.tensor_reduce(nmax[:, 2 * j + t:2 * j + t + 1], prob[:, j, t * P:t * P + (t + 1) * P],
                                                 AX.X, ALU.max, negate=True)
                last.then_inc(s["nmax_ready"], 1)
                eng.wait_ge(s["e_done"], i + 1)
                eng.reciprocal(rinv[:, :], rsum[:, :])
                eng.drain()
                for j in range(2):
                    for t in range(NT):
                        p = prob[:, j, t * P:t * P + (t + 1) * P]
                        last = eng.tensor_scalar(p, p, rinv[:, 2 * j + t:2 * j + t + 1], None, ALU.mult)
                last.then_inc(s["p_ready"], 1)

            def f_body(i, first):
                if past_zero(i * 2):
                    eng.wait_ge(s["s_done"], i * 2)
                for j in range(2):
                    eng.tensor_scalar(selF[:, j, :], fneg[:, :], ident[:, ds(i * 2 + j, 1)], None, ALU.mult)
                    last = eng.tensor_copy(selO[:, j, :], ident[:, ds(i * 2 + j, 1)].broadcast_to([P, T]))
                last.then_inc(s["sel_ready"], 1)
                eng.wait_ge(s["krs_ready"], i + 1)
                eng.scalar_tensor_tensor(out=kT_f[:, :, :].rearrange("p h t -> p (h t)"), in0=B[0][:, :],
                                         scalar=col("k_norm", 0), in1=krs[:, :], op0=ALU.mult, op1=ALU.mult).then_inc(s["kn_ready"], 1)
                eng.wait_ge(s["qrs_ready"], i + 1)
                eng.scalar_tensor_tensor(out=qT_f[:, :, :].rearrange("p h t -> p (h t)"), in0=B[1][:, :], scalar=qw[:, 0:1],
                                         in1=qrs[:, :], op0=ALU.mult, op1=ALU.mult).then_inc(s["qn_ready"], 1)
                if not first:
                    gated_out(s, i - 1, 5, ors_f, on_f, gate_f, "b_onorm", "F")
                eng.wait_ge(s["sig_ready"], i + 1)
                eng.tensor_tensor(gate_f[:, :], B[3][:, :], sig_f[:, :], ALU.mult).then_inc(s["gate_read"], 1)
                softmax_scores(s, i, prob_f, nmax_f, rsum_f, rinv_f, tri)

            pair_loop(f_body)
            outputs_low("F", 0, PAIRS - 1)
            gated_out(s, PAIRS - 1, 5, ors_f, on_f, gate_f, "b_onorm", "F")
            outputs_low("F", PAIRS - 1, 1)
            add_to_stream("OF", "C")
            stream_norm("C", [(hl, hh, "mix")])

            s = sX
            eng.wait_ge(s["kw_ready"], 1)
            for t in range(NT):
                eng.tensor_reduce(kst[:, 0, t:t + 1], kw[:, t, 0:IDX_DIM], AX.X, ALU.add)
            eng.drain()
            eng.tensor_scalar(kst[:, 3, :], kst[:, 0, :], -1.0 / IDX_DIM, None, ALU.mult)
            eng.drain()
            for t in range(NT):
                eng.tensor_scalar(kc[:, t, :], kw[:, t, 0:IDX_DIM], kst[:, 3, t:t + 1], None, ALU.add)
                eng.tensor_scalar(kw[:, t, IDX_DIM:], kw[:, t, IDX_DIM:], float(IDX_HEADS) ** -0.5, None, ALU.mult)
            eng.drain().then_inc(s["kc_ready"], 1)
            eng.wait_ge(s["crs_ready"], 1)
            for c in range(RC):
                last = eng.scalar_tensor_tensor(out=ckvT[:, c, :], in0=B[c // 2][:, (c % 2) * T:(c % 2 + 1) * T],
                                                scalar=col("ckv", c), in1=crs[:, :], op0=ALU.mult, op1=ALU.mult)
                if c == 1:
                    last.then_inc(s["ckv_read"], 1)
            last.then_inc(s["ckv_ready"], 1)
            eng.wait_ge(s["krs_ready"], 1)
            for t in range(NT):
                for a in range(2):
                    last = eng.tensor_scalar(kdup[:, t, a, :], kc[:, t, :], kst[:, 2, t:t + 1], None, ALU.mult)
            last.then_inc(s["kn_ready"], 1)
            eng.memset(iscore[:, :], 0.0)
            eng.wait_ge(s["kt_done"], 1)
            eng.tensor_scalar(kiT[:, :], B[5][:, 0:T], col("idx_g", 0), col("idx_b", 0), ALU.mult, ALU.add).then_inc(s["kt_ready"], 1)
            for n in range(IDX_HEADS):
                eng.wait_ge(s["relu_ready"], n + 1)
                eng.drain()
                for t in range(NT):
                    a = slice(t * P, t * P + (t + 1) * P)
                    last = eng.scalar_tensor_tensor(out=iscore[:, a], in0=relu[:, n % 4, a], scalar=kw[:, t, IDX_DIM + n:IDX_DIM + n + 1],
                                                    in1=iscore[:, a], op0=ALU.mult, op1=ALU.add)
                last.then_inc(s["relu_used"], 1)
            eng.drain()
            eng.tensor_tensor(iscore[:, :], iscore[:, :], tri[:, :], ALU.add)
            eng.drain()
            with eng.Fori(0, TOPK // 8) as _:
                for t in range(NT):
                    eng.max(top8[:, t, :], iscore[:, t * P:t * P + (t + 1) * P])
                eng.drain()
                for t in range(NT):
                    a = slice(t * P, t * P + (t + 1) * P)
                    eng.match_replace(iscore[:, a], top8[:, t, :], iscore[:, a], TAKEN)
                eng.drain()
            eng.tensor_scalar(selmask[:, :], iscore[:, :], -3.2e38, NEG, ALU.is_gt, ALU.mult)
            eng.drain()
            eng.tensor_tensor(selmask[:, :], selmask[:, :], tri[:, :], ALU.add)
            eng.drain()

            s = sC

            def c_tail(i):
                eng.wait_ge(s["o_done"], i + 1)
                eng.wait_ge(s["asig_ready"], i + 1)
                eng.tensor_tensor(on_c[:, :], B[6][:, :], asig[:, :], ALU.mult).then_inc(s["o_read"], 1)
                eng.drain()
                eng.tensor_tensor(chunk(oT, i * 2, 2), on_c[:, :], mixr[:, :], ALU.add).then_inc(mixed, 1)

            def c_body(i, first):
                eng.wait_ge(mm_done, unit(i, BASE["C"] + 1, 2, 2))
                if past_zero(i):
                    eng.wait_ge(s["rg_done"], i)
                for j in range(2):
                    eng.tensor_scalar(xc[:, j, :], B[0][:, j * T:(j + 1) * T], col("cw3", i * 2 + j), col("cb", i * 2 + j),
                                      ALU.mult, ALU.add)
                for d in (1, 2, 3):
                    eng.drain()
                    for j in range(2):
                        last = eng.scalar_tensor_tensor(out=xc[:, j, d:T], in0=B[0][:, j * T:(j + 1) * T - d],
                                                        scalar=col(f"cw{3 - d}", i * 2 + j), in1=xc[:, j, d:T],
                                                        op0=ALU.mult, op1=ALU.add)
                last.then_inc(s["xr_read"], 1)
                eng.drain().then_inc(s["xc_ready"], 1)
                eng.wait_ge(s["ri_read"], i + 1)
                for j in range(2):
                    last = eng.tensor_scalar(la[:, j * T:(j + 1) * T], rg[:, 0, j, :], rg_c[:, ds(i * 2 + j, 1)], None, ALU.mult)
                last.then_inc(s["la_ready"], 1)
                eng.wait_ge(s["ex_ready"], i + 1)
                eng.scalar_tensor_tensor(out=ub[:, 0, :], in0=ae[:, 1, :], scalar=1.0, in1=ae[:, 2, :], op0=ALU.add,
                                         op1=ALU.mult).then_inc(s["prod_ready"], 1)
                eng.tensor_tensor(ub[:, 1, :], rg[:, 1].rearrange("p j t -> p (j t)"), xc[:, :, :].rearrange("p j t -> p (j t)"), ALU.mult)
                eng.drain()
                eng.wait_ge(s["root_ready"], i + 1)
                eng.tensor_tensor(ub[:, 1, :], ub[:, 1, :], ub[:, 0, :], ALU.mult)
                eng.drain()
                for j in range(2):
                    a = slice(j * T, (j + 1) * T)
                    eng.tensor_tensor_scan(out=hs[:, a], data0=ae[:, 0, a], data1=ub[:, 1, a], initial=0.0, op0=ALU.mult, op1=ALU.add)
                if not first:
                    c_tail(i - 1)
                eng.drain()
                eng.wait_ge(s["rsig_ready"], i + 1)
                eng.tensor_tensor(mixr[:, :], hs[:, :], rsig[:, :], ALU.mult).then_inc(s["mix_ready"], 1)
                softmax_scores(s, i, prob_c, nmax_c, rsum_c, rinv_c, selmask)

            pair_loop(c_body)
            outputs_low("C", 0, PAIRS - 1)
            c_tail(PAIRS - 1)
            outputs_low("C", PAIRS - 1, 1)
            add_to_stream("OC", "Q")
            stream_norm("Q", [(hl, hh, "ffn")])

            s = sQ
            eng.wait_ge(consts_ready, 2)

            def top16(vals, inds, src, scratch):
                for n in range(len(src)):
                    eng.max(vals[n][:, 0:8], src[n])
                eng.drain()
                for n in range(len(src)):
                    eng.max_index(inds[n][:, 0:8], vals[n][:, 0:8], src[n])
                    eng.match_replace(scratch[n], vals[n][:, 0:8], src[n], TAKEN)
                eng.drain()
                for n in range(len(src)):
                    eng.max(vals[n][:, 8:16], scratch[n])
                eng.drain()
                for n in range(len(src)):
                    eng.max_index(inds[n][:, 8:16], vals[n][:, 8:16], scratch[n])
                eng.drain()

            def route(h):
                eng.wait_ge(s["sc_ready"], h + 1)
                for n in range(4):
                    eng.tensor_copy(work[n][:, :], S12[:, n // 2, ds(h, 1), (n % 2) * P:(n % 2 + 1) * P].rearrange("p o k -> p (o k)"))
                eng.drain()
                top16([vtop[:, n, :] for n in range(4)], [itop[:, n, :] for n in range(4)], [w[:, :] for w in work],
                      [w[:, :] for w in rest])
                k = [P, PEER_TOPK, PEER_TOPK]
                eng.tensor_copy(itopf[:, :, :], itop[:, :, :])
                for t in range(NT):
                    eng.tensor_tensor(cand[:, t].rearrange("p (a b) -> p a b", a=PEER_TOPK), vtop[:, 2 * t, :].unsqueeze(2).broadcast_to(k),
                                      vtop[:, 2 * t + 1, :].unsqueeze(1).broadcast_to(k), ALU.add)
                eng.drain()
                top16([ctop[:, t, :] for t in range(NT)], [cpos[:, t, :] for t in range(NT)], [cand[:, t, :] for t in range(NT)], cand2)
                eng.tensor_scalar(cab[:, :, 0, :], cpos[:, :, :], 4, None, ALU.logical_shift_right)
                eng.tensor_scalar(cab[:, :, 1, :], cpos[:, :, :], PEER_TOPK - 1, None, ALU.bitwise_and)
                eng.drain()
                eng.tensor_copy(cabf[:, :, :, :], cab[:, :, :, :])
                eng.drain()
                for n in range(4):
                    eng.tensor_tensor(onehot[:, n], cabf[:, n // 2, n % 2, :].unsqueeze(2).broadcast_to(k),
                                      iota[:, 0:PEER_TOPK].unsqueeze(1).broadcast_to(k), ALU.is_equal)
                eng.drain()
                for n in range(4):
                    eng.tensor_tensor(onehot[:, n], onehot[:, n], itopf[:, n, :].unsqueeze(1).broadcast_to(k), ALU.mult)
                eng.drain()
                eng.tensor_reduce(epart[:, :, :], onehot[:, :], AX.X, ALU.add)
                eng.drain()
                for n in range(4):
                    eng.tensor_copy(place[:, n // 2, n % 2, ds(h * PEER_TOPK, PEER_TOPK)], epart[:, n, :])
                eng.tensor_copy(tops[:, :, ds(h, 1), :].rearrange("p t o k -> p t (o k)"), ctop[:, :, :])
                eng.drain()

            def gates(tile):
                k = [P, PEER_HEADS, PEER_TOPK]
                t_ = tops[:, tile]
                eng.tensor_copy(gsum[:, 0, :], t_[:, :, 0])
                eng.drain()
                eng.tensor_tensor(t_, t_, gsum[:, 0, :].unsqueeze(2).broadcast_to(k), ALU.subtract).then_inc(s["sub_ready"], 1)
                eng.wait_ge(s["gexp_ready"], tile + 1)
                eng.tensor_reduce(gsum[:, 0, :], t_, AX.X, ALU.add)
                eng.drain()
                eng.reciprocal(gsum[:, 1, :], gsum[:, 0, :])
                eng.drain()
                eng.tensor_tensor(t_, t_, gsum[:, 1, :].unsqueeze(2).broadcast_to(k), ALU.mult)
                eng.drain()

            def hot_rows(b, i, c):
                n = i * PER_PAIR + (b * BJ + c)
                if past_zero(n - 1):
                    eng.wait_ge(s["g_done"], n - 1)
                tt = ds(i * (PER_PAIR * TG) + c * TG, TG)
                ka, kb = [P, TG, P], [P, TG, BJ]
                eng.tensor_tensor(hot_b[:, :, :], slotT[:, 1, tt].unsqueeze(2).broadcast_to(kb),
                                  iota[:, b * BJ:(b + 1) * BJ].unsqueeze(1).broadcast_to(kb), ALU.is_equal)
                eng.tensor_tensor(hot_a[c % 2][:, :, :], slotT[:, 0, tt].unsqueeze(2).broadcast_to(ka),
                                  iota[:, :].unsqueeze(1).broadcast_to(ka), ALU.is_equal)

            def gate_rows(b, i, c):
                tt = ds(i * (PER_PAIR * TG) + c * TG, TG)
                k = [P, TG, 2, BJ]
                eng.tensor_tensor(gates_b[c % 2][:, :, :, :], hot_b[:, :, :].unsqueeze(2).broadcast_to(k),
                                  gT[:, tt, :].unsqueeze(3).broadcast_to(k), ALU.mult).then_inc(s["pairs_ready"], 1)

            def gate(b, i, c, after=None):
                n = i * PER_PAIR + (b * BJ + c)
                eng.wait_ge(s["g_done"], n + 1)
                two = B[6 + c % 2][:, :].rearrange("p (t n b) -> p t n b", n=2, b=BJ)
                eng.tensor_copy(gsums[:, :, :], two[:, :, 0, :])
                if after is not None:
                    hot_rows(*after)
                eng.drain()
                eng.tensor_tensor(gsums[:, :, :], two[:, :, 1, :], gsums[:, :, :], ALU.add).then_inc(s["g_read"], 1)
                if after is not None:
                    gate_rows(*after)
                eng.drain()
                part = acts[b % 2][:, :, ds(i * (PER_PAIR * TG) + c * TG, TG)]
                eng.scalar_tensor_tensor(out=part, in0=gsums[:, :, :].rearrange("p t b -> p b t"), scalar=1.0 / G_SCALE,
                                         in1=part, op0=ALU.mult, op1=ALU.mult).then_inc(s["gated"], 1)
                eng.drain()

            def gate_turns(b):
                eng.wait_ge(s["z_read"], (b + 1) * BJ)
                last_turn = BJ // PER_PAIR - 1
                with eng.Fori(0, last_turn) as i:
                    for c in range(PER_PAIR):
                        gate(b, i, c, (b, i, c + 2))
                for c in range(PER_PAIR):
                    gate(b, last_turn, c, (b, last_turn, c + 2) if c < PER_PAIR - 2 else (b + 1, 0, c + 2 - PER_PAIR))

            def act_low(b, f, c):
                eng.wait_ge(s["ah_ready"], f * (BJ // 2) + (b * BJ + c + 1))
                eng.tensor_tensor(al[c % 2][:, :, :], acts[b % 2][:, 2 * c:2 * c + 2, :], ah[c % 2][:, :, :].bitcast(F32),
                                  ALU.subtract).then_inc(s["al_ready"], 1)

            def add_experts(b, f):
                eng.wait_ge(mm_done, unit(f * 2, BASE[f"V{b}"] + BJ // 2 - 1, 2, 2))
                for n in range(4):
                    c_ = chunk(xT, f * FH + 2 * n, 2)
                    eng.tensor_tensor(c_, B[n][:, :], c_, ALU.add).then_inc(s["x_added"], 1)

            def v_turns(b):
                gating = b == BLOCKS - 2
                if gating:
                    eng.wait_ge(s["z_read"], BLOCKS * BJ)
                act_low(b, 0, 0)
                for n in range(BJ):
                    if n + 1 < BJ:
                        act_low(b, (n + 1) // (BJ // 2), (n + 1) % (BJ // 2))
                    if gating:
                        gate(b + 1, 0, n, (b + 1, 0, n + 2) if n + 2 < BJ else None)
                    if n % (BJ // 2) == BJ // 2 - 1:
                        add_experts(b, n // (BJ // 2))

            with eng.Fori(0, PEER_HEADS) as h:
                route(h)
            for t in range(NT):
                gates(t)
            eng.drain().then_inc(s["routed"], 1)
            eng.wait_ge(s["rt_done"], 1)
            scaled = gsums[:, :, :].rearrange("p t b -> p (t b)")
            for t in range(NT):
                tt = slice(t * P, (t + 1) * P)
                eng.tensor_copy(slotT[:, :, tt], B[6 + t][:, 0:2 * P].rearrange("p (n k) -> p n k", n=2))
                eng.tensor_scalar(scaled[:, tt], B[6 + t][:, 2 * P:3 * P], G_SCALE, None, ALU.mult)
            eng.drain()
            eng.tensor_copy(gT[:, :, 0], scaled)
            eng.drain()
            eng.tensor_tensor(gT[:, :, 1], scaled, gT[:, :, 0], ALU.subtract)
            eng.drain().then_inc(s["slots_ready"], 1)
            for c in range(2):
                hot_rows(0, 0, c)
                eng.drain()
                gate_rows(0, 0, c)
                eng.drain()
            gate_turns(0)
            v_turns(0)
            gate_turns(1)
            v_turns(1)
            gate_turns(2)
            v_turns(2)
            v_turns(3)
            eng.wait_ge(s["zrs_ready"], 1)
            for g in range(FH):
                for c in (2 * g, 2 * g + 1):
                    last = eng.scalar_tensor_tensor(out=y[:, c, :], in0=xT[:, c, :], scalar=col("fin", c), in1=rstd[:, :],
                                                    op0=ALU.mult, op1=ALU.mult)
                last.then_inc(s["y_ready"], 1)


def kernel(**inputs):
    import numpy as np
    import concourse.bacc as bacc
    from concourse.bass_utils import run_bass_kernel_spmd

    a = {k: np.asarray(v) for k, v in inputs.items()}

    def units(w):
        n = -(-w.shape[1] // P)
        w = np.pad(w, ((0, 0), (0, n * P - w.shape[1])))
        return w.reshape(KC, P, n, P).transpose(2, 1, 0, 3).reshape(n, P, KC * P)

    def wide(v):
        return np.reshape(v, (KC, P)).T

    pack = [wide(a[n][0]) for n in ("a_norm_w", "a_lb_logits", "a_out_norm_w")]
    pack += [wide(a["kv_norm_w"]), wide(a["b_norm_w"][0]), wide(a["b_out_norm_w"][0]), wide(a["norm_mix_g_2"][0])]
    pack += [wide(a["conv_w_2"][0, n]) for n in range(4)]
    pack += [wide(a[n][0]) for n in ("conv_b_2", "rg_ba_2", "rg_bx_2", "rg_lambda_2", "norm_ffn_g_2")] + [wide(a["norm_final_g_2"])]
    pack += [a["k_norm_w"].reshape(P, 1), a["b_q_norm_w"].reshape(P, 1), a["kv_norm_g_2"].reshape(RC, P).T]
    pack += [np.concatenate([a[n][0], a[n][0]]).reshape(P, 1) for n in ("idx_ln_g_2", "idx_ln_b_2")]
    w_c = a["w_in_2"][0]
    i_q = 2 * D + KV_RANK
    i_k = i_q + IDX_HEADS * IDX_DIM
    i_g = i_k + IDX_DIM + IDX_HEADS
    arrays = {
        "x_fm": a["x"][0].T.reshape(KC, P, T).transpose(1, 0, 2),
        "prm_h": np.concatenate(pack, axis=1),
        "f_bias_h": a["kv_f_bias"].reshape(HEADS, 1),
        "w_in_a": units(a["a_w_in"][0]), "w_out_a": units(a["a_w_out"][0]),
        "w_fgate": units(a["kv_w"][:, 2 * D:]), "w_kv": units(a["kv_w"][:, 0:2 * D]),
        "w_in_b": units(a["b_w_in"][0]), "w_out_b": units(a["b_w_out"][0]),
        "w_latent": units(w_c[:, 2 * D:i_q]), "w_ikey": units(w_c[:, i_k:i_g]), "w_iquery": units(w_c[:, i_q:i_k]),
        "w_in_c": np.concatenate([units(w_c[:, c:c + D]) for c in (0, D, i_g, i_g + D)]),
        "rg_wa": a["rg_wa_2"][0], "rg_wx": a["rg_wx_2"][0],
        "w_uk": a["w_uk_2"][0], "w_uv": a["w_uv_2"][0], "w_out_c": units(a["w_o_2"][0]), "w_q": units(a["peer_wq_2"][0]),
        "keys1": a["peer_keys1_2"][0], "keys2": a["peer_keys2_2"][0],
        "peer_u": a["peer_u_2"][0].reshape(P, P, KC, P).transpose(1, 3, 2, 0).reshape(P, P, KC * P),
        "peer_v": a["peer_v_2"][0].reshape(P, BLOCKS, BJ // 2, 2, 2, D // 2).transpose(1, 4, 2, 0, 3, 5).reshape(P, P, D),
    }
    arrays = {k: np.ascontiguousarray(v) for k, v in arrays.items()}
    nc = bacc.Bacc("TRN2", target_bir_lowering=False, num_devices=1)
    aps = {k: nc.dram_tensor(k, v.shape, F32, kind="ExternalInput").ap() for k, v in arrays.items()}
    out = nc.dram_tensor("out", (P, KC, T), F32, kind="ExternalOutput").ap()
    program(nc, out=out, **aps)
    r = run_bass_kernel_spmd(nc, [arrays], core_ids=[0])
    return r.results[0]["out"].transpose(2, 1, 0).reshape(1, T, D)
```
